# Optimizing a Trainium2 kernel written in Bass

```python
import jax, jax.numpy as jnp
from jax import lax
import numpy as np
import math

D_MODEL = 1024
BATCH = 1
SEQ = 512
DEPTH = 1

CHUNK = 64
Q_BLOCK = 128
EPS = 1e-6
DN_HEADS = 8
DN_DK = 128
DN_DV = 128
DN_CONV = 4
MLA_HEADS = 8
MLA_NOPE = 128
MLA_ROPE = 64
MLA_DV = 128
MLA_KV_RANK = 256
ROPE_THETA = 10000.0
D_FF = 2816
FFN_CONV = 3

DN_QK = DN_HEADS * DN_DK
DN_V = DN_HEADS * DN_DV
MLA_QD = MLA_HEADS * (MLA_NOPE + MLA_ROPE)
MLA_VD = MLA_HEADS * MLA_DV
IN_SPLITS = (DN_QK, DN_QK, DN_V, DN_V, DN_HEADS, DN_HEADS, MLA_QD, MLA_KV_RANK, MLA_ROPE, D_MODEL, D_MODEL)
D_IN = DN_QK * 2 + DN_V * 2 + DN_HEADS * 2 + MLA_QD + MLA_KV_RANK + MLA_ROPE + 2 * D_MODEL


def rms_norm(x, w):
    xf = x.astype(jnp.float32)
    y = xf * lax.rsqrt(jnp.mean(xf * xf, axis=-1, keepdims=True) + EPS)
    return (y * w.astype(jnp.float32)).astype(x.dtype)

def l2_norm(x):
    xf = x.astype(jnp.float32)
    return xf * lax.rsqrt(jnp.sum(xf * xf, axis=-1, keepdims=True) + EPS)

def causal_dwconv(x, w, b=None):
    k = w.shape[0]
    y = lax.conv_general_dilated(x, w[:, None, :].astype(x.dtype), window_strides=(1,),
                                 padding=((k - 1, 0),),
                                 dimension_numbers=('NWC', 'WIO', 'NWC'),
                                 feature_group_count=x.shape[-1])
    if b is not None:
        y = y + b
    return y

def apply_rope(x, pos):
    half = x.shape[-1] // 2
    inv = ROPE_THETA ** (-jnp.arange(half, dtype=jnp.float32) / half)
    ang = pos.astype(jnp.float32)[..., None] * inv
    cos = jnp.cos(ang)[:, :, None, :]
    sin = jnp.sin(ang)[:, :, None, :]
    xf = x.astype(jnp.float32)
    x1, x2 = xf[..., :half], xf[..., half:]
    return jnp.concatenate([x1 * cos - x2 * sin, x2 * cos + x1 * sin], axis=-1).astype(x.dtype)

def gated_delta_rule(q, k, v, g, beta):
    out_dtype = v.dtype
    B, S, H, dk = q.shape
    dv = v.shape[-1]
    n = S // CHUNK
    f32 = jnp.float32

    def chunks(t):
        return t.astype(f32).reshape(B, n, CHUNK, H, t.shape[-1]).transpose(0, 3, 1, 2, 4)

    def chunks_s(t):
        return t.astype(f32).reshape(B, n, CHUNK, H).transpose(0, 3, 1, 2)

    qc = chunks(q) * (dk ** -0.5)
    kc = chunks(k)
    vc = chunks(v)
    bc = chunks_s(beta)
    gc = jnp.cumsum(chunks_s(g), axis=-1)
    tri = jnp.tril(jnp.ones((CHUNK, CHUNK), dtype=bool))
    strict = jnp.tril(jnp.ones((CHUNK, CHUNK), dtype=bool), -1)
    decay = jnp.exp(jnp.where(tri, gc[..., :, None] - gc[..., None, :], -jnp.inf))
    k_beta = kc * bc[..., None]
    v_beta = vc * bc[..., None]
    a_mat = jnp.where(strict, jnp.einsum('bhncd,bhnjd->bhncj', k_beta, kc) * decay, 0.0)
    eye = jnp.eye(CHUNK, dtype=f32)
    rhs = jnp.concatenate([v_beta, k_beta * jnp.exp(gc)[..., None]], axis=-1)
    sol = lax.linalg.triangular_solve(eye + a_mat, rhs, left_side=True, lower=True, unit_diagonal=True)
    u, w = sol[..., :dv], sol[..., dv:]
    intra = jnp.where(tri, jnp.einsum('bhncd,bhnjd->bhncj', qc, kc) * decay, 0.0)
    q_e = qc * jnp.exp(gc)[..., None]
    k_dec = kc * jnp.exp(gc[..., -1:] - gc)[..., None]
    chunk_dec = jnp.exp(gc[..., -1])

    def to_n(t):
        return jnp.moveaxis(t, 2, 0)

    xs = (to_n(q_e), to_n(intra), to_n(u), to_n(w), to_n(k_dec), jnp.moveaxis(chunk_dec, 2, 0))

    def step(state, inp):
        qe_i, att_i, u_i, w_i, kd_i, dec_i = inp
        v_new = u_i - jnp.einsum('bhcd,bhde->bhce', w_i, state)
        o_i = jnp.einsum('bhcd,bhde->bhce', qe_i, state) + jnp.einsum('bhcj,bhje->bhce', att_i, v_new)
        state = state * dec_i[..., None, None] + jnp.einsum('bhcd,bhce->bhde', kd_i, v_new)
        return state, o_i

    s0 = jnp.zeros((B, H, dk, dv), f32)
    _, o = lax.scan(step, s0, xs)
    o = o.transpose(1, 0, 3, 2, 4).reshape(B, S, H, dv)
    return o.astype(out_dtype)

def mla_attention(q, c_kv, k_rope, pos, kv_norm_w, w_uk, w_uv, q_norm_w, k_norm_w):
    B, S, _ = q.shape
    q = q.reshape(B, S, MLA_HEADS, MLA_NOPE + MLA_ROPE)
    ckv = rms_norm(c_kv, kv_norm_w)
    k_nope = (ckv @ w_uk).reshape(B, S, MLA_HEADS, MLA_NOPE)
    v = (ckv @ w_uv).reshape(B, S, MLA_HEADS, MLA_DV)
    k = jnp.concatenate([k_nope, jnp.broadcast_to(k_rope[:, :, None, :], (B, S, MLA_HEADS, MLA_ROPE))], axis=-1)
    q = rms_norm(q, q_norm_w)
    k = rms_norm(k, k_norm_w)
    q = jnp.concatenate([q[..., :MLA_NOPE], apply_rope(q[..., MLA_NOPE:], pos)], axis=-1)
    k = jnp.concatenate([k[..., :MLA_NOPE], apply_rope(k[..., MLA_NOPE:], pos)], axis=-1)
    scale = (MLA_NOPE + MLA_ROPE) ** -0.5
    chunk_id = jnp.arange(S) // CHUNK
    outs = []
    for s0 in range(0, S, Q_BLOCK):
        s1 = s0 + Q_BLOCK
        kb, vb = k[:, :s1], v[:, :s1]
        sc = jnp.einsum('bqhd,bkhd->bhqk', q[:, s0:s1], kb, preferred_element_type=jnp.float32) * scale
        mask = chunk_id[s0:s1, None] >= chunk_id[None, :s1]
        sc = jnp.where(mask, sc, -jnp.inf)
        p = jax.nn.softmax(sc, axis=-1).astype(v.dtype)
        outs.append(jnp.einsum('bhqk,bkhd->bqhd', p, vb))
    return jnp.concatenate(outs, axis=1)

def first_inputs(seed: int = 0) -> dict:
    key = jax.random.key(seed)
    ks = jax.random.split(key, 32)
    L = DEPTH
    f32 = jnp.float32

    def w(k, shape, fan_in, mult=1.0):
        return jax.random.normal(k, shape, f32) * (mult * fan_in ** -0.5)

    def gain(k, shape):
        return 1.0 + 0.02 * jax.random.normal(k, shape, f32)

    x = jax.random.normal(ks[0], (BATCH, SEQ, D_MODEL), f32)
    c = jax.random.normal(ks[1], (BATCH, D_MODEL), f32)
    offset = jax.random.randint(ks[2], (BATCH, 1), 0, 8192, dtype=jnp.int32)
    positions = (offset + jnp.arange(SEQ, dtype=jnp.int32)[None, :]).astype(jnp.int32)
    a_init = jax.random.uniform(ks[3], (L, DN_HEADS), f32, 1.0, 16.0)
    dt = jnp.exp(jax.random.uniform(ks[4], (L, DN_HEADS), f32, np.log(1e-3), np.log(1e-1)))
    dt_bias = dt + jnp.log(-jnp.expm1(-dt))
    return {
        "x": x,
        "c": c,
        "positions": positions,
        "w_ada": w(ks[5], (L, D_MODEL, 6 * D_MODEL), D_MODEL, 0.5),
        "b_ada": 0.02 * jax.random.normal(ks[6], (L, 6 * D_MODEL), f32),
        "norm1_w": gain(ks[7], (L, D_MODEL)),
        "w_in": w(ks[8], (L, D_MODEL, D_IN), D_MODEL),
        "dn_conv_w": w(ks[9], (L, DN_CONV, 2 * DN_QK + DN_V), DN_CONV),
        "dn_a_log": jnp.log(a_init),
        "dn_dt_bias": dt_bias,
        "dn_norm_w": gain(ks[10], (L, DN_DV)),
        "mla_kv_norm_w": gain(ks[11], (L, MLA_KV_RANK)),
        "mla_w_uk": w(ks[12], (L, MLA_KV_RANK, MLA_HEADS * MLA_NOPE), MLA_KV_RANK),
        "mla_w_uv": w(ks[13], (L, MLA_KV_RANK, MLA_VD), MLA_KV_RANK),
        "mla_q_norm_w": gain(ks[14], (L, MLA_NOPE + MLA_ROPE)),
        "mla_k_norm_w": gain(ks[15], (L, MLA_NOPE + MLA_ROPE)),
        "w_out_dn": w(ks[16], (L, DN_V, D_MODEL), DN_V),
        "w_out_mla": w(ks[17], (L, MLA_VD, D_MODEL), MLA_VD),
        "w_o": w(ks[18], (L, D_MODEL, D_MODEL), D_MODEL),
        "norm2_w": gain(ks[19], (L, D_MODEL)),
        "ffn_w_up": w(ks[20], (L, D_MODEL, 2 * D_FF), D_MODEL),
        "ffn_conv_w": w(ks[21], (L, FFN_CONV, D_FF), FFN_CONV),
        "ffn_conv_b": 0.02 * jax.random.normal(ks[22], (L, D_FF), f32),
        "ffn_w_down": w(ks[23], (L, D_FF, D_MODEL), D_FF),
    }

def first_block(x, c, positions, w_ada, b_ada, norm1_w, w_in, dn_conv_w, dn_a_log, dn_dt_bias,
              dn_norm_w, mla_kv_norm_w, mla_w_uk, mla_w_uv, mla_q_norm_w, mla_k_norm_w,
              w_out_dn, w_out_mla, w_o, norm2_w, ffn_w_up, ffn_conv_w, ffn_conv_b, ffn_w_down):
    B, S, D = x.shape
    split_at = [int(o) for o in np.cumsum(IN_SPLITS)[:-1]]
    for l in range(DEPTH):
        mod = jax.nn.silu(c) @ w_ada[l] + b_ada[l]
        shift1, scale1, gate1, shift2, scale2, gate2 = jnp.split(mod[:, None, :], 6, axis=-1)

        h = rms_norm(x, norm1_w[l]) * (1 + scale1) + shift1
        proj = h @ w_in[l]
        (dn_q, dn_k, dn_v, dn_z, dn_alpha, dn_beta,
         mla_q, mla_ckv, mla_kr, gate_dn, gate_mla) = jnp.split(proj, split_at, axis=-1)

        qkv = jax.nn.silu(causal_dwconv(jnp.concatenate([dn_q, dn_k, dn_v], axis=-1), dn_conv_w[l]))
        q_a = l2_norm(qkv[..., :DN_QK].reshape(B, S, DN_HEADS, DN_DK))
        k_a = l2_norm(qkv[..., DN_QK:2 * DN_QK].reshape(B, S, DN_HEADS, DN_DK))
        v_a = qkv[..., 2 * DN_QK:].reshape(B, S, DN_HEADS, DN_DV)
        g_a = -jnp.exp(dn_a_log[l].astype(jnp.float32)) * jax.nn.softplus(
            dn_alpha.astype(jnp.float32) + dn_dt_bias[l].astype(jnp.float32))
        beta_a = jax.nn.sigmoid(dn_beta.astype(jnp.float32))
        o_a = gated_delta_rule(q_a, k_a, v_a, g_a, beta_a)
        o_a = rms_norm(o_a, dn_norm_w[l]) * jax.nn.silu(dn_z.reshape(B, S, DN_HEADS, DN_DV))
        y_a = o_a.reshape(B, S, DN_V) @ w_out_dn[l]

        o_b = mla_attention(mla_q, mla_ckv, mla_kr, positions, mla_kv_norm_w[l], mla_w_uk[l],
                            mla_w_uv[l], mla_q_norm_w[l], mla_k_norm_w[l])
        y_b = o_b.reshape(B, S, MLA_VD) @ w_out_mla[l]

        mix = jax.nn.sigmoid(gate_dn) * y_a + jax.nn.sigmoid(gate_mla) * y_b
        x = x + gate1 * (mix @ w_o[l])

        h2 = rms_norm(x, norm2_w[l]) * (1 + scale2) + shift2
        up = h2 @ ffn_w_up[l]
        a_path, v_path = up[..., :D_FF], up[..., D_FF:]
        a_path = jax.nn.gelu(causal_dwconv(a_path, ffn_conv_w[l], ffn_conv_b[l]), approximate=False)
        x = x + gate2 * ((a_path * v_path) @ ffn_w_down[l])
    return x


HEAD_DIM = 64
RWKV_HEADS = 8
RWKV_WIDTH = RWKV_HEADS * HEAD_DIM
ATT_HEADS = 8
ATT_WIDTH = ATT_HEADS * HEAD_DIM
IDX_HEADS = 8
IDX_DIM = 64
DECAY_RANK = 64
AAA_RANK = 64
GATE_RANK = 128
MAX_TOPK = 256
D_FF_2 = ((8 * D_MODEL // 3 + 255) // 256) * 256
NORM_EPS = 1e-6
LNX_EPS = 64e-5

RWKV_COLS = 3 * RWKV_WIDTH + DECAY_RANK + AAA_RANK + GATE_RANK
ATT_COLS = 3 * ATT_WIDTH
IDX_COLS = IDX_HEADS * IDX_DIM + IDX_DIM + IDX_HEADS
GATE_COLS = 2 * D_MODEL
IN_COLS = RWKV_COLS + ATT_COLS + IDX_COLS + GATE_COLS


def rmsnorm(x, g):
    xf = x.astype(jnp.float32)
    y = xf * lax.rsqrt(jnp.mean(xf * xf, axis=-1, keepdims=True) + NORM_EPS)
    return (y * g.astype(jnp.float32)).astype(x.dtype)

def rope(t):
    S, D = t.shape[1], t.shape[-1]
    half = D // 2
    inv = 1.0 / (ROPE_THETA ** (jnp.arange(half, dtype=jnp.float32) * 2.0 / D))
    ang = jnp.arange(S, dtype=jnp.float32)[:, None] * inv[None, :]
    cos = jnp.cos(ang)[None, :, None, :]
    sin = jnp.sin(ang)[None, :, None, :]
    tf = t.astype(jnp.float32)
    t1, t2 = tf[..., :half], tf[..., half:]
    return jnp.concatenate([t1 * cos - t2 * sin, t1 * sin + t2 * cos], axis=-1).astype(t.dtype)

def token_shift(p, mu):
    prev = jnp.pad(p, ((0, 0), (1, 0), (0, 0)))[:, :-1]
    return p + (prev - p) * mu

def rwkv7_mix(p, w_decay_up, w0, a_up, a0, g_up, k_k, k_a, r_k, lnx_g, lnx_b):
    B, S, _ = p.shape
    H, N = RWKV_HEADS, HEAD_DIM
    c = np.cumsum([RWKV_WIDTH, RWKV_WIDTH, RWKV_WIDTH, DECAY_RANK, AAA_RANK])
    r, k, v, wd, ad, gd = jnp.split(p, c, axis=-1)
    w = -jax.nn.softplus(-(w0 + jnp.tanh(wd) @ w_decay_up)) - 0.5
    a = jax.nn.sigmoid(a0 + ad @ a_up)
    g = jax.nn.sigmoid(gd) @ g_up
    kk = (k * k_k).reshape(B, S, H, N).astype(jnp.float32)
    kk = kk / jnp.maximum(jnp.linalg.norm(kk, axis=-1, keepdims=True), 1e-12)
    k = k * (1.0 + (a - 1.0) * k_a)
    heads = lambda t: t.reshape(B, S, H, N).astype(jnp.float32)
    r_h, k_h, v_h, a_h = heads(r), heads(k), heads(v), heads(a)
    decay = jnp.exp(-jnp.exp(heads(w)))
    tm = lambda t: jnp.moveaxis(t, 1, 0)

    def step(state, inp):
        r_t, d_t, k_t, v_t, kk_t, a_t = inp
        sa = jnp.einsum('bhij,bhj->bhi', state, -kk_t)
        state = (state * d_t[:, :, None, :]
                 + sa[..., None] * (kk_t * a_t)[:, :, None, :]
                 + v_t[..., None] * k_t[:, :, None, :])
        y_t = jnp.einsum('bhij,bhj->bhi', state, r_t)
        return state, y_t

    state0 = jnp.zeros((B, H, N, N), jnp.float32)
    _, y = lax.scan(step, state0, (tm(r_h), tm(decay), tm(k_h), tm(v_h), tm(kk), tm(a_h)))
    y = jnp.moveaxis(y, 0, 1)
    mean = jnp.mean(y, axis=-1, keepdims=True)
    var = jnp.mean(jnp.square(y - mean), axis=-1, keepdims=True)
    y = (y - mean) * lax.rsqrt(var + LNX_EPS)
    y = y * lnx_g.reshape(H, N) + lnx_b.reshape(H, N)
    bonus = jnp.sum(r_h * k_h * r_k.astype(jnp.float32), axis=-1, keepdims=True) * v_h
    y = (y + bonus).reshape(B, S, RWKV_WIDTH).astype(p.dtype)
    return y * g

def dsa_attention(q, k, v, q_idx, k_idx, w_idx):
    B, S, H, Dh = q.shape
    topk = min(MAX_TOPK, S // 4)
    nb = S // Q_BLOCK
    blk = lambda t: jnp.moveaxis(t.reshape((B, nb, Q_BLOCK) + t.shape[2:]), 1, 0)
    key_pos = jnp.arange(S)
    idx_scale = IDX_DIM ** -0.5 * IDX_HEADS ** -0.5

    def one_block(args):
        qb, qib, wib, bi = args
        t = bi * Q_BLOCK + jnp.arange(Q_BLOCK)
        sc = jax.nn.relu(jnp.einsum('bqhd,bsd->bqhs', qib, k_idx).astype(jnp.float32))
        score = jnp.einsum('bqhs,bqh->bqs', sc, wib.astype(jnp.float32)) * idx_scale
        causal = key_pos[None, None, :] <= t[None, :, None]
        score = jnp.where(causal, score, -jnp.inf)
        _, sel = lax.top_k(score, topk)
        valid = sel <= t[None, :, None]
        kg = jax.vmap(lambda kb, ib: kb[ib])(k, sel)
        vg = jax.vmap(lambda vb, ib: vb[ib])(v, sel)
        logits = jnp.einsum('bqhd,bqkhd->bqhk', qb, kg).astype(jnp.float32) * Dh ** -0.5
        logits = jnp.where(valid[:, :, None, :], logits, -jnp.inf)
        prob = jax.nn.softmax(logits, axis=-1).astype(vg.dtype)
        return jnp.einsum('bqhk,bqkhd->bqhd', prob, vg)

    out = lax.map(one_block, (blk(q), blk(q_idx), blk(w_idx), jnp.arange(nb)))
    return jnp.moveaxis(out, 0, 1).reshape(B, S, H * Dh)

def second_inputs(seed: int = 0) -> dict:
    key = jax.random.key(seed)
    ks = jax.random.split(key, 24)
    nrm = lambda k, shape, s: jax.random.normal(k, shape, jnp.float32) * s
    return {
        "x": jax.random.normal(ks[0], (BATCH, SEQ, D_MODEL), jnp.float32),
        "norm1_g": 1.0 + nrm(ks[1], (D_MODEL,), 0.05),
        "w_in": nrm(ks[2], (D_MODEL, IN_COLS), D_MODEL ** -0.5),
        "tshift_mu": jax.random.uniform(ks[3], (RWKV_COLS,), jnp.float32),
        "w_decay_up": nrm(ks[4], (DECAY_RANK, RWKV_WIDTH), 0.5 * DECAY_RANK ** -0.5),
        "w0": nrm(ks[5], (RWKV_WIDTH,), 0.5),
        "a_up": nrm(ks[6], (AAA_RANK, RWKV_WIDTH), 0.5 * AAA_RANK ** -0.5),
        "a0": nrm(ks[7], (RWKV_WIDTH,), 0.5),
        "g_up": nrm(ks[8], (GATE_RANK, RWKV_WIDTH), GATE_RANK ** -0.5),
        "k_k": 0.85 + nrm(ks[9], (RWKV_WIDTH,), 0.05),
        "k_a": 1.0 + nrm(ks[10], (RWKV_WIDTH,), 0.05),
        "r_k": nrm(ks[11], (RWKV_HEADS, HEAD_DIM), 0.1),
        "lnx_g": 1.0 + nrm(ks[12], (RWKV_WIDTH,), 0.05),
        "lnx_b": nrm(ks[13], (RWKV_WIDTH,), 0.01),
        "w_o_rwkv": nrm(ks[14], (RWKV_WIDTH, D_MODEL), RWKV_WIDTH ** -0.5),
        "w_o_att": nrm(ks[15], (ATT_WIDTH, D_MODEL), ATT_WIDTH ** -0.5),
        "w_out": nrm(ks[16], (D_MODEL, D_MODEL), D_MODEL ** -0.5),
        "norm2_g": 1.0 + nrm(ks[17], (D_MODEL,), 0.05),
        "w_ffn_in": nrm(ks[18], (D_MODEL, 2 * D_FF_2), D_MODEL ** -0.5),
        "w_ffn_out": nrm(ks[19], (D_FF_2, D_MODEL), D_FF_2 ** -0.5),
        "normf_g": 1.0 + nrm(ks[20], (D_MODEL,), 0.05),
    }

def second_block(x, norm1_g, w_in, tshift_mu, w_decay_up, w0, a_up, a0, g_up, k_k, k_a, r_k,
              lnx_g, lnx_b, w_o_rwkv, w_o_att, w_out, norm2_g, w_ffn_in, w_ffn_out, normf_g):
    B, S, _ = x.shape
    h = x
    for _layer in range(DEPTH):
        u = rmsnorm(h, norm1_g)
        proj = u @ w_in
        c = np.cumsum([RWKV_COLS, ATT_COLS, IDX_COLS])
        p_rwkv, p_att, p_idx, p_gate = jnp.split(proj, c, axis=-1)

        y_a = rwkv7_mix(token_shift(p_rwkv, tshift_mu), w_decay_up, w0, a_up, a0, g_up,
                        k_k, k_a, r_k, lnx_g, lnx_b)

        q, k, v = jnp.split(p_att, 3, axis=-1)
        hv = lambda t: t.reshape(B, S, ATT_HEADS, HEAD_DIM)
        q, k, v = rope(hv(q)), rope(hv(k)), hv(v)
        ci = np.cumsum([IDX_HEADS * IDX_DIM, IDX_DIM])
        q_idx, k_idx, w_idx = jnp.split(p_idx, ci, axis=-1)
        q_idx = rope(q_idx.reshape(B, S, IDX_HEADS, IDX_DIM))
        k_idx = rope(k_idx[:, :, None, :])[:, :, 0, :]
        y_b = dsa_attention(q, k, v, q_idx, k_idx, w_idx)

        g_a, g_b = jnp.split(jax.nn.sigmoid(p_gate), 2, axis=-1)
        merged = g_a * (y_a @ w_o_rwkv) + g_b * (y_b @ w_o_att)
        h = h + merged @ w_out

        z = rmsnorm(h, norm2_g) @ w_ffn_in
        z_gate, z_up = jnp.split(z, 2, axis=-1)
        h = h + (jax.nn.silu(z_gate) * z_up) @ w_ffn_out
    return rmsnorm(h, normf_g)


def setup_inputs(seed=0):
    out = dict(first_inputs(seed))
    for name, value in second_inputs(seed + 1).items():
        if name != "x":
            out[name + "_2"] = value
    return out


def reference(
    x, c, positions, w_ada, b_ada, norm1_w, w_in, dn_conv_w, dn_a_log, dn_dt_bias, dn_norm_w,
    mla_kv_norm_w, mla_w_uk, mla_w_uv, mla_q_norm_w, mla_k_norm_w, w_out_dn, w_out_mla, w_o,
    norm2_w, ffn_w_up, ffn_conv_w, ffn_conv_b, ffn_w_down, norm1_g_2, w_in_2, tshift_mu_2,
    w_decay_up_2, w0_2, a_up_2, a0_2, g_up_2, k_k_2, k_a_2, r_k_2, lnx_g_2, lnx_b_2, w_o_rwkv_2,
    w_o_att_2, w_out_2, norm2_g_2, w_ffn_in_2, w_ffn_out_2, normf_g_2,
):
    x = first_block(
        x, c, positions, w_ada, b_ada, norm1_w, w_in, dn_conv_w, dn_a_log, dn_dt_bias,
        dn_norm_w, mla_kv_norm_w, mla_w_uk, mla_w_uv, mla_q_norm_w, mla_k_norm_w, w_out_dn,
        w_out_mla, w_o, norm2_w, ffn_w_up, ffn_conv_w, ffn_conv_b, ffn_w_down,
    )
    return second_block(
        x, norm1_g_2, w_in_2, tshift_mu_2, w_decay_up_2, w0_2, a_up_2, a0_2, g_up_2, k_k_2,
        k_a_2, r_k_2, lnx_g_2, lnx_b_2, w_o_rwkv_2, w_o_att_2, w_out_2, norm2_g_2, w_ffn_in_2,
        w_ffn_out_2, normf_g_2,
    )


_drawn_inputs = setup_inputs


def setup_inputs(seed=0):
    import zlib

    import numpy as np

    out = dict(_drawn_inputs(seed))
    spreads = {}
    factors = {'norm1_w': 7.674,
     'dn_norm_w': 8.0,
     'mla_kv_norm_w': 8.0,
     'mla_w_uk': 2.77,
     'mla_q_norm_w': 8.0,
     'mla_k_norm_w': 8.0,
     'norm2_w': 18.355,
     'ffn_conv_b': 25.565,
     'w_decay_up_2': 70.848,
     'k_k_2': 200.0,
     'k_a_2': 12.707,
     'lnx_g_2': 200.0,
     'lnx_b_2': 200.0,
     'norm1_g_2': 5.786,
     'w0_2': 26.568,
     'r_k_2': 6.86,
     'w_o_att_2': 23.841,
     'norm2_g_2': 64.0}
    for name, (base, spread) in spreads.items():
        noise = np.random.default_rng([zlib.crc32(name.encode()), seed]).standard_normal(out[name].shape)
        drawn = base * np.exp(spread * noise) if base else spread * noise
        out[name] = __import__('jax').numpy.asarray(drawn.astype(out[name].dtype))
    for name, factor in factors.items():
        out[name] = (out[name] * factor).astype(out[name].dtype)
    return out
```

```python
from contextlib import ExitStack

import numpy as np

import concourse.bass as bass
from concourse import mybir

F32 = mybir.dt.float32
I32 = mybir.dt.int32
ALU = mybir.AluOpType
ACT = mybir.ActivationFunctionType
AX_X = mybir.AxisListType.X

P = 128
S = 512
D = 1024
KD = D // P
NT = S // P
H = 8
FF = 2816
NF = FF // P
HALF = H // 2
RANK = 256
ROPE = 64
N64 = 64
TOPK = 128
EPS = 1e-6
LNX_EPS = 64e-5
NEG = -1e30
LOW = -3e38
PANEL = 4096
SLOTS = 3
TMP = 12


class Order:

    def __init__(self):
        self.job, self.last, self.n, self.steps = {}, {}, 0, 0

    def add(self, name, jobs=1, steps=1):
        for i in range(jobs):
            self.job[name, i] = self.n
            for s in range(steps):
                self.steps += 1
                self.last[name, i, s] = self.steps
            self.last[name, i] = self.steps
            self.n += 1

    def bank(self, name, i=0):
        return self.job[name, i] % 8

    def use(self, name, i=0):
        return self.job[name, i] // 8


CONST_128 = ["ident", "ones", "top64", "low64", "same64", "rot", "utri", "neg_after", "strict64",
             "incl64", "rotq"] + [f"lvl{i}" for i in range(7)]


def constants():
    j, c = np.meshgrid(np.arange(P), np.arange(P), indexing="ij")
    m = {}
    m["ident"] = j == c
    m["ones"] = j >= 0
    m["top64"] = j < 64
    m["low64"] = j >= 64
    m["same64"] = j // 64 == c // 64
    same = j // 64 == c // 64
    m["rot"] = np.where(same & (j % 64 == c % 64 + 32), -1.0, 0) + np.where(same & (j % 64 + 32 == c % 64), 1.0, 0)
    m["rotq"] = m["rot"]
    m["utri"] = j <= c
    m["neg_after"] = np.where(j > c, NEG, 0)
    m["strict64"] = same & (j < c)
    m["incl64"] = same & (j <= c)
    for i in range(7):
        b = 1 << i
        m[f"lvl{i}"] = (j // (2 * b) == c // (2 * b)) & (j % (2 * b) < b) & (c % (2 * b) >= b)
    sq = np.stack([np.asarray(m[k], np.float32) for k in CONST_128], 1)
    wide = np.zeros((6, P, S), np.float32)
    q, k = j, c
    wide[0, :, S - P:] = np.where((q < 64) & (k >= 64), NEG, 0)
    wide[1, :, S - P:] = np.where(k > q, NEG, 0)
    wide[2, :, S - P:] = np.where(k > q, LOW, 0)
    half = 32
    inv = (1.0 / (np.float32(10000.0) ** (np.arange(half, dtype=np.float32) * np.float32(2.0) / np.float32(64)))).astype(np.float32)
    ang = np.arange(S, dtype=np.float32)[None, :] * inv[np.arange(P) % 32][:, None]
    wide[3] = np.cos(ang)
    wide[4] = np.sin(ang)
    wide[5] = (np.arange(S) % 64 != 0)[None, :]
    inv_mla = (np.float32(10000.0) ** (-np.arange(half, dtype=np.float32) / np.float32(half))).astype(np.float32)
    col = inv_mla[np.arange(P) % 32][:, None].astype(np.float32)
    return np.ascontiguousarray(sq), np.ascontiguousarray(wide.transpose(1, 0, 2)), np.ascontiguousarray(col)


COLS = [("one", 1), ("eps", 1), ("qscale", 1), ("lnx", 1), ("ln1024", 1), ("b_ada", 48), ("norm1", 8), ("conv", 96), ("dn_norm", 1),
        ("kv_norm", 2), ("qn_nope", 1), ("qn_rope", 1), ("kn_nope", 1), ("kn_rope", 1), ("norm2", 8), ("fconv", 66),
        ("fbias", 22), ("a_log", 8), ("dt_bias", 8), ("inv_freq", 1),
        ("norm1_2", 8), ("mu", 14), ("w0", 4), ("a0", 4), ("k_k", 4), ("k_a", 4), ("r_k", 4), ("lnx_g", 4), ("lnx_b", 4),
        ("norm2_2", 8), ("normf", 8)]
COL_AT, NCOLS = {}, 0
for _name, _width in COLS:
    COL_AT[_name] = NCOLS
    NCOLS += _width

def attention_order(order, name, units):
    n = len(units)
    for u in range(n + 2):
        if u < n:
            order.add((name, "scores", u))
        if 1 <= u <= n:
            order.add((name, "turn", u - 1))
        if u >= 2:
            order.add((name, "values", u - 2))


def inverse_order(order, name, t, levels):
    for hf in range(2):
        order.add((name, "x0", t, hf))
    for lv in range(1, levels):
        for hf in range(2):
            order.add((name, "p1", t, lv, hf))
        for hf in range(2):
            order.add((name, "xt", t, lv, hf))
            if lv < levels - 1:
                order.add((name, "x", t, lv, hf))


def plan_1(order):
    order.add("ada", 12)
    order.add("rms1")
    order.add("qkv", 24)
    order.add("ab")
    order.add("l2", 16)
    order.add("gc")
    for t in range(NT):
        for hf in range(2):
            for what in ("gb", "bb", "kk", "kq", "kt", "vt"):
                order.add((what, t, hf))
        inverse_order(order, "gdn", t, 7)
        for what in ("ks", "vn", "ot", "su"):
            for hf in range(2):
                order.add((what, t, hf))
    order.add("onorm", 8)
    order.add("z", 8)
    order.add("mq", 12)
    order.add("mkv", 3)
    order.add("kvn")
    order.add("uk", 8)
    order.add("mv", 8)
    order.add("kss", 8)
    order.add("krot")
    order.add("qss", 8)
    order.add("qrot", 4)
    attention_order(order, "mla", UNITS)
    for fb in range(2):
        order.add(f"gate_dn{fb}", 4)
        order.add(f"y_dn{fb}", 4)
        order.add(f"gate_mla{fb}", 4)
        order.add(f"y_mla{fb}", 4)
    order.add("wo", 8)
    order.add("rms2")
    order.add("up", 44)
    order.add("down", 8, steps=3)


def plan_2(order):
    order.add("rms3")
    order.add("rkv", 12)
    order.add("wag", 2)
    for what in ("wup", "aup", "gup", "kkn", "bon"):
        order.add(what, 4)
    for t in range(NT):
        for what in ("vrow", "brow", "krow"):
            order.add((what, t))
        for par in range(2):
            for what in ("rm", "rn", "rb", "rk"):
                order.add((what, t, par))
        order.add(("nv", t))
        inverse_order(order, "rw", t, 6)
        for e in range(2):
            for par in range(2):
                order.add(("rs", t, e, par))
            order.add(("ru", t, e))
            for par in range(2):
                order.add(("ry", t, e, par))
            order.add(("rz", t, e))
        order.add(("yi", t))
    order.add("gmean", 4)
    order.add("gvar", 4)
    order.add("ai", 5)
    order.add("wi")
    order.add("irot", 5)
    order.add("index", 24)
    order.add("aq", 8)
    order.add("av", 4)
    order.add("arot", 8)
    order.add("gate_a", 8)
    order.add("yr", 8)
    attention_order(order, "dsa", UNITS)
    order.add("gate_b", 8)
    order.add("ya", 8)
    order.add("wout", 8)
    order.add("rms4")
    order.add("up_2", 44)
    order.add("down_2", 8, steps=3)
    order.add("rms5")


UNITS = [(h, qt) for h in range(H) for qt in range(NT)]


def panel_plan(order, parts):
    first, release = {}, []

    def add(stage, releases):
        first[stage] = len(release)
        release.extend(releases)

    last = order.last
    if 1 in parts:
        add("ada", [last["ada", i] for i in range(12)])
        add("qkv", [last["qkv", 4 * i + 3] for i in range(6)])
        add("z", [last["z", 4 * i + 3] for i in range(2)])
        add("mq", [last["mq", 4 * i + 3] for i in range(3)])
        add("mkv", [last["mkv", 2]])
        add("ukv", [last["mv", 7]])
        for fb in range(2):
            for what in ("gate_dn", "y_dn", "gate_mla", "y_mla"):
                add(f"{what}{fb}", [last[f"{what}{fb}", 3]])
        add("wo", [last["wo", 4 * i + 3] for i in range(2)])
        add("up", [last["up", 4 * i + 3] for i in range(11)])
        add("down", [last["down", 4 * half + 3, s] for half in range(2) for s in range(3)])
    if 2 in parts:
        add("rkv", [last["rkv", 4 * i + 3] for i in range(3)])
        add("wag", [last["wag", 1]])
        add("ai", [last["ai", 3], last["ai", 4]])
        add("aq", [last["aq", 4 * i + 3] for i in range(2)])
        add("av", [last["av", 3]])
        add("gate_a", [last["gate_a", 4 * i + 3] for i in range(2)])
        add("yr", [last["yr", 7]])
        add("gate_b", [last["gate_b", 4 * i + 3] for i in range(2)])
        add("ya", [last["ya", 7]])
        add("wout", [last["wout", 4 * i + 3] for i in range(2)])
        add("up_2", [last["up_2", 4 * i + 3] for i in range(11)])
        add("down_2", [last["down_2", 4 * half + 3, s] for half in range(2) for s in range(3)])
    return first, release


def build(nc, a, parts=(1, 2)):
    order = Order()
    if 1 in parts:
        plan_1(order)
    if 2 in parts:
        plan_2(order)
    bank, use, last = order.bank, order.use, order.last
    panel_first, panel_release = panel_plan(order, parts)

    with ExitStack() as ctx:
        def sb(name, shape, dt=F32):
            return ctx.enter_context(nc.sbuf_tensor(name, shape, dt))

        sems = {}

        def sem(name):
            if name not in sems:
                sems[name] = ctx.enter_context(nc.semaphore(name))
            return sems[name]

        xT = sb("xT", [P, KD, S])
        hT = sb("hT", [P, KD, S])
        W = sb("W", [P, SLOTS, PANEL])
        ar = sb("ar", [P, 50, S])
        cm = sb("cm", [P, len(CONST_128), P])
        wide = sb("wide", [P, 4, S])
        trig = sb("trig", [P, 2, S])
        cols = sb("cols", [P, NCOLS])
        modT = sb("modT", [P, 48])
        amp = sb("amp", [P, 2, KD])
        cT = sb("cT", [P, KD])
        wab = sb("wab", [P, KD, 16])
        sm4 = sb("sm4", [P, 12, NT, 16])
        st = sb("st", [P, 64])
        wix = sb("wix", [P, KD, 8])
        sm2 = sb("sm2", [P, 160])
        ps = ctx.enter_context(nc.psum_tensor("ps", [P, 8, S], F32))

        def col(name, i=0, n=1):
            return cols[:, COL_AT[name] + i:COL_AT[name] + i + n]

        def const(name):
            return cm[:, CONST_128.index(name), :]

        pe_done = sem("pe_done")
        bank_read = [sem(f"bank{b}_read") for b in range(8)]
        panel_in = [sem(f"panel_in{s}") for s in range(SLOTS)]
        cols_in, consts_in, x_in, small2_in, ab_in, pos_in, trig_in, out_sent = (
            sem(n) for n in ("cols_in", "consts_in", "x_in", "small2_in", "ab_in", "pos_in", "trig_in", "out_sent"))

        def pst(name, i=0):
            return ps[:, bank(name, i), :]

        def filled(eng, name, i=0):
            eng.wait_ge(pe_done, last[name, i])

        def read(name, i=0):
            return bank_read[bank(name, i)], use(name, i) + 1

        def emptied(eng, name, i=0):
            eng.wait_ge(*read(name, i))

        def linker(eng, chain):
            n = [0]

            def link(ins, s=None, value=None):
                if s is None:
                    n[0] += 1
                    s, value = chain, n[0]
                ins.then_inc(s, 1)
                eng.wait_ge(s, value)
            return link

        def tile(i):
            return ar[:, i, :]

        def pair(i, hf):
            return ar[:, i + hf, :].rearrange("p (h c) -> p h c", c=P)

        def heads(i, h):
            return ar[:, i + h // HALF, (h % HALF) * P:(h % HALF + 1) * P]

        Q0, K0, V0 = 0, 8, 16
        BASES = {"gdn": (26, 36, 38, 40, 42), "rw": (36, 38, 40, 42, 44)}
        DT, AM, ATT, KD_ROW, VB, QE, XTR, XX, MK, P1, EGB, VN, ST = 24, 26, 28, 30, 32, 34, 36, 38, 40, 42, 44, 48, 46
        RHS = DT
        LORA = 46
        lora = ar[:, LORA:LORA + 2, :]
        RHO, KT, V2, WA, GD, BT, G2, LD, KAP, GCUM, BV = 0, 4, 8, 12, 13, 14, 18, 22, 26, 30, 32
        NTR, BRT, KRT, VROW, BROW, KROW, RSB, UU, ST2, NVT = 46, 48, 22, 24, 25, 12, 13, 30, 31, 46
        AQ, AK, QI, KI, AV, SEL, SCO, WORK, REL, OA, MERGE = 4, 8, 12, 16, 18, 22, 25, 28, (29, 17), 35, 42
        OM_MU, OM_KA, EC, WI, TOP8 = 0, 14, 24, 56, 88
        QN, QR, KN, KR, MV, CKV, KROPE, KRW = 24, 32, 36, 44, 0, 8, 10, 11
        MIX, G0 = 0, 16

        def bh(x, n=P):
            return x.unsqueeze(2).to_broadcast([x.shape[0], x.shape[1], n])

        def bm(x, n=HALF):
            return x.unsqueeze(1).to_broadcast([x.shape[0], n, x.shape[1]])

        def heads4(name, i=0):
            return pst(name, i).rearrange("p (h c) -> p h c", c=P)

        AB_X, AB_A, AB_E, AB_B, G, GC, EGC, KDEC, BE, BETA, AB_R = range(11)

        def tok(which, t, lo=0, n=8):
            return sm4[:, which, t, lo:lo + n]

        block = ctx.enter_context(nc.Block())

        @block.sync
        def _(sp):
            sp.dma_start(cols[:], a["cols"]).then_inc(cols_in, 16)
            sp.dma_start(cT[:], a["cT"]).then_inc(cols_in, 16)
            for n, free in enumerate(panel_release):
                if n >= SLOTS:
                    sp.wait_ge(pe_done, panel_release[n - SLOTS])
                sp.dma_start(W[:, n % SLOTS, :], a["panels"][n]).then_inc(panel_in[n % SLOTS], 16)
                if n == 0:
                    sp.dma_start(xT[:], a["xT"]).then_inc(x_in, 16)
                    sp.dma_start(cm[:], a["cm"]).then_inc(consts_in, 16)
                    sp.dma_start(wide[:], a["wide"]).then_inc(consts_in, 16)
                    sp.dma_start(wab[:], a["wab"]).then_inc(ab_in, 16)
                if 1 in parts and n == 2:
                    sp.dma_start(trig[:, 0, :].bitcast(I32), a["posb"]).then_inc(pos_in, 16)
                if 2 in parts:
                    if n == panel_first["rkv"]:
                        sp.dma_start(lora[:], a["lora"]).then_inc(small2_in, 16)
                        sp.dma_start(wix[:], a["wix"]).then_inc(small2_in, 16)
                        if 1 in parts:
                            sp.wait_ge(pe_done, last["down", 0, 0])
                        sp.dma_start(trig[:], a["trig"]).then_inc(trig_in, 16)
            if 2 in parts:
                sp.wait_ge(sem("y_out"), KD)
                sp.dma_start(a["out"], xT[:]).then_inc(out_sent, 16)
            else:
                sp.wait_ge(sem("x2"), KD)
                sp.dma_start(a["out"], xT[:]).then_inc(out_sent, 16)
            sp.wait_ge(out_sent, 16)

        @block.tensor
        def _(pe):
            mm = nc.tensor.matmul

            def begin(name, i=0):
                if use(name, i):
                    pe.wait_ge(bank_read[bank(name, i)], use(name, i))

            def end(ins):
                ins.then_inc(pe_done, 1)

            def panel(stage, i=0, width=S):
                n = panel_first[stage] + i
                pe.wait_ge(panel_in[n % SLOTS], 16 * (n // SLOTS + 1))
                return W[:, n % SLOTS, :].rearrange("p (k c) -> p k c", c=width)

            def project(stage, src, jobs, wait=None, kt=KD, per=4):
                for i in range(jobs):
                    w = panel(stage, i // per)
                    if wait and i == 0:
                        wait()
                    begin(stage, i)
                    for k in range(kt):
                        ins = mm(pst(stage, i), w[:, k, (i % per) * P:(i % per + 1) * P], src[:, k, :],
                                 start=(k == 0), stop=(k == kt - 1))
                    end(ins)

            def column_sums(name, i, squares, waits=(), sel="ones"):
                begin(name, i)
                for k, sq in enumerate(squares):
                    if k < len(waits):
                        pe.wait_ge(*waits[k])
                    ins = mm(pst(name, i), sel[k] if isinstance(sel, list) else const(sel), sq,
                             start=(k == 0), stop=(k == len(squares) - 1))
                end(ins)

            def inverse(name, t, levels):
                am, xtr, xx, mk, p1 = BASES[name]
                for hf in range(2):
                    pe.wait_ge(sem(f"{name}_xt0"), 2 * t + hf + 1)
                    begin((name, "x0", t, hf))
                    for h in range(HALF):
                        ins = nc.tensor.transpose(heads4((name, "x0", t, hf))[:, h, :], pair(xtr, hf)[:, h, :], const("ident"))
                    end(ins)
                for lv in range(1, levels):
                    for hf in range(2):
                        k = (t * (levels - 1) + lv - 1) * 2 + hf
                        pe.wait_ge(sem(f"{name}_masked"), k + 1)
                        if lv == 1:
                            emptied(pe, (name, "x0", t, hf))
                        else:
                            emptied(pe, (name, "xt", t, lv - 1, hf))
                            emptied(pe, (name, "x", t, lv - 1, hf))
                        begin((name, "p1", t, lv, hf))
                        for h in range(HALF):
                            ins = mm(heads4((name, "p1", t, lv, hf))[:, h, :], pair(mk, hf)[:, h, :], pair(xx, hf)[:, h, :],
                                     start=True, stop=True)
                        end(ins)
                    for hf in range(2):
                        emptied(pe, (name, "p1", t, lv, hf))
                        begin((name, "xt", t, lv, hf))
                        for h in range(HALF):
                            ins = mm(heads4((name, "xt", t, lv, hf))[:, h, :], pair(p1, hf)[:, h, :], pair(xtr, hf)[:, h, :],
                                     start=True, stop=True)
                        end(ins)
                        if lv < levels - 1:
                            begin((name, "x", t, lv, hf))
                            for h in range(HALF):
                                ins = mm(heads4((name, "x", t, lv, hf))[:, h, :], pair(xtr, hf)[:, h, :], pair(p1, hf)[:, h, :],
                                         start=True, stop=True)
                            end(ins)

            def attention(name, units, score, value, smt, ptt):
                n = len(units)
                for u in range(n + 2):
                    if u < n:
                        h, qt = units[u]
                        begin((name, "scores", u))
                        end(score(pst((name, "scores", u))[:, 0:(qt + 1) * P], h, qt))
                    if 1 <= u <= n:
                        h, qt = units[u - 1]
                        pe.wait_ge(sem(f"{name}_probs"), u)
                        begin((name, "turn", u - 1))
                        for kt in range(qt + 1):
                            ins = nc.tensor.transpose(pst((name, "turn", u - 1))[:, kt * P:(kt + 1) * P],
                                                      tile(smt[(u - 1) % 3])[:, kt * P:(kt + 1) * P], const("ident"))
                        end(ins)
                    if u >= 2:
                        h, qt = units[u - 2]
                        emptied(pe, (name, "turn", u - 2))
                        begin((name, "values", u - 2))
                        for kt in range(qt + 1):
                            out, lhs = value(pst((name, "values", u - 2)), h, kt)
                            ins = mm(out, lhs, tile(ptt[u % 2])[:, kt * P:(kt + 1) * P], start=(kt == 0), stop=(kt == qt))
                        end(ins)

            def feed_forward(sfx, h_ready):
                def wait():
                    pe.wait_ge(sem(h_ready), KD)
                project("up" + sfx, hT, 44, wait)
                for half in range(2):
                    for m in range(4):
                        i = 4 * half + m
                        begin("down" + sfx, i)
                        for s in range(3):
                            w = panel("down" + sfx, 3 * half + s)
                            nk = min(8, NF - 8 * s)
                            if i == 0:
                                pe.wait_ge(sem("gated" + sfx), min(8 * s + 8, NF))
                            for k in range(nk):
                                kk = 8 * s + k
                                ins = mm(pst("down" + sfx, i), w[:, k, m * P:(m + 1) * P], tile(G0 + kk),
                                         start=(kk == 0), stop=(kk == NF - 1))
                            end(ins)

            def block_1():
                pe.wait_ge(sem("silu_c"), 1)
                for i in range(12):
                    w = panel("ada", i)
                    begin("ada", i)
                    for m in range(4):
                        for k in range(KD):
                            ins = mm(pst("ada", i)[:, m:m + 1], w[:, k, m * P:(m + 1) * P], st[:, k:k + 1],
                                     start=(k == 0), stop=(k == KD - 1))
                    end(ins)
                pe.wait_ge(consts_in, 32)
                column_sums("rms1", 0, [tile(24 + i) for i in range(KD)], [(sem("rms1_sq"), i + 1) for i in range(KD)])
                project("qkv", hT, 24, lambda: pe.wait_ge(sem("rms1_h"), KD))
                pe.wait_ge(ab_in, 16)
                begin("ab")
                for t in range(NT):
                    for k in range(KD):
                        ins = mm(pst("ab")[:, t * 16:(t + 1) * 16], hT[:, k, t * P:(t + 1) * P], wab[:, k, :],
                                 start=(k == 0), stop=(k == KD - 1))
                end(ins)
                for i in range(16):
                    column_sums("l2", i, [tile(24 + i % 4)], [(sem("l2_sq"), i + 1)])
                pe.wait_ge(sem("g_ready"), 1)
                begin("gc")
                for t in range(NT):
                    mm(pst("gc")[:, t * 16:t * 16 + 8], const("utri"), tok(G, t), start=True, stop=True)
                    ins = mm(pst("gc")[:, t * 16 + 8:t * 16 + 16], const("ones"), tok(G, t), start=True, stop=True)
                end(ins)
                for t in range(NT):
                    c = slice(t * P, (t + 1) * P)
                    for hf in range(2):
                        hs = range(hf * HALF, (hf + 1) * HALF)
                        begin(("gb", t, hf))
                        for h in hs:
                            ins = mm(heads4(("gb", t, hf))[:, h % HALF, :], tok(G, t, h, 1).to_broadcast([P, P]), const("utri"),
                                     start=True, stop=True)
                        end(ins)
                        pe.wait_ge(sem("beta_ready"), 1)
                        begin(("bb", t, hf))
                        for h in hs:
                            ins = mm(heads4(("bb", t, hf))[:, h % HALF, :], tok(BETA, t, h, 1).to_broadcast([P, P]), const("ident"),
                                     start=True, stop=True)
                        end(ins)
                        pe.wait_ge(sem("qk_normed"), 16)
                        for what, other in (("kk", K0), ("kq", Q0)):
                            begin((what, t, hf))
                            for h in hs:
                                ins = mm(heads4((what, t, hf))[:, h % HALF, :], tile(K0 + h)[:, c], tile(other + h)[:, c],
                                         start=True, stop=True)
                            end(ins)
                        if t == 0:
                            pe.wait_ge(sem("conv_silu"), 24)
                        for what, src in (("kt", K0), ("vt", V0)):
                            begin((what, t, hf))
                            for h in hs:
                                ins = nc.tensor.transpose(heads4((what, t, hf))[:, h % HALF, :], tile(src + h)[:, c], const("ident"))
                            end(ins)
                    inverse("gdn", t, 7)
                    for hf in range(2):
                        begin(("ks", t, hf))
                        if t:
                            pe.wait_ge(sem("gdn_state"), 2 * t + hf + 1)
                        else:
                            pe.wait_ge(sem("gdn_state"), hf + 1)
                        for h in range(hf * HALF, (hf + 1) * HALF):
                            ins = mm(heads4(("ks", t, hf))[:, h % HALF, :], tile(K0 + h)[:, c], heads(ST, h), start=True, stop=True)
                        end(ins)
                    for hf in range(2):
                        pe.wait_ge(sem("gdn_rhs"), 2 * t + hf + 1)
                        emptied(pe, ("gdn", "xt", t, 6, hf))
                        begin(("vn", t, hf))
                        for h in range(HALF):
                            ins = mm(heads4(("vn", t, hf))[:, h, :], pair(XTR, hf)[:, h, :], pair(RHS, hf)[:, h, :],
                                     start=True, stop=True)
                        end(ins)
                    for hf in range(2):
                        emptied(pe, ("vn", t, hf))
                        pe.wait_ge(sem("gdn_qe"), 2 * t + hf + 1)
                        pe.wait_ge(sem("gdn_att"), 2 * t + hf + 1)
                        begin(("ot", t, hf))
                        for h in range(hf * HALF, (hf + 1) * HALF):
                            o = heads4(("ot", t, hf))[:, h % HALF, :]
                            mm(o, heads(ST, h), heads(QE, h), start=True, stop=False)
                            ins = mm(o, heads(VN, h), heads(ATT, h), start=False, stop=True)
                        end(ins)
                    for hf in range(2):
                        begin(("su", t, hf))
                        for h in range(hf * HALF, (hf + 1) * HALF):
                            ins = mm(heads4(("su", t, hf))[:, h % HALF, :], heads(KD_ROW, h), heads(VN, h), start=True, stop=True)
                        end(ins)
                for h in range(H):
                    column_sums("onorm", h, [tile(24 + h % 4)], [(sem("onorm_sq"), h + 1)])
                project("z", hT, 8)
                project("mq", hT, 12)
                project("mkv", hT, 3)
                column_sums("kvn", 0, [tile(12), tile(13)], [(sem("kv_sq"), i + 1) for i in range(2)])
                w = panel("ukv", 0, D)
                for h in range(H):
                    pe.wait_ge(sem("ckv"), 2)
                    begin("uk", h)
                    for k in range(2):
                        ins = mm(pst("uk", h), w[:, k, h * P:(h + 1) * P], tile(CKV + k), start=(k == 0), stop=(k == 1))
                    end(ins)
                for i in range(8):
                    t, half = i // 2, i % 2
                    begin("mv", i)
                    for k in range(2):
                        ins = mm(pst("mv", i), tile(CKV + k)[:, t * P:(t + 1) * P], w[:, 2 + k, half * S:(half + 1) * S],
                                 start=(k == 0), stop=(k == 1))
                    end(ins)
                for h in range(H):
                    column_sums("kss", h, [tile(12), tile(13 + h % 2)], [(sem("kr_sq"), 1), (sem("kn_sq"), h + 1)],
                                sel=[const("top64"), const("ones")])
                pe.wait_ge(sem("kr_w"), 1)
                begin("krot")
                end(mm(pst("krot"), const("rot"), tile(KROPE), start=True, stop=True))
                for h in range(H):
                    column_sums("qss", h, [tile(8 + (h // 2) % 2), tile(13 + h % 2)],
                                [(sem("qr_sq"), h // 2 + 1), (sem("qn_sq"), h + 1)],
                                sel=[const("low64" if h % 2 else "top64"), const("ones")])
                for p in range(4):
                    pe.wait_ge(sem("qr_w"), p + 1)
                    begin("qrot", p)
                    end(mm(pst("qrot", p), const("rot"), tile(QR + p), start=True, stop=True))

                pe.wait_ge(sem("mla_qk"), 1)
                emptied(pe, "mv", 7)

                def score(out, h, qt):
                    b = slice(64 * (h % 2), 64 * (h % 2) + 64)
                    mm(out, tile(QN + h)[:, qt * P:(qt + 1) * P], tile(KN + h)[:, 0:(qt + 1) * P], start=True, stop=False)
                    return mm(out, tile(QR + h // 2)[b, qt * P:(qt + 1) * P], tile(KR + h // 2)[b, 0:(qt + 1) * P],
                              start=False, stop=True)

                def value(out, h, kt):
                    return out[:, 0:P], ar[:, MV + 2 * kt + h // 4, (h % 4) * P:(h % 4 + 1) * P]

                attention("mla", UNITS, score, value, (12, 13, 14), (15, 48))
                oT = ar[:, V0:V0 + 8, :]
                obT = ar[:, QN:QN + 8, :]
                for fb in range(2):
                    project(f"gate_dn{fb}", hT, 4)
                    project(f"y_dn{fb}", oT, 4, lambda: pe.wait_ge(sem("o_dn"), 8))
                    project(f"gate_mla{fb}", hT, 4)
                    project(f"y_mla{fb}", obT, 4, lambda: [emptied(pe, ("mla", "values", u)) for u in (30, 31)])
                project("wo", ar[:, MIX:MIX + 8, :], 8, lambda: pe.wait_ge(sem("mix"), 8))
                column_sums("rms2", 0, [tile(i) for i in range(KD)], [(sem("rms2_sq"), i + 1) for i in range(KD)])
                feed_forward("", "rms2_h")

            def head64(x, h):
                return x[64 * (h % 2):64 * (h % 2) + 64]

            def block_2():
                pe.wait_ge(consts_in, 32)
                column_sums("rms3", 0, [tile(38 + i) for i in range(KD)], [(sem("rms3_sq"), i + 1) for i in range(KD)])
                project("rkv", hT, 12, lambda: pe.wait_ge(sem("rms3_h"), KD))
                project("wag", hT, 2)
                pe.wait_ge(small2_in, 32)
                pe.wait_ge(sem("lora_act"), 2)
                for p in range(4):
                    begin("wup", p)
                    end(mm(pst("wup", p), lora[0:64, 0, p * P:(p + 1) * P], tile(WA)[0:64, :], start=True, stop=True))
                for p in range(4):
                    begin("aup", p)
                    end(mm(pst("aup", p), lora[64:P, 0, p * P:(p + 1) * P], tile(WA)[64:P, :], start=True, stop=True))
                for p in range(4):
                    begin("gup", p)
                    end(mm(pst("gup", p), lora[:, 1, p * P:(p + 1) * P], tile(GD), start=True, stop=True))
                for p in range(4):
                    column_sums("kkn", p, [tile(40 + p)], [(sem("kk_sq"), p + 1)], sel="same64")
                for p in range(4):
                    column_sums("bon", p, [tile(44 + p)], [(sem("bonus_in"), p + 1)], sel="same64")
                pe.wait_ge(sem("rw_ready"), 4)
                for t in range(NT):
                    c = slice(t * P, (t + 1) * P)
                    for what, src in (("vrow", V2), ("brow", BT), ("krow", KT)):
                        begin((what, t))
                        for p in range(4):
                            ins = nc.tensor.transpose(heads4((what, t))[:, p, :], tile(src + p)[:, c], const("ident"))
                        end(ins)
                    for par in range(2):
                        b = slice(64 * par, 64 * par + 64)
                        for what, lhs, rhs in (("rm", BT, KAP), ("rn", KT, KAP), ("rb", BT, RHO), ("rk", KT, RHO)):
                            begin((what, t, par))
                            for p in range(4):
                                ins = mm(heads4((what, t, par))[:, p, :], tile(lhs + p)[b, c], tile(rhs + p)[b, c], start=True, stop=True)
                            end(ins)
                    pe.wait_ge(sem("rw_n"), 2 * t + 2)
                    emptied(pe, ("vrow", t))
                    begin(("nv", t))
                    for h in range(H):
                        ins = mm(pst(("nv", t))[:, h * 64:(h + 1) * 64], pair(NTR, h % 2)[:, h // 2, :], tile(VROW)[:, h * 64:(h + 1) * 64],
                                 start=True, stop=True)
                    end(ins)
                    inverse("rw", t, 6)
                    for e in range(2):
                        eb, n = slice(64 * e, 64 * e + 64), 2 * t + e
                        ec = slice(t * P + 64 * e, t * P + 64 * e + 64)
                        pe.wait_ge(sem("rw_state"), n + 1)
                        for par in range(2):
                            b = slice(64 * par, 64 * par + 64)
                            begin(("rs", t, e, par))
                            for p in range(4):
                                ins = mm(pst(("rs", t, e, par))[eb, p * 64:(p + 1) * 64], tile(KAP + p)[b, ec],
                                         tile(ST2)[b, p * 64:(p + 1) * 64], start=True, stop=True)
                            end(ins)
                        if e == 0:
                            for par in range(2):
                                emptied(pe, ("rw", "xt", t, 5, par))
                        pe.wait_ge(sem("rw_rhs"), n + 1)
                        begin(("ru", t, e))
                        for h in range(H):
                            ins = mm(pst(("ru", t, e))[eb, h * 64:(h + 1) * 64], pair(38, h % 2)[eb, h // 2, eb],
                                     tile(RSB)[eb, h * 64:(h + 1) * 64], start=True, stop=True)
                        end(ins)
                        for par in range(2):
                            b = slice(64 * par, 64 * par + 64)
                            begin(("ry", t, e, par))
                            for p in range(4):
                                ins = mm(pst(("ry", t, e, par))[b, p * 64:(p + 1) * 64], tile(ST2)[b, p * 64:(p + 1) * 64],
                                         tile(RHO + p)[b, ec], start=True, stop=True)
                            end(ins)
                        emptied(pe, ("ru", t, e))
                        emptied(pe, ("brow", t))
                        emptied(pe, ("krow", t))
                        begin(("rz", t, e))
                        for h in range(H):
                            o = head64(pst(("rz", t, e)), h)[:, (h // 2) * 64:(h // 2) * 64 + 64]
                            mm(o, tile(BROW)[eb, h * 64:(h + 1) * 64], tile(UU)[eb, h * 64:(h + 1) * 64], start=True, stop=False)
                            ins = mm(o, tile(KROW)[eb, h * 64:(h + 1) * 64], tile(VROW)[eb, h * 64:(h + 1) * 64], start=False, stop=True)
                        end(ins)
                    pe.wait_ge(sem("rw_b"), 4 * t + 4)
                    begin(("yi", t))
                    for h in range(H):
                        o = head64(pst(("yi", t)), h)[:, (h // 2) * P:(h // 2 + 1) * P]
                        mm(o, tile(VROW)[:, h * 64:(h + 1) * 64], pair(KRT, h % 2)[:, h // 2, :], start=True, stop=False)
                        ins = mm(o, tile(UU)[:, h * 64:(h + 1) * 64], pair(BRT, h % 2)[:, h // 2, :], start=False, stop=True)
                    end(ins)
                for p in range(4):
                    column_sums("gmean", p, [tile(RHO + p)], [(sem("y_sum"), 4 * NT)], sel="same64")
                for p in range(4):
                    column_sums("gvar", p, [tile(36 + p)], [(sem("gn_sq"), p + 1)], sel="same64")
                project("ai", hT, 5)
                begin("wi")
                for t in range(NT):
                    for k in range(KD):
                        ins = mm(pst("wi")[:, t * 8:t * 8 + 8], hT[:, k, t * P:(t + 1) * P], wix[:, k, :], start=(k == 0), stop=(k == KD - 1))
                end(ins)
                for i in range(5):
                    emptied(pe, "ai", i)
                    begin("irot", i)
                    end(mm(pst("irot", i), const("rot"), tile(QI + i), start=True, stop=True))
                pe.wait_ge(sem("index_qk"), 1)
                for i in range(24):
                    qt, h = i // 8 + 1, i % 8
                    begin("index", i)
                    end(mm(pst("index", i)[:, 0:(qt + 1) * P], head64(tile(QI + h // 2), h)[:, qt * P:(qt + 1) * P],
                           head64(tile(KI), h)[:, 0:(qt + 1) * P], start=True, stop=True))
                project("aq", hT, 8)
                w = panel("av")
                for t in range(NT):
                    begin("av", t)
                    for k in range(KD):
                        ins = mm(pst("av", t), hT[:, k, t * P:(t + 1) * P], w[:, k, :], start=(k == 0), stop=(k == KD - 1))
                    end(ins)
                for i in range(8):
                    emptied(pe, "aq", i)
                    begin("arot", i)
                    end(mm(pst("arot", i), const("rot"), tile(AQ + i), start=True, stop=True))
                project("gate_a", hT, 8)
                w = panel("yr", 0, D)
                pe.wait_ge(sem("y_rw"), 4)
                for m in range(8):
                    begin("yr", m)
                    for k in range(4):
                        ins = mm(pst("yr", m), w[:, k, m * P:(m + 1) * P], tile(RHO + k), start=(k == 0), stop=(k == 3))
                    end(ins)
                pe.wait_ge(sem("dsa_qk"), 1)
                emptied(pe, "av", 3)

                def score(out, h, qt):
                    return mm(out, head64(tile(AQ + h // 2), h)[:, qt * P:(qt + 1) * P], head64(tile(AK + h // 2), h)[:, 0:(qt + 1) * P],
                              start=True, stop=True)

                def value(out, h, kt):
                    return head64(out, h)[:, 0:P], tile(AV + kt)[:, h * 64:(h + 1) * 64]

                attention("dsa", UNITS, score, value, (30, 31, 32), (33, 34))
                project("gate_b", hT, 8)
                w = panel("ya", 0, D)
                for u in (30, 31):
                    emptied(pe, ("dsa", "values", u))
                for m in range(8):
                    begin("ya", m)
                    for k in range(4):
                        ins = mm(pst("ya", m), w[:, k, m * P:(m + 1) * P], tile(OA + k), start=(k == 0), stop=(k == 3))
                    end(ins)
                project("wout", ar[:, MERGE:MERGE + 8, :], 8, lambda: pe.wait_ge(sem("merged"), 8))
                column_sums("rms4", 0, [tile(i) for i in range(KD)], [(sem("rms4_sq"), i + 1) for i in range(KD)])
                feed_forward("_2", "rms4_h")
                column_sums("rms5", 0, [tile(i) for i in range(KD)], [(sem("rms5_sq"), i + 1) for i in range(KD)])

            if 1 in parts:
                block_1()
            if 2 in parts:
                block_2()

        @block.scalar
        def _(act):
            link = linker(act, sem("act_chain"))
            af = nc.scalar.activation

            def squares(name, base, k=KD):
                for i in range(k):
                    link(af(tile(base + i), xT[:, i, :], ACT.Square), sem(f"{name}_sq"), i + 1)

            def rstd(job, i, tmp, out, scale, done, value, bias="eps", power_bias=0.0):
                filled(act, job, i)
                link(af(tmp, pst(job, i), ACT.Ln, bias=col(bias), scale=scale), *read(job, i))
                link(af(out, tmp, ACT.Exp, bias=power_bias, scale=-0.5), done, value)

            def inverse(name, t, levels):
                am, xtr, xx, mk, p1 = BASES[name]
                for hf in range(2):
                    filled(act, (name, "x0", t, hf))
                    link(nc.scalar.copy(pair(xx, hf), heads4((name, "x0", t, hf))), *read((name, "x0", t, hf)))
                for lv in range(1, levels):
                    for hf in range(2):
                        filled(act, (name, "p1", t, lv, hf))
                        link(nc.scalar.copy(pair(p1, hf), heads4((name, "p1", t, lv, hf))), *read((name, "p1", t, lv, hf)))

            def attention(name, units, scale, smt, ptt, out):
                n = len(units)
                for u in range(n + 2):
                    if u < n:
                        h, qt = units[u]
                        w = (qt + 1) * P
                        act.wait_ge(sem(f"{name}_peak"), u + 1)
                        link(af(tile(smt[u % 3])[:, 0:w], tile(smt[u % 3])[:, 0:w], ACT.Exp, bias=st[:, u % 3:u % 3 + 1],
                                scale=scale, accum_out=st[:, 4 + u % 3:5 + u % 3]), sem(f"{name}_exp"), u + 1)
                    if 1 <= u <= n:
                        h, qt = units[u - 1]
                        w = (qt + 1) * P
                        filled(act, (name, "turn", u - 1))
                        if u >= 3:
                            filled(act, (name, "values", u - 3))
                        link(nc.scalar.copy(tile(ptt[(u - 1) % 2])[:, 0:w], pst((name, "turn", u - 1))[:, 0:w]), *read((name, "turn", u - 1)))
                    if u >= 2:
                        h, qt = units[u - 2]
                        filled(act, (name, "values", u - 2))
                        dst, src = out(h, qt, pst((name, "values", u - 2)))
                        link(nc.scalar.copy(dst, src), *read((name, "values", u - 2)))

            def gelu(sfx):
                for i in range(NF):
                    act.wait_ge(sem("fconv" + sfx), i + 1)
                    link(af(tile(i % 4), tile(i % 4), ACT.Gelu if sfx == "" else ACT.Silu), sem("gelu" + sfx), i + 1)

            def block_1():
                act.wait_ge(cols_in, 32)
                link(af(st[:, 0:8], cT[:], ACT.Silu), sem("silu_c"), 1)
                act.wait_ge(x_in, 16)
                squares("rms1", 24)
                act.wait_ge(consts_in, 32)
                rstd("rms1", 0, tile(32), tile(33), 1.0 / D, sem("rms1_rstd"), 1)
                for i in range(24):
                    act.wait_ge(sem("conv"), i + 1)
                    link(af(tile(Q0 + i), tile(Q0 + i), ACT.Silu), sem("conv_silu"), i + 1)
                act.wait_ge(sem("ab_dve"), 1)
                link(af(sm4[:, AB_E, :, 0:8], sm4[:, AB_A, :, 0:8], ACT.Exp, scale=-1.0))
                link(af(sm4[:, AB_R, 0, 8:16], col("a_log", 0, 8), ACT.Exp))
                link(af(sm4[:, AB_B, :, 0:8], sm4[:, AB_B, :, 0:8], ACT.Exp, scale=-1.0))
                link(af(sm4[:, AB_E, :, 8:16], sm4[:, AB_E, :, 0:8], ACT.Ln, bias=col("one")), sem("ab_act"), 1)
                for i in range(16):
                    if i >= 2:
                        act.wait_ge(sem("qk_normed"), i - 1)
                    rstd("l2", i, tile(28 + i % 2), tile(30 + i % 2), 1.0, sem("l2_rstd"), i + 1,
                         power_bias=(col("qscale") if i < 8 else 0.0))
                act.wait_ge(sem("gc_dve"), 1)
                link(af(sm4[:, EGC, :, :], sm4[:, GC, :, :], ACT.Exp))
                link(af(sm4[:, KDEC, :, 0:8], sm4[:, KDEC, :, 0:8], ACT.Exp), sem("gc_act"), 1)
                for t in range(NT):
                    for hf in range(2):
                        n = 2 * t + hf + 1
                        act.wait_ge(sem("gb_minus"), n)
                        link(af(pair(EGB, hf), heads4(("gb", t, hf)), ACT.Exp), *read(("gb", t, hf)))
                        act.wait_ge(sem("gb_masked"), n)
                        link(af(pair(DT, hf), pair(DT, hf), ACT.Exp), sem("gdn_decay"), n)
                    inverse("gdn", t, 7)
                    for hf in range(2):
                        filled(act, ("vn", t, hf))
                        link(nc.scalar.copy(pair(VN, hf), heads4(("vn", t, hf))), *read(("vn", t, hf)))
                    for hf in range(2):
                        filled(act, ("ot", t, hf))
                        link(nc.scalar.copy(ar[:, V0 + hf * HALF:V0 + (hf + 1) * HALF, t * P:(t + 1) * P],
                                            heads4(("ot", t, hf))), *read(("ot", t, hf)))
                for h in range(H):
                    if h >= 2:
                        act.wait_ge(sem("o_scaled"), h - 1)
                    rstd("onorm", h, tile(28 + h % 2), tile(30 + h % 2), 1.0 / P, sem("o_rstd"), h + 1)
                for h in range(H):
                    filled(act, "z", h)
                    link(af(tile(Q0 + h), pst("z", h), ACT.Silu), *read("z", h))
                for i in range(12):
                    filled(act, "mq", i)
                    if i == 0:
                        act.wait_ge(sem("o_scaled"), 8)
                    link(nc.scalar.copy(tile(QN + i), pst("mq", i)), *read("mq", i))
                for i in range(2):
                    act.wait_ge(sem("angle"), 2)
                    link(af(trig[:, i, :], tile(10 + i) if i == 0 else tile(9), ACT.Sin), sem("trig"), i + 1)
                for i in range(3):
                    filled(act, "mkv", i)
                    if i == 0:
                        act.wait_ge(sem("o_dn"), 8)
                    link(nc.scalar.copy(tile(CKV + i), pst("mkv", i)), *read("mkv", i))
                for i in range(2):
                    link(af(tile(12 + i), tile(CKV + i), ACT.Square), sem("kv_sq"), i + 1)
                rstd("kvn", 0, tile(14), tile(15), 1.0 / RANK, sem("kv_rstd"), 1)
                for h in range(H):
                    filled(act, "uk", h)
                    link(nc.scalar.copy(tile(KN + h), pst("uk", h)), *read("uk", h))
                for i in range(8):
                    filled(act, "mv", i)
                    link(nc.scalar.copy(tile(MV + i), pst("mv", i)), *read("mv", i))
                link(af(tile(12), tile(KROPE), ACT.Square), sem("kr_sq"), 1)
                for h in range(H):
                    if h >= 2:
                        filled(act, "kss", h - 2)
                    link(af(tile(13 + h % 2), tile(KN + h), ACT.Square), sem("kn_sq"), h + 1)
                    if h:
                        if h >= 3:
                            act.wait_ge(sem("k_scaled"), h - 2)
                        rstd("kss", h - 1, tile(15), tile(48 + (h - 1) % 2), 1.0 / 192, sem("k_rstd"), h)
                act.wait_ge(sem("k_scaled"), 6)
                rstd("kss", 7, tile(15), tile(49), 1.0 / 192, sem("k_rstd"), 8)
                for h in range(H):
                    p = h // 2
                    if h % 2 == 0:
                        if p >= 2:
                            filled(act, "qss", 2 * p - 3)
                        else:
                            act.wait_ge(sem("ckv_free"), 1)
                        link(af(tile(8 + p % 2), tile(QR + p), ACT.Square), sem("qr_sq"), p + 1)
                    if h >= 2:
                        filled(act, "qss", h - 2)
                    else:
                        filled(act, "kss", 6 + h)
                    link(af(tile(13 + h % 2), tile(QN + h), ACT.Square), sem("qn_sq"), h + 1)
                    if h:
                        act.wait_ge(sem("q_scaled" if h >= 3 else "k_scaled"), h - 2 if h >= 3 else 6 + h)
                        rstd("qss", h - 1, tile(15), tile(48 + (h - 1) % 2), 1.0 / 192, sem("q_rstd"), h)
                act.wait_ge(sem("q_scaled"), 6)
                rstd("qss", 7, tile(15), tile(49), 1.0 / 192, sem("q_rstd"), 8)
                attention("mla", UNITS, 192 ** -0.5, (12, 13, 14), (15, 48),
                          lambda h, qt, src: (tile(QN + h)[:, qt * P:(qt + 1) * P], src[:, 0:P]))
                for fb in range(2):
                    for j, what in enumerate(("gate_dn", "gate_mla")):
                        for m in range(4):
                            k = 2 * fb + j
                            filled(act, f"{what}{fb}", m)
                            if k:
                                act.wait_ge(sem("gate_used"), 4 * (k - 1) + m + 1)
                            link(af(tile(8 + m), pst(f"{what}{fb}", m), ACT.Sigmoid), *read(f"{what}{fb}", m))
                for i in range(KD):
                    act.wait_ge(sem("x1"), i + 1)
                    if i == 0:
                        filled(act, "wo", 7)
                    link(af(tile(i), xT[:, i, :], ACT.Square), sem("rms2_sq"), i + 1)
                rstd("rms2", 0, tile(8), tile(9), 1.0 / D, sem("rms2_rstd"), 1)
                gelu("")

            def block_2():
                if 1 not in parts:
                    act.wait_ge(x_in, 16)
                for i in range(KD):
                    if 1 in parts:
                        act.wait_ge(sem("x2"), i + 1)
                    link(af(tile(38 + i), xT[:, i, :], ACT.Square), sem("rms3_sq"), i + 1)
                act.wait_ge(consts_in, 32)
                act.wait_ge(cols_in, 32)
                rstd("rms3", 0, tile(48), tile(49), 1.0 / D, sem("rms3_rstd"), 1)
                act.wait_ge(sem("shifted"), 14)
                link(af(tile(WA)[0:64, :], tile(WA)[0:64, :], ACT.Tanh), sem("lora_act"), 1)
                link(af(tile(GD), tile(GD), ACT.Sigmoid), sem("lora_act"), 2)
                for what, base, bias in (("wup", LD, "w0"), ("aup", BT, "a0")):
                    for p in range(4):
                        filled(act, what, p)
                        link(af(tile(base + p), pst(what, p), ACT.Sigmoid, bias=col(bias, p)), *read(what, p))
                for p in range(4):
                    filled(act, "gup", p)
                    link(nc.scalar.copy(tile(G2 + p), pst("gup", p)), *read("gup", p))
                for p in range(4):
                    link(af(tile(40 + p), tile(KT + p), ACT.Square, scale=col("k_k", p)), sem("kk_sq"), p + 1)
                for p in range(4):
                    act.wait_ge(sem("kk_clamped"), p + 1)
                    link(af(tile(48), tile(36 + p % 2), ACT.Ln, scale=float(2 ** 20)))
                    if p >= 2:
                        act.wait_ge(sem("kk_used"), p - 1)
                    link(af(tile(38 + p % 2), tile(48), ACT.Exp, scale=-0.5, bias=col("ln1024")), sem("kk_rstd"), p + 1)
                for p in range(4):
                    act.wait_ge(sem("g_cum"), p + 1)
                    gc = tile(GCUM + p % 2)
                    link(af(tile(40), gc, ACT.Exp))
                    link(af(sm2[:, EC + 8 * p:EC + 8 * p + 8], gc[:, 63:S:64], ACT.Exp))
                    link(af(tile(42), gc, ACT.Exp, scale=-1.0))
                    link(af(tile(41), tile(36), ACT.Exp), sem("decays"), p + 1)
                    act.wait_ge(sem("rw_ready"), p + 1)
                for t in range(NT):
                    for what, dst in (("vrow", VROW), ("brow", BROW), ("krow", KROW)):
                        filled(act, (what, t))
                        link(nc.scalar.copy(tile(dst), pst((what, t))), *read((what, t)))
                    filled(act, ("nv", t))
                    link(nc.scalar.copy(tile(NVT), pst(("nv", t))), *read(("nv", t)))
                    inverse("rw", t, 6)
                    for e in range(2):
                        eb, n = slice(64 * e, 64 * e + 64), 2 * t + e
                        ec = slice(t * P + 64 * e, t * P + 64 * e + 64)
                        filled(act, ("ru", t, e))
                        link(nc.scalar.mul(tile(UU)[eb, :], pst(("ru", t, e))[eb, :], -1.0), *read(("ru", t, e)))
                        for par in range(2):
                            b = slice(64 * par, 64 * par + 64)
                            filled(act, ("ry", t, e, par))
                            link(nc.scalar.copy(ar[b, RHO:RHO + 4, ec], pst(("ry", t, e, par))[b, 0:256].rearrange("p (h c) -> p h c", c=64)),
                                 *read(("ry", t, e, par)))
                for p in range(4):
                    act.wait_ge(sem("gn_centred"), p + 1)
                    link(af(tile(36 + p), tile(RHO + p), ACT.Square), sem("gn_sq"), p + 1)
                for p in range(4):
                    if p >= 2:
                        act.wait_ge(sem("gn_used"), p - 1)
                    rstd("gvar", p, tile(40), tile(41 + p % 2), 1.0 / 64, sem("gn_rstd"), p + 1, bias="lnx")
                act.wait_ge(sem("y_rw"), 4)
                for i in range(5):
                    filled(act, "ai", i)
                    link(nc.scalar.copy(tile(QI + i), pst("ai", i)), *read("ai", i))
                for i in range(24):
                    w = (i // 8 + 2) * P
                    if i >= 2:
                        act.wait_ge(sem("index_used"), i - 1)
                    filled(act, "index", i)
                    link(af(tile(REL[i % 2])[:, 0:w], pst("index", i)[:, 0:w], ACT.Relu), *read("index", i))
                for i in range(8):
                    filled(act, "aq", i)
                    link(nc.scalar.copy(tile(AQ + i), pst("aq", i)), *read("aq", i))
                for t in range(NT):
                    filled(act, "av", t)
                    link(nc.scalar.copy(tile(AV + t), pst("av", t)), *read("av", t))
                for m in range(8):
                    filled(act, "gate_a", m)
                    link(af(tile(MERGE + m), pst("gate_a", m), ACT.Sigmoid), *read("gate_a", m))
                attention("dsa", UNITS, 64 ** -0.5, (30, 31, 32), (33, 34),
                          lambda h, qt, src: (tile(OA + h // 2)[64 * (h % 2):64 * (h % 2) + 64, qt * P:(qt + 1) * P],
                                              src[64 * (h % 2):64 * (h % 2) + 64, 0:P]))
                for m in range(8):
                    filled(act, "gate_b", m)
                    link(af(tile(AQ + m), pst("gate_b", m), ACT.Sigmoid), *read("gate_b", m))
                for i in range(KD):
                    act.wait_ge(sem("x3"), i + 1)
                    if i == 0:
                        filled(act, "wout", 7)
                    link(af(tile(i), xT[:, i, :], ACT.Square), sem("rms4_sq"), i + 1)
                rstd("rms4", 0, tile(8), tile(9), 1.0 / D, sem("rms4_rstd"), 1)
                for p in range(11):
                    for j in range(2):
                        i, job = 2 * p + j, 4 * p + j
                        filled(act, "up_2", job)
                        if i >= 4:
                            act.wait_ge(sem("gated_2"), i - 3)
                        link(af(tile(i % 4), pst("up_2", job), ACT.Silu), *read("up_2", job))
                for i in range(KD):
                    act.wait_ge(sem("x4"), i + 1)
                    if i == 0:
                        filled(act, "down_2", 7)
                    link(af(tile(i), xT[:, i, :], ACT.Square), sem("rms5_sq"), i + 1)
                rstd("rms5", 0, tile(8), tile(9), 1.0 / D, sem("rms5_rstd"), 1)

            if 1 in parts:
                block_1()
            if 2 in parts:
                block_2()

        @block.vector
        def _(dve):
            link = linker(dve, sem("dve_chain"))
            v = nc.vector
            tt, ts, stt = v.tensor_tensor, v.tensor_scalar, v.scalar_tensor_tensor

            def normed(name, rs, scale, shift):
                dve.wait_ge(sem(f"{name}_rstd"), 1)
                for i in range(KD):
                    link(tt(hT[:, i, :], xT[:, i, :], rs, ALU.mult))
                    if shift is None:
                        link(ts(hT[:, i, :], hT[:, i, :], scale(i), None, ALU.mult), sem(f"{name}_h"), i + 1)
                    else:
                        link(ts(hT[:, i, :], hT[:, i, :], scale(i), shift(i), ALU.mult, ALU.add), sem(f"{name}_h"), i + 1)

            def causal_conv(job, i, out, taps, done, value, bias=None):
                src = pst(job, i)
                n = len(taps)
                link(ts(out, src, taps[-1], bias, ALU.mult, ALU.add if bias is not None else ALU.bypass))
                for j in range(1, n):
                    ins = stt(out[:, j:S], src[:, 0:S - j], taps[n - 1 - j], out[:, j:S], ALU.mult, ALU.add)
                    if j < n - 1:
                        link(ins)
                    else:
                        link(ins, *read(job, i))

            def inverse(name, t, levels):
                am, xtr, xx, mk, p1 = BASES[name]
                for hf in range(2):
                    dve.wait_ge(sem(f"{name}_masked0"), 2 * t + hf + 1)
                    link(tt(pair(xtr, hf), bm(const("ident")), pair(mk, hf), ALU.subtract), sem(f"{name}_xt0"), 2 * t + hf + 1)
                for lv in range(1, levels):
                    for hf in range(2):
                        if lv < levels - 1:
                            filled(dve, (name, "x", t, lv, hf))
                        filled(dve, (name, "xt", t, lv, hf))
                        link(tt(pair(xtr, hf), pair(xtr, hf), heads4((name, "xt", t, lv, hf)), ALU.subtract), *read((name, "xt", t, lv, hf)))
                        if lv < levels - 1:
                            link(tt(pair(xx, hf), pair(xx, hf), heads4((name, "x", t, lv, hf)), ALU.subtract), *read((name, "x", t, lv, hf)))

            def attention(name, units, scale, smt, bias, before=None):
                n = len(units)
                for u in range(n + 1):
                    if u < n:
                        h, qt = units[u]
                        w = (qt + 1) * P
                        if before:
                            before(u)
                        filled(dve, (name, "scores", u))
                        if u >= 3:
                            filled(dve, (name, "turn", u - 3))
                        link(v.tensor_tensor_reduce(out=tile(smt[u % 3])[:, 0:w], in0=pst((name, "scores", u))[:, 0:w], in1=bias(qt),
                                                    scale=1.0, scalar=LOW, op0=ALU.add, op1=ALU.max,
                                                    accum_out=st[:, 8 + u % 3:9 + u % 3]), *read((name, "scores", u)))
                        link(ts(st[:, u % 3:u % 3 + 1], st[:, 8 + u % 3:9 + u % 3], -scale, None, ALU.mult), sem(f"{name}_peak"), u + 1)
                    if u >= 1:
                        h, qt = units[u - 1]
                        w = (qt + 1) * P
                        dve.wait_ge(sem(f"{name}_exp"), u)
                        r = st[:, 12 + (u - 1) % 3:13 + (u - 1) % 3]
                        link(v.reciprocal(r, st[:, 4 + (u - 1) % 3:5 + (u - 1) % 3]))
                        link(ts(tile(smt[(u - 1) % 3])[:, 0:w], tile(smt[(u - 1) % 3])[:, 0:w], r, None, ALU.mult), sem(f"{name}_probs"), u)

            def gated_up(sfx, conv):
                for p in range(11):
                    for j in range(2):
                        i, job = 2 * p + j, 4 * p + j
                        filled(dve, "up" + sfx, job)
                        if i >= 4:
                            dve.wait_ge(sem("gated" + sfx), i - 3)
                        conv(job, i, tile(i % 4))
                    for j in range(2):
                        i, job = 2 * p + j, 4 * p + 2 + j
                        filled(dve, "up" + sfx, job)
                        dve.wait_ge(sem("gelu" + sfx), i + 1)
                        link(tt(tile(G0 + i), tile(i % 4), pst("up" + sfx, job), ALU.mult), *read("up" + sfx, job))
                        link(v.memset(st[:, 63:64], 0.0), sem("gated" + sfx), i + 1)

            def tell(s, value):
                link(v.memset(st[:, 63:64], 0.0), s, value)

            def rope(dst, src, job, i, tmp):
                filled(dve, job, i)
                link(tt(tmp, pst(job, i), trig[:, 1, :], ALU.mult), *read(job, i))
                link(tt(dst, src, trig[:, 0, :], ALU.mult))
                link(tt(dst, dst, tmp, ALU.add))

            def block_1():
                dve.wait_ge(cols_in, 32)
                for i in range(12):
                    filled(dve, "ada", i)
                    link(tt(modT[:, 4 * i:4 * i + 4], pst("ada", i)[:, 0:4], col("b_ada", 4 * i, 4), ALU.add), *read("ada", i))
                link(stt(amp[:, 0, :], modT[:, 8:16], 1.0, col("norm1", 0, 8), ALU.add, ALU.mult))
                link(stt(amp[:, 1, :], modT[:, 32:40], 1.0, col("norm2", 0, 8), ALU.add, ALU.mult))
                normed("rms1", tile(33), lambda i: amp[:, 0, i:i + 1], lambda i: modT[:, i:i + 1])
                for i in range(24):
                    filled(dve, "qkv", i)
                    if 8 <= i < 18:
                        pass
                    causal_conv("qkv", i, tile(Q0 + i), [col("conv", 4 * i + j) for j in range(4)], None, None)
                    tell(sem("conv"), i + 1)
                filled(dve, "ab")
                ab = pst("ab")[:, 0:64].rearrange("p (t c) -> p t c", c=16)
                link(tt(sm4[:, AB_X, :, 0:8], ab[:, :, 0:8], bm(col("dt_bias", 0, 8), NT), ALU.add))
                link(v.tensor_copy(sm4[:, AB_B, :, 0:8], ab[:, :, 8:16]), *read("ab"))
                link(ts(sm4[:, AB_A, :, 0:8], sm4[:, AB_X, :, 0:8], -1.0, None, ALU.mult))
                link(tt(sm4[:, AB_A, :, 0:8], sm4[:, AB_X, :, 0:8], sm4[:, AB_A, :, 0:8], ALU.max), sem("ab_dve"), 1)
                dve.wait_ge(sem("ab_act"), 1)
                link(stt(sm4[:, AB_X, :, 0:8], sm4[:, AB_X, :, 0:8], 0.0, sm4[:, AB_E, :, 8:16], ALU.max, ALU.add))
                link(stt(sm4[:, G, :, 0:8], sm4[:, AB_X, :, 0:8], -1.0, bm(sm4[:, AB_R, 0, 8:16], NT), ALU.mult, ALU.mult), sem("g_ready"), 1)
                link(ts(sm4[:, AB_B, :, 0:8], sm4[:, AB_B, :, 0:8], 1.0, None, ALU.add))
                link(v.reciprocal(sm4[:, BETA, :, 0:8], sm4[:, AB_B, :, 0:8]), sem("beta_ready"), 1)
                for i in range(16):
                    dve.wait_ge(sem("l2_rstd"), i + 1)
                    link(tt(tile(Q0 + i), tile(Q0 + i), tile(30 + i % 2), ALU.mult), sem("qk_normed"), i + 1)
                filled(dve, "gc")
                link(v.tensor_copy(sm4[:, GC, :, :], pst("gc")[:, 0:64].rearrange("p (t c) -> p t c", c=16)), *read("gc"))
                link(tt(sm4[:, KDEC, :, 0:8], sm4[:, GC, :, 8:16], sm4[:, GC, :, 0:8], ALU.subtract), sem("gc_dve"), 1)
                dve.wait_ge(sem("gc_act"), 1)
                link(tt(sm4[:, BE, :, 0:8], sm4[:, BETA, :, 0:8], sm4[:, EGC, :, 0:8], ALU.mult))
                for hf in range(2):
                    link(v.memset(pair(ST, hf), 0.0), sem("gdn_state"), hf + 1)
                for t in range(NT):
                    for hf in range(2):
                        n, h0 = 2 * t + hf + 1, hf * HALF
                        filled(dve, ("gb", t, hf))
                        link(tt(pair(DT, hf), heads4(("gb", t, hf)), bh(tok(GC, t, h0, 4)), ALU.subtract), sem("gb_minus"), n)
                        link(tt(pair(DT, hf), pair(DT, hf), bm(const("neg_after")), ALU.add), sem("gb_masked"), n)
                        dve.wait_ge(sem("gdn_decay"), n)
                        filled(dve, ("kk", t, hf))
                        link(tt(pair(AM, hf), heads4(("kk", t, hf)), pair(DT, hf), ALU.mult), *read(("kk", t, hf)))
                        filled(dve, ("bb", t, hf))
                        link(tt(pair(AM, hf), heads4(("bb", t, hf)), pair(AM, hf), ALU.mult), *read(("bb", t, hf)))
                        tell(sem("gdn_a"), n)
                        filled(dve, ("kq", t, hf))
                        link(tt(pair(ATT, hf), heads4(("kq", t, hf)), pair(DT, hf), ALU.mult), *read(("kq", t, hf)))
                        tell(sem("gdn_att"), n)
                        filled(dve, ("kt", t, hf))
                        link(tt(pair(KD_ROW, hf), heads4(("kt", t, hf)), bh(tok(KDEC, t, h0, 4)), ALU.mult), *read(("kt", t, hf)))
                        filled(dve, ("vt", t, hf))
                        link(tt(pair(VB, hf), heads4(("vt", t, hf)), bh(tok(BETA, t, h0, 4)), ALU.mult), *read(("vt", t, hf)))
                    inverse("gdn", t, 7)
                    for hf in range(2):
                        filled(dve, ("ks", t, hf))
                        link(tt(pair(RHS, hf), heads4(("ks", t, hf)), bh(tok(BE, t, hf * HALF, 4)), ALU.mult), *read(("ks", t, hf)))
                        link(tt(pair(RHS, hf), pair(VB, hf), pair(RHS, hf), ALU.subtract), sem("gdn_rhs"), 2 * t + hf + 1)
                    for hf in range(2):
                        filled(dve, ("su", t, hf))
                        link(tt(pair(ST, hf), pair(ST, hf), bh(tok(EGC, t, 8 + hf * HALF, 4)), ALU.mult))
                        link(tt(pair(ST, hf), pair(ST, hf), heads4(("su", t, hf)), ALU.add), *read(("su", t, hf)))
                        tell(sem("gdn_state"), 2 * t + hf + 3)
                for h in range(H):
                    dve.wait_ge(sem("o_rstd"), h + 1)
                    link(stt(tile(V0 + h), tile(V0 + h), col("dn_norm"), tile(30 + h % 2), ALU.mult, ALU.mult), sem("o_scaled"), h + 1)
                for h in range(H):
                    emptied(dve, "z", h)
                    link(tt(tile(V0 + h), tile(V0 + h), tile(Q0 + h), ALU.mult), sem("o_dn"), h + 1)
                dve.wait_ge(pos_in, 16)
                link(v.tensor_copy(tile(8), trig[:, 0, :].bitcast(I32)))
                link(ts(tile(8), tile(8), col("inv_freq"), None, ALU.mult))
                for i in range(2):
                    dst = tile(9) if i == 0 else tile(10)
                    link(ts(tile(11), tile(8), 1.0 / (2 * np.pi), 0.25 * i, ALU.mult, ALU.add))
                    link(ts(tile(11), tile(11), 12582912.0, None, ALU.add))
                    link(ts(tile(11), tile(11), -12582912.0, None, ALU.add))
                    link(stt(dst, tile(11), -TURN[0], tile(8), ALU.mult, ALU.add))
                    link(stt(dst, tile(11), -TURN[1], dst, ALU.mult, ALU.add))
                    link(stt(dst, tile(11), -TURN[2], dst, ALU.mult, ALU.add))
                    if i:
                        link(ts(dst, dst, float(np.float32(np.pi / 2)), None, ALU.add))
                    link(ts(dst, dst, PI_IN, -PI_IN, ALU.min, ALU.max), sem("angle"), i + 1)
                dve.wait_ge(sem("kv_rstd"), 1)
                for k in range(2):
                    link(stt(tile(CKV + k), tile(CKV + k), col("kv_norm", k), tile(15), ALU.mult, ALU.mult), sem("ckv"), k + 1)
                dve.wait_ge(sem("kr_sq"), 1)
                link(ts(tile(KROPE), tile(KROPE), col("kn_rope"), None, ALU.mult), sem("kr_w"), 1)
                dve.wait_ge(sem("trig"), 2)
                for h in range(H):
                    dve.wait_ge(sem("k_rstd"), h + 1)
                    rs = tile(48 + h % 2)
                    b = slice(64 * (h % 2), 64 * (h % 2) + 64)
                    link(stt(tile(KN + h), tile(KN + h), col("kn_nope"), rs, ALU.mult, ALU.mult))
                    link(v.tensor_copy(tile(KR + h // 2)[b, :], rs[b, :]), sem("k_scaled"), h + 1)
                rope(tile(KRW), tile(KROPE), "krot", 0, tile(12))
                for p in range(4):
                    link(tt(tile(KR + p), tile(KR + p), tile(KRW), ALU.mult))
                filled(dve, "mv", 7)
                link(v.memset(st[:, 62:63], 0.0), sem("ckv_free"), 1)
                for h in range(H):
                    dve.wait_ge(sem("q_rstd"), h + 1)
                    rs = tile(48 + h % 2)
                    b = slice(64 * (h % 2), 64 * (h % 2) + 64)
                    link(stt(tile(QN + h), tile(QN + h), col("qn_nope"), rs, ALU.mult, ALU.mult))
                    link(stt(tile(QR + h // 2)[b, :], tile(QR + h // 2)[b, :], col("qn_rope")[b, :], rs[b, :], ALU.mult, ALU.mult),
                         sem("q_scaled"), h + 1)
                    if h % 2:
                        link(v.memset(st[:, 62:63], 0.0), sem("qr_w"), h // 2 + 1)
                for p in range(4):
                    rope(tile(QR + p), tile(QR + p), "qrot", p, tile(8 + p % 2))
                link(v.memset(st[:, 62:63], 0.0), sem("mla_qk"), 1)
                attention("mla", UNITS, 192 ** -0.5, (12, 13, 14), lambda qt: wide[:, 0, S - (qt + 1) * P:S])
                for fb in range(2):
                    for m in range(4):
                        emptied(dve, f"gate_dn{fb}", m)
                        filled(dve, f"y_dn{fb}", m)
                        if m == 0 and fb == 0:
                            emptied(dve, ("mla", "values", 31))
                        link(tt(tile(MIX + 4 * fb + m), tile(8 + m), pst(f"y_dn{fb}", m), ALU.mult), *read(f"y_dn{fb}", m))
                        tell(sem("gate_used"), 8 * fb + m + 1)
                    for m in range(4):
                        emptied(dve, f"gate_mla{fb}", m)
                        filled(dve, f"y_mla{fb}", m)
                        link(tt(tile(12 + m % 2), tile(8 + m), pst(f"y_mla{fb}", m), ALU.mult), *read(f"y_mla{fb}", m))
                        tell(sem("gate_used"), 8 * fb + 4 + m + 1)
                        link(tt(tile(MIX + 4 * fb + m), tile(MIX + 4 * fb + m), tile(12 + m % 2), ALU.add), sem("mix"), 4 * fb + m + 1)
                for i in range(KD):
                    filled(dve, "wo", i)
                    link(stt(xT[:, i, :], pst("wo", i), modT[:, 16 + i:17 + i], xT[:, i, :], ALU.mult, ALU.add), *read("wo", i))
                    tell(sem("x1"), i + 1)
                normed("rms2", tile(9), lambda i: amp[:, 1, i:i + 1], lambda i: modT[:, 24 + i:25 + i])

                def conv(job, i, dst):
                    causal_conv("up", job, dst, [col("fconv", 3 * i + j) for j in range(3)], None, None, bias=col("fbias", i))
                    tell(sem("fconv"), i + 1)

                filled(dve, "rms2")
                gated_up("", conv)
                for i in range(KD):
                    filled(dve, "down", i)
                    link(stt(xT[:, i, :], pst("down", i), modT[:, 40 + i:41 + i], xT[:, i, :], ALU.mult, ALU.add), *read("down", i))
                    tell(sem("x2"), i + 1)

            def block_2():
                if 1 not in parts:
                    dve.wait_ge(cols_in, 32)
                    dve.wait_ge(consts_in, 32)
                    dve.wait_ge(x_in, 16)
                link(ts(sm2[:, OM_MU:OM_MU + 14], col("mu", 0, 14), -1.0, 1.0, ALU.mult, ALU.add))
                link(ts(sm2[:, OM_KA:OM_KA + 4], col("k_a", 0, 4), -1.0, 1.0, ALU.mult, ALU.add))
                normed("rms3", tile(49), lambda i: col("norm1_2", i), None)
                for i in range(14):
                    job, k = ("rkv", i) if i < 12 else ("wag", i - 12)
                    filled(dve, job, k)
                    causal_conv(job, k, tile(i), [col("mu", i), sm2[:, OM_MU + i:OM_MU + i + 1]], None, None)
                    tell(sem("shifted"), i + 1)
                for p in range(4):
                    filled(dve, "kkn", p)
                    if p >= 2:
                        dve.wait_ge(sem("kk_rstd"), p - 1)
                    link(ts(tile(36 + p % 2), pst("kkn", p), 1e-24, None, ALU.max), *read("kkn", p))
                    tell(sem("kk_clamped"), p + 1)
                    dve.wait_ge(sem("kk_rstd"), p + 1)
                    link(stt(tile(KAP + p), tile(KT + p), col("k_k", p), tile(38 + p % 2), ALU.mult, ALU.mult), sem("kk_used"), p + 1)
                    emptied(dve, "aup", p)
                    link(ts(tile(47), tile(BT + p), col("k_a", p), sm2[:, OM_KA + p:OM_KA + p + 1], ALU.mult, ALU.add))
                    link(tt(tile(KT + p), tile(KT + p), tile(47), ALU.mult))
                    link(tt(tile(BT + p), tile(BT + p), tile(KAP + p), ALU.mult))
                for p in range(4):
                    link(stt(tile(44 + p), tile(RHO + p), col("r_k", p), tile(KT + p), ALU.mult, ALU.mult), sem("bonus_in"), p + 1)
                for p in range(4):
                    filled(dve, "bon", p)
                    link(tt(tile(BV + p), pst("bon", p), tile(V2 + p), ALU.mult), *read("bon", p))
                for p in range(4):
                    gc = tile(GCUM + p % 2)
                    emptied(dve, "wup", p)
                    link(ts(tile(LD + p), tile(LD + p), -float(np.exp(-0.5)), None, ALU.mult))
                    link(v.tensor_tensor_scan(gc, wide[:, 3, :], tile(LD + p), 0.0, ALU.mult, ALU.add))
                    link(tt(tile(36), gc, tile(LD + p), ALU.subtract), sem("g_cum"), p + 1)
                    dve.wait_ge(sem("decays"), p + 1)
                    link(tt(tile(RHO + p), tile(RHO + p), tile(40), ALU.mult))
                    link(tt(tile(KAP + p), tile(KAP + p), tile(41), ALU.mult))
                    link(tt(tile(BT + p), tile(BT + p), tile(42), ALU.mult))
                    link(tt(tile(KT + p), tile(KT + p), tile(42), ALU.mult), sem("rw_ready"), p + 1)
                link(v.memset(tile(ST2)[:, 0:256], 0.0), sem("rw_state"), 1)
                for t in range(NT):
                    for par in range(2):
                        n = 2 * t + par + 1
                        filled(dve, ("rm", t, par))
                        link(v.tensor_copy(pair(36, par), heads4(("rm", t, par))), *read(("rm", t, par)))
                        tell(sem("rw_a"), n)
                        filled(dve, ("rn", t, par))
                        link(tt(pair(NTR, par), heads4(("rn", t, par)), bm(const("strict64")), ALU.mult), *read(("rn", t, par)))
                        tell(sem("rw_n"), n)
                        for k, (what, dst) in enumerate((("rb", BRT), ("rk", KRT))):
                            filled(dve, (what, t, par))
                            link(tt(pair(dst, par), heads4((what, t, par)), bm(const("incl64")), ALU.mult), *read((what, t, par)))
                            tell(sem("rw_b"), 2 * n + k - 1)
                    inverse("rw", t, 6)
                    emptied(dve, ("nv", t))
                    for e in range(2):
                        eb, n = slice(64 * e, 64 * e + 64), 2 * t + e
                        for par in range(2):
                            filled(dve, ("rs", t, e, par))
                            view = lambda x: x[eb, :].rearrange("p (k two c) -> p k two c", two=2, c=64)[:, :, par, :]
                            link(tt(view(tile(RSB)), pst(("rs", t, e, par))[eb, 0:256].rearrange("p (k c) -> p k c", c=64), view(tile(NVT)), ALU.add),
                                 *read(("rs", t, e, par)))
                        tell(sem("rw_rhs"), n + 1)
                        filled(dve, ("rz", t, e))
                        link(tt(tile(ST2)[:, 0:256], tile(ST2)[:, 0:256], pst(("rz", t, e))[:, 0:256], ALU.add), *read(("rz", t, e)))
                        s4 = tile(ST2)[:, 0:256].rearrange("p (k c) -> p k c", c=64)
                        link(tt(s4, s4, bh(sm2[:, EC + n:EC + 32:8], 64), ALU.mult), sem("rw_state"), n + 2)
                    filled(dve, ("yi", t))
                    for par in range(2):
                        emptied(dve, ("ry", t, 1, par))
                    y4 = ar[:, RHO:RHO + 4, t * P:(t + 1) * P]
                    link(tt(y4, y4, heads4(("yi", t)), ALU.add), *read(("yi", t)))
                    for k in range(4):
                        tell(sem("y_sum"), 4 * t + k + 1)
                for p in range(4):
                    filled(dve, "gmean", p)
                    link(stt(tile(RHO + p), pst("gmean", p), -1.0 / 64, tile(RHO + p), ALU.mult, ALU.add), *read("gmean", p))
                    tell(sem("gn_centred"), p + 1)
                for p in range(4):
                    dve.wait_ge(sem("gn_rstd"), p + 1)
                    link(stt(tile(RHO + p), tile(RHO + p), col("lnx_g", p), tile(41 + p % 2), ALU.mult, ALU.mult), sem("gn_used"), p + 1)
                    link(stt(tile(RHO + p), tile(RHO + p), col("lnx_b", p), tile(BV + p), ALU.add, ALU.add))
                    link(tt(tile(RHO + p), tile(RHO + p), tile(G2 + p), ALU.mult), sem("y_rw"), p + 1)
                filled(dve, "wi")
                link(v.tensor_copy(sm2[:, WI:WI + 32], pst("wi")[:, 0:32]), *read("wi"))
                dve.wait_ge(trig_in, 16)
                for i in range(5):
                    rope(tile(QI + i), tile(QI + i), "irot", i, tile(39))
                link(v.memset(st[:, 62:63], 0.0), sem("index_qk"), 1)
                for i in range(24):
                    q, h = i // 8, i % 8
                    w = (q + 2) * P
                    acc, wt = tile(SCO + q)[:, 0:w], sm2[:, WI + 8 * (q + 1) + h:WI + 8 * (q + 1) + h + 1]
                    emptied(dve, "index", i)
                    if h == 0:
                        link(ts(acc, tile(REL[i % 2])[:, 0:w], wt, None, ALU.mult), sem("index_used"), i + 1)
                    else:
                        link(stt(acc, tile(REL[i % 2])[:, 0:w], wt, acc, ALU.mult, ALU.add), sem("index_used"), i + 1)
                for i in range(8):
                    rope(tile(AQ + i), tile(AQ + i), "arot", i, tile(39))
                link(v.memset(st[:, 62:63], 0.0), sem("dsa_qk"), 1)
                for q in range(3):
                    w = (q + 2) * P
                    acc, work, sel = (tile(i)[:, 0:w] for i in (SCO + q, WORK, SEL + q))
                    top = sm2[:, TOP8:TOP8 + 8]
                    link(stt(acc, acc, 64 ** -0.5 * 8 ** -0.5, wide[:, 2, S - w:S], ALU.mult, ALU.add))
                    for r in range(TOPK // 8):
                        src = work if r else acc
                        link(v.max(top, src))
                        link(v.match_replace(work, top, src, -3.3e38))
                    link(tt(sel, work, acc, ALU.is_equal))
                    link(ts(sel, sel, NEG, None, ALU.mult))
                for m in range(8):
                    filled(dve, "yr", m)
                    emptied(dve, "gate_a", m)
                    link(tt(tile(MERGE + m), tile(MERGE + m), pst("yr", m), ALU.mult), *read("yr", m))
                attention("dsa", UNITS, 64 ** -0.5, (30, 31, 32),
                          lambda qt: tile(SEL + qt - 1)[:, 0:(qt + 1) * P] if qt else wide[:, 1, S - P:S])
                for m in range(8):
                    filled(dve, "ya", m)
                    emptied(dve, "gate_b", m)
                    link(tt(tile(AQ + m), tile(AQ + m), pst("ya", m), ALU.mult), *read("ya", m))
                    link(tt(tile(MERGE + m), tile(MERGE + m), tile(AQ + m), ALU.add), sem("merged"), m + 1)
                for i in range(KD):
                    filled(dve, "wout", i)
                    link(tt(xT[:, i, :], xT[:, i, :], pst("wout", i), ALU.add), *read("wout", i))
                    tell(sem("x3"), i + 1)
                normed("rms4", tile(9), lambda i: col("norm2_2", i), None)
                for p in range(11):
                    for j in range(2):
                        i, job = 2 * p + j, 4 * p + 2 + j
                        filled(dve, "up_2", job)
                        emptied(dve, "up_2", 4 * p + j)
                        link(tt(tile(G0 + i), tile(i % 4), pst("up_2", job), ALU.mult), *read("up_2", job))
                        tell(sem("gated_2"), i + 1)
                for i in range(KD):
                    filled(dve, "down_2", i)
                    link(tt(xT[:, i, :], xT[:, i, :], pst("down_2", i), ALU.add), *read("down_2", i))
                    tell(sem("x4"), i + 1)
                dve.wait_ge(sem("rms5_rstd"), 1)
                for i in range(KD):
                    link(stt(xT[:, i, :], xT[:, i, :], col("normf", i), tile(9), ALU.mult, ALU.mult), sem("y_out"), i + 1)

            if 1 in parts:
                block_1()
            if 2 in parts:
                block_2()

        @block.gpsimd
        def _(pool):
            link = linker(pool, sem("pool_chain"))
            g = nc.gpsimd
            tt = g.tensor_tensor

            def inverse(name, t, levels):
                am, xtr, xx, mk, p1 = BASES[name]
                for lv in range(levels):
                    for hf in range(2):
                        if lv == 0:
                            pool.wait_ge(sem(f"{name}_a"), 2 * t + hf + 1)
                            s, value = sem(f"{name}_masked0"), 2 * t + hf + 1
                        else:
                            s, value = sem(f"{name}_masked"), (t * (levels - 1) + lv - 1) * 2 + hf + 1
                            if lv == 1:
                                pool.wait_ge(sem(f"{name}_xt0"), 2 * t + hf + 1)
                            else:
                                filled(pool, (name, "p1", t, lv - 1, hf))
                        link(tt(pair(mk, hf), pair(am, hf), bm(const(f"lvl{lv}")), ALU.mult), s, value)

            def block_1():
                pool.wait_ge(consts_in, 32)
                for i in range(16):
                    pool.wait_ge(sem("conv_silu"), i + 1)
                    if i >= 4:
                        filled(pool, "l2", i - 4)
                    link(tt(tile(24 + i % 4), tile(Q0 + i), tile(Q0 + i), ALU.mult), sem("l2_sq"), i + 1)
                for t in range(NT):
                    for hf in range(2):
                        n = 2 * t + hf + 1
                        emptied(pool, ("gb", t, hf))
                        if n == 1:
                            pool.wait_ge(sem("qk_normed"), 16)
                        if t:
                            filled(pool, ("ot", t - 1, hf))
                        link(tt(pair(QE, hf), ar[:, Q0 + hf * HALF:Q0 + (hf + 1) * HALF, t * P:(t + 1) * P], pair(EGB, hf), ALU.mult),
                             sem("gdn_qe"), n)
                    inverse("gdn", t, 7)
                emptied(pool, ("ot", NT - 1, 1))
                emptied(pool, ("ot", NT - 1, 0))
                for h in range(H):
                    if h >= 4:
                        filled(pool, "onorm", h - 4)
                    link(tt(tile(24 + h % 4), tile(V0 + h), tile(V0 + h), ALU.mult), sem("onorm_sq"), h + 1)

            if 1 in parts:
                block_1()
            if 2 in parts:
                pool.wait_ge(consts_in, 32)
                for t in range(NT):
                    inverse("rw", t, 6)


_T = 2 * np.pi
TURN = [201.0 / 32.0]
_r = _T - TURN[0]
TURN.append(float(np.float32(np.round(_r * 2 ** 22) / 2 ** 22)))
TURN.append(float(np.float32(_r - TURN[1])))
PI_IN = float(np.nextafter(np.float32(np.pi), np.float32(0)))


def _panels(w, width=S):
    out = []
    kt = w.shape[0] // P
    per = PANEL // width
    for n in range(0, w.shape[1], width):
        for k in range(0, kt, per):
            part = w[k * P:min(kt, k + per) * P, n:n + width]
            x = np.zeros((P, per, width), w.dtype)
            x[:, :part.shape[0] // P, :part.shape[1]] = part.reshape(-1, P, part.shape[1]).transpose(1, 0, 2)
            out.append(x.reshape(P, PANEL))
    return out


def _col(v):
    return np.asarray(v).reshape(-1, P).T


def _row(v):
    return np.broadcast_to(np.asarray(v).reshape(1, -1), (P, np.asarray(v).size))


def _pairs(w, n):
    k = w.shape[0]
    return w.reshape(k, 2, n // 256, 256).transpose(0, 2, 1, 3).reshape(k, 2 * n)


def lay_out_2(f, c, out, panels, parts):
    w = f["w_in_2"]
    c["norm1_2"], c["norm2_2"], c["normf"] = _col(f["norm1_g_2"]), _col(f["norm2_g_2"]), _col(f["normf_g_2"])
    c["mu"] = _col(f["tshift_mu_2"])
    for n in ("w0", "a0", "k_k", "k_a", "lnx_g", "lnx_b"):
        c[n] = _col(f[n + "_2"])
    c["r_k"] = _col(f["r_k_2"].reshape(-1))
    c["ln1024"] = np.full((P, 1), 10 * np.log(2.0), np.float32)
    out["lora"] = np.ascontiguousarray(np.stack([np.concatenate([f["w_decay_up_2"], f["a_up_2"]], 0), f["g_up_2"]], 1))
    out["wix"] = np.ascontiguousarray(w[:, 3904:3912].reshape(KD, P, 8).transpose(1, 0, 2))
    if 2 in parts:
        kidx = w[:, 3840:3904]
        panels += _panels(w[:, 0:1536]) + _panels(w[:, 1536:1792])
        panels += _panels(np.concatenate([w[:, 3328:3840], kidx, kidx], 1))
        panels += _panels(w[:, 1792:2816]) + _panels(w[:, 2816:3328])
        panels += _panels(w[:, 3912:4936]) + _panels(f["w_o_rwkv_2"], D) + _panels(w[:, 4936:5960]) + _panels(f["w_o_att_2"], D)
        panels += _panels(f["w_out_2"]) + _panels(_pairs(f["w_ffn_in_2"], FF)) + _panels(f["w_ffn_out_2"])


def lay_out(i, parts=(1, 2)):
    f = {k: np.asarray(v) for k, v in i.items()}
    cm, wide, inv = constants()
    out = {"cm": cm, "wide": np.ascontiguousarray(wide[:, [0, 1, 2, 5]]), "trig": np.ascontiguousarray(wide[:, [3, 4]])}
    c = {"one": np.ones((P, 1), np.float32), "eps": np.full((P, 1), EPS, np.float32),
         "qscale": np.full((P, 1), -0.5 * np.log(128.0), np.float32), "lnx": np.full((P, 1), LNX_EPS, np.float32), "inv_freq": inv}
    panels = []
    if True:
        w_in = f["w_in"][0]
        at = np.cumsum([0, 1024, 1024, 1024, 1024, 8, 8, 1536, 256, 64, 1024, 1024])
        q, k, v, z, al, be, mq, ckv, kr, gd, gm = (w_in[:, at[j]:at[j + 1]] for j in range(11))
        c["b_ada"], c["norm1"] = _col(f["b_ada"][0]), _col(f["norm1_w"][0])
        c["conv"] = f["dn_conv_w"][0].reshape(4, 24, P).transpose(2, 1, 0).reshape(P, 96)
        c["dn_norm"] = _col(f["dn_norm_w"][0])
        c["kv_norm"] = _col(f["mla_kv_norm_w"][0])
        for n, w in (("qn", f["mla_q_norm_w"][0]), ("kn", f["mla_k_norm_w"][0])):
            c[n + "_nope"] = _col(w[:128])
            c[n + "_rope"] = _col(np.concatenate([w[128:], w[128:]]))
        c["norm2"] = _col(f["norm2_w"][0])
        c["fconv"] = f["ffn_conv_w"][0].reshape(3, NF, P).transpose(2, 1, 0).reshape(P, 3 * NF)
        c["fbias"] = _col(f["ffn_conv_b"][0])
        c["a_log"], c["dt_bias"] = _row(f["dn_a_log"][0]), _row(f["dn_dt_bias"][0])
        mq = mq.reshape(D, H, 192)
        nope, rope = mq[:, :, :128].reshape(D, 1024), mq[:, :, 128:].reshape(D, 512)
        if 1 in parts:
            panels += _panels(f["w_ada"][0])
            panels += _panels(np.concatenate([q, k, v], 1))
            panels += _panels(z) + _panels(np.concatenate([nope, rope], 1)) + _panels(np.concatenate([ckv, kr, kr], 1))
            panels += [np.concatenate([w.reshape(2, P, 1024).transpose(1, 0, 2).reshape(P, 2048)
                                       for w in (f["mla_w_uk"][0], f["mla_w_uv"][0])], 1)]
            gd, gm, yd, ym = _panels(gd), _panels(gm), _panels(f["w_out_dn"][0]), _panels(f["w_out_mla"][0])
            panels += [p[b] for b in range(2) for p in (gd, yd, gm, ym)]
            panels += _panels(f["w_o"][0]) + _panels(_pairs(f["ffn_w_up"][0], FF)) + _panels(f["ffn_w_down"][0])
        out["wab"] = np.ascontiguousarray(np.concatenate([al, be], 1).reshape(KD, P, 16).transpose(1, 0, 2))
        out["cT"] = np.ascontiguousarray(_col(f["c"][0]))
        out["posb"] = np.ascontiguousarray(_row(f["positions"][0]).astype(np.int32))
    lay_out_2(f, c, out, panels, parts)
    out["panels"] = np.stack(panels)
    out["cols"] = np.concatenate([c[n] if n in c else np.zeros((P, w), np.float32) for n, w in COLS], 1).astype(np.float32)
    out["xT"] = np.ascontiguousarray(f["x"][0].T.reshape(KD, P, S).transpose(1, 0, 2))
    return out


def kernel(**inputs):
    import concourse.bacc as bacc
    from concourse.bass_utils import run_bass_kernel_spmd

    arrays = lay_out(inputs)
    nc = bacc.Bacc("TRN2", target_bir_lowering=False, num_devices=1)
    aps = {n: nc.dram_tensor(n + "_dram", x.shape, mybir.dt.from_np(x.dtype), kind="ExternalInput").ap() for n, x in arrays.items()}
    aps["out"] = nc.dram_tensor("out_dram", (P, KD, S), F32, kind="ExternalOutput").ap()
    build(nc, aps)
    r = run_bass_kernel_spmd(nc, [{n + "_dram": x for n, x in arrays.items()}], core_ids=[0])
    y = r.results[0]["out_dram"]
    return np.ascontiguousarray(y.transpose(1, 0, 2).reshape(D, S).T).reshape(1, S, D)
```

```python
from contextlib import ExitStack

import numpy as np

import concourse.bass as bass
from concourse import mybir

F32 = mybir.dt.float32
F32R = mybir.dt.float32r
I32 = mybir.dt.int32
ALU = mybir.AluOpType
ACT = mybir.ActivationFunctionType
AX_X = mybir.AxisListType.X

P = 128
S = 512
D = 1024
KD = D // P
NT = S // P
H = 8
FF = 2816
NF = FF // P
HALF = H // 2
RANK = 256
ROPE = 64
N64 = 64
TOPK = 128
EPS = 1e-6
LNX_EPS = 64e-5
NEG = -1e30
LOW = -3e38
PANEL = 2048
RAW = 2
SPLIT = 2
ADA_BASE = (8, 16, 34, 42)
TMP = 12


class Order:

    def __init__(self):
        self.job, self.last, self.n, self.steps = {}, {}, 0, 0

    def add(self, name, jobs=1, steps=1, first=0):
        for i in range(first, first + jobs):
            self.job[name, i] = self.n
            for s in range(steps):
                self.steps += 1
                self.last[name, i, s] = self.steps
            self.last[name, i] = self.steps
            self.n += 1

    def add_together(self, name, jobs, steps):
        for i in jobs:
            self.job[name, i] = self.n
            self.n += 1
        for s in range(steps):
            for i in jobs:
                self.steps += 1
                self.last[name, i, s] = self.last[name, i] = self.steps

    def bank(self, name, i=0):
        return self.job[name, i] % 8

    def use(self, name, i=0):
        return self.job[name, i] // 8


CONST_128 = ["ident", "ones", "top64", "low64", "same64", "rot", "utri", "neg_after", "strict64",
             "incl64"] + [f"lvl{i}" for i in range(7)]


def constants():
    j, c = np.meshgrid(np.arange(P), np.arange(P), indexing="ij")
    m = {}
    m["ident"] = j == c
    m["ones"] = j >= 0
    m["top64"] = j < 64
    m["low64"] = j >= 64
    m["same64"] = j // 64 == c // 64
    same = j // 64 == c // 64
    m["rot"] = np.where(same & (j % 64 == c % 64 + 32), -1.0, 0) + np.where(same & (j % 64 + 32 == c % 64), 1.0, 0)
    m["utri"] = j <= c
    m["neg_after"] = np.where(j > c, NEG, 0)
    m["strict64"] = same & (j < c)
    m["incl64"] = same & (j <= c)
    for i in range(7):
        b = 1 << i
        m[f"lvl{i}"] = (j // (2 * b) == c // (2 * b)) & (j % (2 * b) < b) & (c % (2 * b) >= b)
    sq = np.stack([np.asarray(m[k], np.float32) for k in CONST_128], 1)
    wide = np.zeros((6, P, S), np.float32)
    q, k = j, c
    wide[0, :, S - P:] = np.where((q < 64) & (k >= 64), NEG, 0)
    wide[1, :, S - P:] = np.where(k > q, NEG, 0)
    wide[2, :, S - P:] = np.where(k > q, LOW, 0)
    half = 32
    inv = (1.0 / (np.float32(10000.0) ** (np.arange(half, dtype=np.float32) * np.float32(2.0) / np.float32(64)))).astype(np.float32)
    ang = np.arange(S, dtype=np.float32)[None, :] * inv[np.arange(P) % 32][:, None]
    wide[3] = np.cos(ang)
    wide[4] = np.sin(ang)
    wide[5] = (np.arange(S) % 64 != 0)[None, :]
    inv_mla = (np.float32(10000.0) ** (-np.arange(half, dtype=np.float32) / np.float32(half))).astype(np.float32)
    col = inv_mla[np.arange(P) % 32][:, None].astype(np.float32)
    return np.ascontiguousarray(sq), np.ascontiguousarray(wide.transpose(1, 0, 2)), np.ascontiguousarray(col)


COLS = [("one", 1), ("eps", 1), ("qscale", 1), ("lnx", 1), ("ln1024", 1), ("b_ada", 48), ("norm1", 8), ("conv", 96), ("dn_norm", 1),
        ("kv_norm", 2), ("qn_nope", 1), ("qn_rope", 1), ("kn_nope", 1), ("kn_rope", 1), ("norm2", 8), ("fconv", 66),
        ("fbias", 22), ("a_log", 8), ("dt_bias", 8), ("inv_freq", 1),
        ("norm1_2", 8), ("mu", 14), ("w0", 4), ("a0", 4), ("k_k", 4), ("k_a", 4), ("r_k", 4), ("lnx_g", 4), ("lnx_b", 4),
        ("norm2_2", 8), ("normf", 8)]
COL_AT, NCOLS = {}, 0
for _name, _width in COLS:
    COL_AT[_name] = NCOLS
    NCOLS += _width

def attention_order(order, name, units):
    n = len(units)
    for u in range(n + 3):
        if u < n:
            order.add((name, "scores", u))
        if 2 <= u < n + 2:
            order.add((name, "turn", u - 2))
        if u >= 3:
            order.add((name, "values", u - 3))


def inverse_order(order, name, t, levels):
    for hf in range(2):
        order.add((name, "x0", t, hf))
    for lv in range(1, levels):
        for hf in range(2):
            order.add((name, "p1", t, lv, hf))
        for hf in range(2):
            order.add((name, "xt", t, lv, hf))
            if lv < levels - 1:
                order.add((name, "x", t, lv, hf))


def plan_1(order):
    order.add("ada", 4)
    order.add("rms1")
    for m in range(12):
        order.add("qkv", 2, first=2 * m)
        if 2 <= m < 10:
            order.add("ada", first=2 + m)
    order.add("ab")
    order.add("l2", 16)
    order.add("gc")
    for t in range(NT):
        for hf in range(2):
            for what in ("gb", "bb", "kk", "kq", "kt", "vt"):
                order.add((what, t, hf))
        inverse_order(order, "gdn", t, 7)
        for what in ("ks", "vn", "ot", "su"):
            for hf in range(2):
                order.add((what, t, hf))
    order.add("onorm", 8)
    order.add("z", 8)
    order.add("mq", 12)
    order.add("mkv", 3)
    order.add("kvn")
    order.add("uk", 8)
    order.add("mv", 8)
    order.add("kss", 8)
    order.add("krot")
    order.add("qss", 8)
    order.add("qrot", 4)
    attention_order(order, "mla", UNITS)
    for fb in range(2):
        order.add(f"gate_dn{fb}", 4)
        order.add(f"y_dn{fb}", 4)
        order.add(f"gate_mla{fb}", 4)
        order.add(f"y_mla{fb}", 4)
    order.add("wo", 8)
    order.add("rms2")
    order.add("up", 44)
    for p in range(4):
        order.add_together("down", (2 * p, 2 * p + 1), 3)


def plan_2(order):
    order.add("rms3")
    order.add("rkv", 12)
    order.add("wag", 2)
    for what in ("wup", "aup", "gup", "kkn", "bon"):
        order.add(what, 4)
    for t in range(NT):
        for what in ("vrow", "brow", "krow"):
            order.add((what, t))
        for par in range(2):
            for what in ("rm", "rn", "rb", "rk"):
                order.add((what, t, par))
        order.add(("nv", t))
        inverse_order(order, "rw", t, 6)
        for e in range(2):
            for par in range(2):
                order.add(("rs", t, e, par))
            order.add(("ru", t, e))
            for par in range(2):
                order.add(("ry", t, e, par))
            order.add(("rz", t, e))
        order.add(("yi", t))
    order.add("gmean", 4)
    order.add("gvar", 4)
    order.add("ai", 5)
    order.add("wi")
    order.add("irot", 5)
    order.add("index", 24)
    order.add("aq", 8)
    order.add_together("av", range(NT), 2)
    order.add("arot", 8)
    order.add("gate_a", 8)
    order.add("yr", 8)
    attention_order(order, "dsa", UNITS)
    order.add("gate_b", 8)
    order.add("ya", 8)
    order.add("wout", 8)
    order.add("rms4")
    order.add("up_2", 44)
    for p in range(4):
        order.add_together("down_2", (2 * p, 2 * p + 1), 3)
    order.add("rms5")


UNITS = [(h, qt) for h in range(H) for qt in range(NT)]


def panel_plan(order):
    first, release = {}, []

    def add(stage, releases):
        first[stage] = len(release)
        release.extend(releases)

    last = order.last

    def each(stage, jobs, per=2):
        add(stage, [last[stage, min(i + per, jobs) - 1] for i in range(0, jobs, per)])

    each("qkv", 24)
    each("z", 8)
    each("mq", 12)
    each("mkv", 3)
    add("ukv", [last["uk", 7], last["mv", 7]])
    for fb in range(2):
        for what in ("gate_dn", "y_dn", "gate_mla", "y_mla"):
            each(f"{what}{fb}", 4)
    each("wo", 8)
    each("up", 44)
    add("down", [last["down", 2 * p + 1, s] for p in range(4) for s in range(3)])
    each("rkv", 12)
    each("wag", 2)
    each("ai", 5)
    each("aq", 8)
    add("av", [last["av", NT - 1, s] for s in range(2)])
    each("gate_a", 8)
    each("yr", 8, 4)
    each("gate_b", 8)
    each("ya", 8, 4)
    each("wout", 8)
    each("up_2", 44)
    add("down_2", [last["down_2", 2 * p + 1, s] for p in range(4) for s in range(3)])
    return first, release


def build(nc, a):
    order = Order()
    plan_1(order)
    plan_2(order)
    bank, use, last = order.bank, order.use, order.last
    panel_first, panel_release = panel_plan(order)

    with ExitStack() as ctx:
        def sb(name, shape, dt=F32):
            return ctx.enter_context(nc.sbuf_tensor(name, shape, dt))

        sems = {}

        def sem(name):
            if name not in sems:
                sems[name] = ctx.enter_context(nc.semaphore(name))
            return sems[name]

        with nc.sbuf_tensor("xT", [P, KD, S], F32) as xT:
            pass
        xL = sb("xL", [P, KD, S], F32R)
        hH = sb("hH", [P, KD, S], F32R)
        raw = sb("raw", [P, RAW, PANEL])
        W = sb("W", [P, SPLIT, 2, PANEL], F32R)
        with nc.sbuf_tensor("ar", [P, 50, S], F32) as ar:
            pass
        arR = sb("arR", [P, 50, S], F32R)
        cm = sb("cm", [P, len(CONST_128), P])
        wide = sb("wide", [P, 4, S])
        trig = sb("trig", [P, 2, S])
        cols = sb("cols", [P, NCOLS])
        modT = sb("modT", [P, 48])
        amp = sb("amp", [P, 2, KD])
        cT = sb("cT", [P, KD])
        wab = sb("wab", [P, KD, 16])
        narrow = sb("narrow", [P, 2, KD * 16], F32R)
        sm4 = sb("sm4", [P, 12, NT, 16])
        st = sb("st", [P, 64])
        wix = sb("wix", [P, KD, 8])
        sm2 = sb("sm2", [P, 160])
        ps = ctx.enter_context(nc.psum_tensor("ps", [P, 8, S], F32))

        def col(name, i=0, n=1):
            return cols[:, COL_AT[name] + i:COL_AT[name] + i + n]

        def const(name):
            return cm[:, CONST_128.index(name), :]

        pe_done = sem("pe_done")
        bank_read = [sem(f"bank{b}_read") for b in range(8)]
        panel_in = [sem(f"panel_in{s}") for s in range(RAW)]
        panel_high, panel_low = sem("panel_high"), sem("panel_low")
        ada_in = [sem(f"ada_in{b}") for b in range(4)]
        cols_in, consts_in, x_in, small2_in, ab_in, pos_in, trig_in, out_sent = (
            sem(n) for n in ("cols_in", "consts_in", "x_in", "small2_in", "ab_in", "pos_in", "trig_in", "out_sent"))

        def pst(name, i=0):
            return ps[:, bank(name, i), :]

        split_before = {}

        def ahead(eng, name, i=0):
            if eng in split_before:
                split_before[eng](last[name, i])

        def filled(eng, name, i=0):
            ahead(eng, name, i)
            eng.wait_ge(pe_done, last[name, i])

        def read(name, i=0):
            return bank_read[bank(name, i)], use(name, i) + 1

        def emptied(eng, name, i=0):
            ahead(eng, name, i)
            eng.wait_ge(*read(name, i))

        def linker(eng, chain):
            n = [0]

            def link(ins, s=None, value=None):
                if s is None:
                    n[0] += 1
                    s, value = chain, n[0]
                ins.then_inc(s, 1)
                eng.wait_ge(s, value)
            return link

        def tile(i):
            return ar[:, i, :]

        def tileR(i):
            return arR[:, i, :]

        def parts_in(high, low):
            return lambda k: (tileR(high[k]), tileR(low[k]))

        def h_mix(k):
            return hH[:, k, :], xL[:, k, :]

        def h_ff(k):
            return hH[:, k, :], tileR(H_LOW + k)

        def pair(i, hf):
            return ar[:, i + hf, :].rearrange("p (h c) -> p h c", c=P)

        def heads(i, h):
            return ar[:, i + h // HALF, (h % HALF) * P:(h % HALF + 1) * P]

        Q0, K0, V0 = 0, 8, 16
        BASES = {"gdn": (26, 36, 38, 40, 42), "rw": (36, 38, 40, 42, 44)}
        DT, AM, ATT, KD_ROW, VB, QE, XTR, XX, MK, P1, EGB, VN, ST = 24, 26, 28, 30, 32, 34, 36, 38, 40, 42, 44, 48, 46
        RHS = DT
        LORA = 46
        lora = ar[:, LORA:LORA + 2, :]
        RHO, KT, V2, WA, GD, BT, G2, LD, KAP, GCUM, BV = 0, 4, 8, 12, 13, 14, 18, 22, 26, 30, 32
        NTR, BRT, KRT, VROW, BROW, KROW, RSB, UU, ST2, NVT = 46, 48, 22, 24, 25, 12, 13, 30, 31, 46
        AQ, AK, QI, KI, AV, SEL, SCO, WORK, REL, OA, MERGE = 4, 8, 12, 16, 18, 22, 25, 28, (29, 17), 35, 42
        OM_MU, OM_KA, EC, WI, TOP8 = 0, 14, 24, 56, 88
        QN, QR, KN, KR, MV, CKV, KROPE, KRW = 24, 32, 36, 44, 0, 8, 10, 11
        MIX = 0
        H_LOW, G_HIGH, G_LOW, NG, G_REST = 42, 4, 20, 16, 36
        O_DN_HIGH, O_MLA_HIGH, MIX_HIGH = list(range(36, 44)), [32, 33, 34, 35, 44, 45, 46, 47], list(range(16, 24))
        CKV_HIGH, Y_HIGH, MERGE_HIGH = [12, 13], list(range(30, 34)), list(range(12, 20))

        def bh(x, n=P):
            return x.unsqueeze(2).to_broadcast([x.shape[0], x.shape[1], n])

        def bm(x, n=HALF):
            return x.unsqueeze(1).to_broadcast([x.shape[0], n, x.shape[1]])

        def heads4(name, i=0):
            return pst(name, i).rearrange("p (h c) -> p h c", c=P)

        AB_X, AB_A, AB_E, AB_B, G, GC, EGC, KDEC, BE, BETA, AB_R = range(11)

        def tok(which, t, lo=0, n=8):
            return sm4[:, which, t, lo:lo + n]

        SPLIT_AT = {"ckv": 0, "o_dn": 2, "o_mla": 10, "mix": 18, "y_rw": 26, "o_dsa": 30, "merged": 34}

        def part_ready(which, name, k):
            return sem(f"operand_{which}"), SPLIT_AT[name] + k + 1

        def norm_step(what, name, i=0):
            n = int(name[3:]) - 1
            return sem(f"norm_{what}"), n + 1 if what == "rstd" else KD * n + i + 1

        T_OF = {"rms1": 25, "rms2": 10, "rms3": 34, "rms4": 10}

        block = ctx.enter_context(nc.Block())

        @block.sync
        def _(sp):
            sp.dma_start(cols[:], a["cols"]).then_inc(cols_in, 16)
            sp.dma_start(cT[:], a["cT"]).then_inc(cols_in, 16)

            def load_ada(i):
                if i >= 4:
                    sp.wait_ge(sem("ada_used"), i - 1)
                b = i if i < 4 else 2 + i % 2
                sp.dma_start(ar[:, ADA_BASE[b]:ADA_BASE[b] + 8, :], a["ada"][i]).then_inc(ada_in[b], 16)

            load_ada(0)
            sp.dma_start(xT[:], a["xT"]).then_inc(x_in, 16)
            load_ada(1)
            load_ada(2)
            load_ada(3)
            sp.dma_start(cm[:], a["cm"]).then_inc(consts_in, 16)
            for n, free in enumerate(panel_release):
                if n >= RAW:
                    sp.wait_ge(panel_low, n - RAW + 1)
                sp.dma_start(raw[:, n % RAW, :], a["panels"][n]).then_inc(panel_in[n % RAW], 16)
                if n == 1:
                    sp.dma_start(wab[:], a["wab"]).then_inc(ab_in, 16)
                    sp.dma_start(wide[:], a["wide"]).then_inc(sem("wide_in"), 16)
                    sp.dma_start(trig[:, 0, :].bitcast(I32), a["posb"]).then_inc(pos_in, 16)
                if 1 <= n <= 8:
                    load_ada(n + 3)
                if n == panel_first["wo"]:
                    sp.wait_ge(pe_done, last["gate_mla1", 3])
                    sp.dma_start(xT[:], a["xT"]).then_inc(x_in, 16)
                if n == panel_first["rkv"]:
                    sp.wait_ge(sem("x2"), KD)
                    sp.dma_start(a["out"], xT[:]).then_inc(sem("x_kept"), 16)
                if n == panel_first["rkv"] + 1:
                    sp.wait_ge(pe_done, last["rms3", 0])
                    sp.dma_start(lora[:], a["lora"]).then_inc(small2_in, 16)
                    sp.dma_start(wix[:], a["wix"]).then_inc(small2_in, 16)
                    sp.dma_start(trig[:], a["trig"]).then_inc(trig_in, 16)
                if n == panel_first["wout"]:
                    sp.wait_ge(sem("x_kept"), 16)
                    sp.wait_ge(pe_done, last["gate_b", 7])
                    sp.dma_start(xT[:], a["out"]).then_inc(sem("x3_in"), 16)
            sp.wait_ge(sem("y_out"), KD)
            sp.dma_start(a["out"], xT[:]).then_inc(out_sent, 16)
            sp.wait_ge(out_sent, 16)

        @block.tensor
        def _(pe):
            mm = nc.tensor.matmul

            def begin(name, i=0):
                if use(name, i):
                    pe.wait_ge(bank_read[bank(name, i)], use(name, i))

            def end(ins):
                ins.then_inc(pe_done, 1)

            def panel(stage, i=0, width=256):
                n = panel_first[stage] + i
                pe.wait_ge(panel_low, n + 1)
                return [W[:, n % SPLIT, j, :].rearrange("p (k c) -> p k c", c=width) for j in range(2)]

            def product(out, lhs, rhs, first, final):
                mm(out, lhs[0], rhs[0], start=first, stop=False)
                mm(out, lhs[0], rhs[1], start=False, stop=False)
                return mm(out, lhs[1], rhs[0], start=False, stop=final)

            def project(stage, src, jobs, ready=None, kt=KD, per=2, i0=0):
                for i in range(i0, i0 + jobs):
                    w = panel(stage, i // per, PANEL // kt)
                    begin(stage, i)
                    for k in range(kt):
                        if ready and i == 0:
                            pe.wait_ge(*ready(k))
                        ins = product(pst(stage, i), [x[:, k, (i % per) * P:(i % per + 1) * P] for x in w], src(k), k == 0, k == kt - 1)
                    end(ins)

            def tokens(x, t):
                return [part[:, t * P:(t + 1) * P] for part in x]

            def column_sums(name, i, squares, waits=(), sel="ones"):
                begin(name, i)
                for k, sq in enumerate(squares):
                    if k < len(waits):
                        pe.wait_ge(*waits[k])
                    ins = mm(pst(name, i), sel[k] if isinstance(sel, list) else const(sel), sq,
                             start=(k == 0), stop=(k == len(squares) - 1))
                end(ins)

            def inverse(name, t, levels):
                am, xtr, xx, mk, p1 = BASES[name]
                for hf in range(2):
                    pe.wait_ge(sem(f"{name}_xt0"), 2 * t + hf + 1)
                    begin((name, "x0", t, hf))
                    for h in range(HALF):
                        ins = nc.tensor.transpose(heads4((name, "x0", t, hf))[:, h, :], pair(xtr, hf)[:, h, :], const("ident"))
                    end(ins)
                for lv in range(1, levels):
                    for hf in range(2):
                        k = (t * (levels - 1) + lv - 1) * 2 + hf
                        pe.wait_ge(sem(f"{name}_masked"), k + 1)
                        if lv == 1:
                            emptied(pe, (name, "x0", t, hf))
                        else:
                            emptied(pe, (name, "xt", t, lv - 1, hf))
                            emptied(pe, (name, "x", t, lv - 1, hf))
                        begin((name, "p1", t, lv, hf))
                        for h in range(HALF):
                            ins = mm(heads4((name, "p1", t, lv, hf))[:, h, :], pair(mk, hf)[:, h, :], pair(xx, hf)[:, h, :],
                                     start=True, stop=True)
                        end(ins)
                    for hf in range(2):
                        emptied(pe, (name, "p1", t, lv, hf))
                        begin((name, "xt", t, lv, hf))
                        for h in range(HALF):
                            ins = mm(heads4((name, "xt", t, lv, hf))[:, h, :], pair(p1, hf)[:, h, :], pair(xtr, hf)[:, h, :],
                                     start=True, stop=True)
                        end(ins)
                        if lv < levels - 1:
                            begin((name, "x", t, lv, hf))
                            for h in range(HALF):
                                ins = mm(heads4((name, "x", t, lv, hf))[:, h, :], pair(xtr, hf)[:, h, :], pair(p1, hf)[:, h, :],
                                         start=True, stop=True)
                            end(ins)

            def attention(name, units, score, value, smt, ptt):
                n = len(units)
                for u in range(n + 3):
                    if u < n:
                        h, qt = units[u]
                        begin((name, "scores", u))
                        end(score(pst((name, "scores", u))[:, 0:(qt + 1) * P], h, qt))
                    if 2 <= u < n + 2:
                        h, qt = units[u - 2]
                        pe.wait_ge(sem(f"{name}_probs"), u - 1)
                        begin((name, "turn", u - 2))
                        for kt in range(qt + 1):
                            ins = nc.tensor.transpose(pst((name, "turn", u - 2))[:, kt * P:(kt + 1) * P],
                                                      tile(smt[(u - 2) % 4])[:, kt * P:(kt + 1) * P], const("ident"))
                        end(ins)
                    if u >= 3:
                        h, qt = units[u - 3]
                        emptied(pe, (name, "turn", u - 3))
                        begin((name, "values", u - 3))
                        for kt in range(qt + 1):
                            out, lhs = value(pst((name, "values", u - 3)), h, kt)
                            ins = mm(out, lhs, tile(ptt[(u - 3) % 2])[:, kt * P:(kt + 1) * P], start=(kt == 0), stop=(kt == qt))
                        end(ins)

            def feed_forward(sfx, norm):
                project("up" + sfx, h_ff, 44, lambda k: norm_step("low", norm, k))
                for p in range(4):
                    jobs = (2 * p, 2 * p + 1)
                    for s in range(3):
                        w = panel("down" + sfx, 3 * p + s)
                        nk = min(8, NF - 8 * s)
                        if p == 0:
                            pe.wait_ge(sem("gated_low" + sfx), min(8 * s + 8, NF))
                        for m, i in enumerate(jobs):
                            if s == 0:
                                begin("down" + sfx, i)
                            for k in range(nk):
                                kk = 8 * s + k
                                g = (tileR(G_HIGH + kk), tileR(G_LOW + kk)) if kk < NG else (hH[:, kk - NG, :], tileR(G_REST + kk - NG))
                                ins = product(pst("down" + sfx, i), [x[:, k, m * P:(m + 1) * P] for x in w], g, kk == 0, kk == NF - 1)
                            end(ins)

            def block_1():
                def ada(i):
                    pe.wait_ge(sem("ada_used"), i + 1)
                    begin("ada", i)
                    for m in range(4):
                        ins = mm(pst("ada", i)[:, m:m + 1], tile(32 + i % 2)[:, m * P:(m + 1) * P], const("ones")[:, 0:1], start=True, stop=True)
                    end(ins)

                pe.wait_ge(consts_in, 16)
                for i in range(4):
                    ada(i)
                column_sums("rms1", 0, [tile(i) for i in range(KD)], [norm_step("squares", "rms1", i) for i in range(KD)])
                for m in range(12):
                    project("qkv", h_mix, 2, lambda k: norm_step("low", "rms1", k), i0=2 * m)
                    if 2 <= m < 10:
                        ada(2 + m)
                pe.wait_ge(sem("narrow"), 1)
                begin("ab")
                for t in range(NT):
                    for k in range(KD):
                        ins = product(pst("ab")[:, t * 16:(t + 1) * 16], tokens(h_mix(k), t), [narrow[:, j, k * 16:(k + 1) * 16] for j in range(2)],
                                      k == 0, k == KD - 1)
                end(ins)
                for i in range(16):
                    column_sums("l2", i, [tile(24 + i % 4)], [(sem("l2_sq"), i + 1)])
                pe.wait_ge(sem("g_ready"), 1)
                begin("gc")
                for t in range(NT):
                    mm(pst("gc")[:, t * 16:t * 16 + 8], const("utri"), tok(G, t), start=True, stop=True)
                    ins = mm(pst("gc")[:, t * 16 + 8:t * 16 + 16], const("ones"), tok(G, t), start=True, stop=True)
                end(ins)
                for t in range(NT):
                    c = slice(t * P, (t + 1) * P)
                    for hf in range(2):
                        hs = range(hf * HALF, (hf + 1) * HALF)
                        begin(("gb", t, hf))
                        for h in hs:
                            ins = mm(heads4(("gb", t, hf))[:, h % HALF, :], tok(G, t, h, 1).to_broadcast([P, P]), const("utri"),
                                     start=True, stop=True)
                        end(ins)
                        pe.wait_ge(sem("beta_ready"), 1)
                        begin(("bb", t, hf))
                        for h in hs:
                            ins = mm(heads4(("bb", t, hf))[:, h % HALF, :], tok(BETA, t, h, 1).to_broadcast([P, P]), const("ident"),
                                     start=True, stop=True)
                        end(ins)
                        pe.wait_ge(sem("qk_normed"), 16)
                        for what, other in (("kk", K0), ("kq", Q0)):
                            begin((what, t, hf))
                            for h in hs:
                                ins = mm(heads4((what, t, hf))[:, h % HALF, :], tile(K0 + h)[:, c], tile(other + h)[:, c],
                                         start=True, stop=True)
                            end(ins)
                        if t == 0:
                            pe.wait_ge(sem("conv_silu"), 24)
                        for what, src in (("kt", K0), ("vt", V0)):
                            begin((what, t, hf))
                            for h in hs:
                                ins = nc.tensor.transpose(heads4((what, t, hf))[:, h % HALF, :], tile(src + h)[:, c], const("ident"))
                            end(ins)
                    inverse("gdn", t, 7)
                    for hf in range(2):
                        begin(("ks", t, hf))
                        if t:
                            pe.wait_ge(sem("gdn_state"), 2 * t + hf + 1)
                        else:
                            pe.wait_ge(sem("gdn_state"), hf + 1)
                        for h in range(hf * HALF, (hf + 1) * HALF):
                            ins = mm(heads4(("ks", t, hf))[:, h % HALF, :], tile(K0 + h)[:, c], heads(ST, h), start=True, stop=True)
                        end(ins)
                    for hf in range(2):
                        pe.wait_ge(sem("gdn_rhs"), 2 * t + hf + 1)
                        emptied(pe, ("gdn", "xt", t, 6, hf))
                        begin(("vn", t, hf))
                        for h in range(HALF):
                            ins = mm(heads4(("vn", t, hf))[:, h, :], pair(XTR, hf)[:, h, :], pair(RHS, hf)[:, h, :],
                                     start=True, stop=True)
                        end(ins)
                    for hf in range(2):
                        emptied(pe, ("vn", t, hf))
                        pe.wait_ge(sem("gdn_qe"), 2 * t + hf + 1)
                        pe.wait_ge(sem("gdn_att"), 2 * t + hf + 1)
                        begin(("ot", t, hf))
                        for h in range(hf * HALF, (hf + 1) * HALF):
                            o = heads4(("ot", t, hf))[:, h % HALF, :]
                            mm(o, heads(ST, h), heads(QE, h), start=True, stop=False)
                            ins = mm(o, heads(VN, h), heads(ATT, h), start=False, stop=True)
                        end(ins)
                    for hf in range(2):
                        begin(("su", t, hf))
                        for h in range(hf * HALF, (hf + 1) * HALF):
                            ins = mm(heads4(("su", t, hf))[:, h % HALF, :], heads(KD_ROW, h), heads(VN, h), start=True, stop=True)
                        end(ins)
                for h in range(H):
                    column_sums("onorm", h, [tile(24 + h % 4)], [(sem("onorm_sq"), h + 1)])
                project("z", h_mix, 8)
                project("mq", h_mix, 12)
                project("mkv", h_mix, 3)
                column_sums("kvn", 0, [tile(12), tile(13)], [(sem("kv_sq"), i + 1) for i in range(2)])
                w = panel("ukv", 0, D)
                latent = parts_in(CKV_HIGH, [CKV, CKV + 1])
                pe.wait_ge(*part_ready("low", "ckv", 1))
                for h in range(H):
                    begin("uk", h)
                    for k in range(2):
                        ins = product(pst("uk", h), [x[:, k, h * P:(h + 1) * P] for x in w], latent(k), k == 0, k == 1)
                    end(ins)
                w = panel("ukv", 1, D)
                for i in range(8):
                    t, half = i // 2, i % 2
                    begin("mv", i)
                    for k in range(2):
                        ins = product(pst("mv", i), tokens(latent(k), t), [x[:, k, half * S:(half + 1) * S] for x in w], k == 0, k == 1)
                    end(ins)
                for h in range(H):
                    column_sums("kss", h, [tile(12), tile(13 + h % 2)], [(sem("kr_sq"), 1), (sem("kn_sq"), h + 1)],
                                sel=[const("top64"), const("ones")])
                pe.wait_ge(sem("kr_w"), 1)
                begin("krot")
                end(mm(pst("krot"), const("rot"), tile(KROPE), start=True, stop=True))
                for h in range(H):
                    column_sums("qss", h, [tile(8 + (h // 2) % 2), tile(13 + h % 2)],
                                [(sem("qr_sq"), h // 2 + 1), (sem("qn_sq"), h + 1)],
                                sel=[const("low64" if h % 2 else "top64"), const("ones")])
                for p in range(4):
                    pe.wait_ge(sem("qr_w"), p + 1)
                    begin("qrot", p)
                    end(mm(pst("qrot", p), const("rot"), tile(QR + p), start=True, stop=True))

                pe.wait_ge(sem("mla_qk"), 1)
                emptied(pe, "mv", 7)

                def score(out, h, qt):
                    b = slice(64 * (h % 2), 64 * (h % 2) + 64)
                    mm(out, tile(QN + h)[:, qt * P:(qt + 1) * P], tile(KN + h)[:, 0:(qt + 1) * P], start=True, stop=False)
                    return mm(out, tile(QR + h // 2)[b, qt * P:(qt + 1) * P], tile(KR + h // 2)[b, 0:(qt + 1) * P],
                              start=False, stop=True)

                def value(out, h, kt):
                    return out[:, 0:P], ar[:, MV + 2 * kt + h // 4, (h % 4) * P:(h % 4 + 1) * P]

                attention("mla", UNITS, score, value, (12, 13, 14, 11), (15, 48))
                for fb in range(2):
                    project(f"gate_dn{fb}", h_mix, 4)
                    project(f"y_dn{fb}", parts_in(O_DN_HIGH, range(V0, V0 + 8)), 4, lambda k: part_ready("low", "o_dn", k))
                    project(f"gate_mla{fb}", h_mix, 4)
                    project(f"y_mla{fb}", parts_in(O_MLA_HIGH, range(QN, QN + 8)), 4, lambda k: part_ready("low", "o_mla", k))
                project("wo", parts_in(MIX_HIGH, range(MIX, MIX + 8)), 8, lambda k: part_ready("low", "mix", k))
                column_sums("rms2", 0, [tile(24 + i) for i in range(KD)], [norm_step("squares", "rms2", i) for i in range(KD)])
                feed_forward("", "rms2")

            def head64(x, h):
                return x[64 * (h % 2):64 * (h % 2) + 64]

            def block_2():
                pe.wait_ge(consts_in, 16)
                column_sums("rms3", 0, [tile(42 + i) for i in range(KD)], [norm_step("squares", "rms3", i) for i in range(KD)])
                project("rkv", h_mix, 12, lambda k: norm_step("low", "rms3", k))
                project("wag", h_mix, 2)
                pe.wait_ge(small2_in, 32)
                pe.wait_ge(sem("lora_act"), 2)
                for p in range(4):
                    begin("wup", p)
                    end(mm(pst("wup", p), lora[0:64, 0, p * P:(p + 1) * P], tile(WA)[0:64, :], start=True, stop=True))
                for p in range(4):
                    begin("aup", p)
                    end(mm(pst("aup", p), lora[64:P, 0, p * P:(p + 1) * P], tile(WA)[64:P, :], start=True, stop=True))
                for p in range(4):
                    begin("gup", p)
                    end(mm(pst("gup", p), lora[:, 1, p * P:(p + 1) * P], tile(GD), start=True, stop=True))
                for p in range(4):
                    column_sums("kkn", p, [tile(40 + p)], [(sem("kk_sq"), p + 1)], sel="same64")
                for p in range(4):
                    column_sums("bon", p, [tile(44 + p)], [(sem("bonus_in"), p + 1)], sel="same64")
                pe.wait_ge(sem("rw_ready"), 4)
                for t in range(NT):
                    c = slice(t * P, (t + 1) * P)
                    for what, src in (("vrow", V2), ("brow", BT), ("krow", KT)):
                        begin((what, t))
                        for p in range(4):
                            ins = nc.tensor.transpose(heads4((what, t))[:, p, :], tile(src + p)[:, c], const("ident"))
                        end(ins)
                    for par in range(2):
                        b = slice(64 * par, 64 * par + 64)
                        for what, lhs, rhs in (("rm", BT, KAP), ("rn", KT, KAP), ("rb", BT, RHO), ("rk", KT, RHO)):
                            begin((what, t, par))
                            for p in range(4):
                                ins = mm(heads4((what, t, par))[:, p, :], tile(lhs + p)[b, c], tile(rhs + p)[b, c], start=True, stop=True)
                            end(ins)
                    pe.wait_ge(sem("rw_n"), 2 * t + 2)
                    emptied(pe, ("vrow", t))
                    begin(("nv", t))
                    for h in range(H):
                        ins = mm(pst(("nv", t))[:, h * 64:(h + 1) * 64], pair(NTR, h % 2)[:, h // 2, :], tile(VROW)[:, h * 64:(h + 1) * 64],
                                 start=True, stop=True)
                    end(ins)
                    inverse("rw", t, 6)
                    for e in range(2):
                        eb, n = slice(64 * e, 64 * e + 64), 2 * t + e
                        ec = slice(t * P + 64 * e, t * P + 64 * e + 64)
                        pe.wait_ge(sem("rw_state"), n + 1)
                        for par in range(2):
                            b = slice(64 * par, 64 * par + 64)
                            begin(("rs", t, e, par))
                            for p in range(4):
                                ins = mm(pst(("rs", t, e, par))[eb, p * 64:(p + 1) * 64], tile(KAP + p)[b, ec],
                                         tile(ST2)[b, p * 64:(p + 1) * 64], start=True, stop=True)
                            end(ins)
                        if e == 0:
                            for par in range(2):
                                emptied(pe, ("rw", "xt", t, 5, par))
                        pe.wait_ge(sem("rw_rhs"), n + 1)
                        begin(("ru", t, e))
                        for h in range(H):
                            ins = mm(pst(("ru", t, e))[eb, h * 64:(h + 1) * 64], pair(38, h % 2)[eb, h // 2, eb],
                                     tile(RSB)[eb, h * 64:(h + 1) * 64], start=True, stop=True)
                        end(ins)
                        for par in range(2):
                            b = slice(64 * par, 64 * par + 64)
                            begin(("ry", t, e, par))
                            for p in range(4):
                                ins = mm(pst(("ry", t, e, par))[b, p * 64:(p + 1) * 64], tile(ST2)[b, p * 64:(p + 1) * 64],
                                         tile(RHO + p)[b, ec], start=True, stop=True)
                            end(ins)
                        emptied(pe, ("ru", t, e))
                        emptied(pe, ("brow", t))
                        emptied(pe, ("krow", t))
                        begin(("rz", t, e))
                        for h in range(H):
                            o = head64(pst(("rz", t, e)), h)[:, (h // 2) * 64:(h // 2) * 64 + 64]
                            mm(o, tile(BROW)[eb, h * 64:(h + 1) * 64], tile(UU)[eb, h * 64:(h + 1) * 64], start=True, stop=False)
                            ins = mm(o, tile(KROW)[eb, h * 64:(h + 1) * 64], tile(VROW)[eb, h * 64:(h + 1) * 64], start=False, stop=True)
                        end(ins)
                    pe.wait_ge(sem("rw_b"), 4 * t + 4)
                    begin(("yi", t))
                    for h in range(H):
                        o = head64(pst(("yi", t)), h)[:, (h // 2) * P:(h // 2 + 1) * P]
                        mm(o, tile(VROW)[:, h * 64:(h + 1) * 64], pair(KRT, h % 2)[:, h // 2, :], start=True, stop=False)
                        ins = mm(o, tile(UU)[:, h * 64:(h + 1) * 64], pair(BRT, h % 2)[:, h // 2, :], start=False, stop=True)
                    end(ins)
                for p in range(4):
                    column_sums("gmean", p, [tile(RHO + p)], [(sem("y_sum"), 4 * NT)], sel="same64")
                for p in range(4):
                    column_sums("gvar", p, [tile(36 + p)], [(sem("gn_sq"), p + 1)], sel="same64")
                project("ai", h_mix, 5)
                pe.wait_ge(sem("narrow"), 2)
                begin("wi")
                for t in range(NT):
                    for k in range(KD):
                        ins = product(pst("wi")[:, t * 8:t * 8 + 8], tokens(h_mix(k), t), [narrow[:, j, k * 8:(k + 1) * 8] for j in range(2)],
                                      k == 0, k == KD - 1)
                end(ins)
                for i in range(5):
                    emptied(pe, "ai", i)
                    begin("irot", i)
                    end(mm(pst("irot", i), const("rot"), tile(QI + i), start=True, stop=True))
                pe.wait_ge(sem("index_qk"), 1)
                for i in range(24):
                    qt, h = i // 8 + 1, i % 8
                    begin("index", i)
                    end(mm(pst("index", i)[:, 0:(qt + 1) * P], head64(tile(QI + h // 2), h)[:, qt * P:(qt + 1) * P],
                           head64(tile(KI), h)[:, 0:(qt + 1) * P], start=True, stop=True))
                project("aq", h_mix, 8)
                for s in range(2):
                    w = panel("av", s)
                    for t in range(NT):
                        if s == 0:
                            begin("av", t)
                        for k in range(KD):
                            ins = product(pst("av", t)[:, 256 * s:256 * s + 256], tokens(h_mix(k), t), [x[:, k, :] for x in w], k == 0, k == KD - 1)
                        end(ins)
                for i in range(8):
                    emptied(pe, "aq", i)
                    begin("arot", i)
                    end(mm(pst("arot", i), const("rot"), tile(AQ + i), start=True, stop=True))
                project("gate_a", h_mix, 8)
                project("yr", parts_in(Y_HIGH, range(RHO, RHO + 4)), 8, lambda k: part_ready("low", "y_rw", k), kt=4, per=4)
                pe.wait_ge(sem("dsa_qk"), 1)
                emptied(pe, "av", 3)

                def score(out, h, qt):
                    return mm(out, head64(tile(AQ + h // 2), h)[:, qt * P:(qt + 1) * P], head64(tile(AK + h // 2), h)[:, 0:(qt + 1) * P],
                              start=True, stop=True)

                def value(out, h, kt):
                    return head64(out, h)[:, 0:P], tile(AV + kt)[:, h * 64:(h + 1) * 64]

                attention("dsa", UNITS, score, value, (30, 31, 32, 29), (33, 34))
                project("gate_b", h_mix, 8)
                project("ya", parts_in(Y_HIGH, range(OA, OA + 4)), 8, lambda k: part_ready("low", "o_dsa", k), kt=4, per=4)
                project("wout", parts_in(MERGE_HIGH, range(MERGE, MERGE + 8)), 8, lambda k: part_ready("low", "merged", k))
                column_sums("rms4", 0, [tile(i) for i in range(KD)], [norm_step("squares", "rms4", i) for i in range(KD)])
                feed_forward("_2", "rms4")
                column_sums("rms5", 0, [tile(42 + i) for i in range(KD)], [norm_step("squares", "rms5", i) for i in range(KD)])

            block_1()
            block_2()

        @block.scalar
        def _(act):
            link = linker(act, sem("act_chain"))
            af = nc.scalar.activation
            highs = [0]

            def split(value):
                while highs[0] < len(panel_release):
                    n = highs[0]
                    if n >= SPLIT:
                        if panel_release[n - SPLIT] > value:
                            break
                        act.wait_ge(pe_done, panel_release[n - SPLIT])
                    highs[0] += 1
                    act.wait_ge(panel_in[n % RAW], 16 * (n // RAW + 1))
                    link(nc.scalar.copy(W[:, n % SPLIT, 0, :], raw[:, n % RAW, :]), panel_high, n + 1)

            def high(dst, src, done, value):
                link(nc.scalar.copy(dst, src), done, value)

            def high_input(name, shift=None):
                for i in range(KD):
                    act.wait_ge(*norm_step("scaled", name, i))
                    if shift is None:
                        high(hH[:, i, :], tile(T_OF[name] + i % 4), *norm_step("high", name, i))
                    else:
                        link(af(hH[:, i, :], tile(T_OF[name] + i % 4), ACT.Identity, bias=shift(i)), *norm_step("high", name, i))

            def high_gated(sfx, i):
                ahead(act, "up" + sfx, 4 * (i // 2) + 2 + i % 2)
                act.wait_ge(sem("gated" + sfx), i + 1)
                if i < NG:
                    high(tileR(G_HIGH + i), tile(i % 4), sem("gated_high" + sfx), i + 1)

            def high_rest(sfx):
                for i in range(NG, NF):
                    if i == NG:
                        filled(act, "up" + sfx, 43)
                    act.wait_ge(sem("gated" + sfx), i + 1)
                    high(hH[:, i - NG, :], tile(G_REST + i - NG), sem("gated_high" + sfx), i + 1)

            def squares(name, base, k=KD):
                for i in range(k):
                    link(af(tile(base + i), xT[:, i, :], ACT.Square), *norm_step("squares", name, i))

            def rstd(job, i, tmp, out, scale, done, value, bias="eps", power_bias=0.0):
                filled(act, job, i)
                link(af(tmp, pst(job, i), ACT.Ln, bias=col(bias), scale=scale), *read(job, i))
                link(af(out, tmp, ACT.Exp, bias=power_bias, scale=-0.5), done, value)

            def inverse(name, t, levels):
                am, xtr, xx, mk, p1 = BASES[name]
                for hf in range(2):
                    filled(act, (name, "x0", t, hf))
                    link(nc.scalar.copy(pair(xx, hf), heads4((name, "x0", t, hf))), *read((name, "x0", t, hf)))
                for lv in range(1, levels):
                    for hf in range(2):
                        filled(act, (name, "p1", t, lv, hf))
                        link(nc.scalar.copy(pair(p1, hf), heads4((name, "p1", t, lv, hf))), *read((name, "p1", t, lv, hf)))

            def attention(name, units, scale, smt, ptt, out):
                n = len(units)
                for u in range(n + 3):
                    if u < n:
                        h, qt = units[u]
                        w = (qt + 1) * P
                        act.wait_ge(sem(f"{name}_peak"), u + 1)
                        link(af(tile(smt[u % 4])[:, 0:w], tile(smt[u % 4])[:, 0:w], ACT.Exp, bias=st[:, u % 4:u % 4 + 1],
                                scale=scale, accum_out=st[:, 4 + u % 4:5 + u % 4]), sem(f"{name}_exp"), u + 1)
                    if 2 <= u < n + 2:
                        h, qt = units[u - 2]
                        w = (qt + 1) * P
                        filled(act, (name, "turn", u - 2))
                        if u >= 4:
                            filled(act, (name, "values", u - 4))
                        link(nc.scalar.copy(tile(ptt[(u - 2) % 2])[:, 0:w], pst((name, "turn", u - 2))[:, 0:w]), *read((name, "turn", u - 2)))
                    if u >= 3:
                        h, qt = units[u - 3]
                        filled(act, (name, "values", u - 3))
                        dst, src = out(h, qt, pst((name, "values", u - 3)))
                        link(nc.scalar.copy(dst, src), *read((name, "values", u - 3)))

            def gelu(sfx):
                for p in range(11):
                    for i in (2 * p, 2 * p + 1):
                        ahead(act, "up" + sfx, 4 * p + i % 2)
                        act.wait_ge(sem("fconv" + sfx), i + 1)
                        link(af(tile(i % 4), tile(i % 4), ACT.Gelu), sem("gelu" + sfx), i + 1)
                    for i in (2 * p, 2 * p + 1):
                        high_gated(sfx, i)
                high_rest(sfx)

            def block_1():
                act.wait_ge(cols_in, 32)
                link(af(st[:, 0:8], cT[:], ACT.Silu), sem("silu_c"), 1)
                act.wait_ge(x_in, 16)
                squares("rms1", 0)
                rstd("rms1", 0, tile(24), tile(24), 1.0 / D, *norm_step("rstd", "rms1"))
                split_before[act] = split
                split(0)
                high_input("rms1", lambda i: modT[:, i:i + 1])
                act.wait_ge(ab_in, 16)
                high(narrow[:, 0, :], wab[:].rearrange("p k c -> p (k c)"), sem("narrow_high"), 1)
                for i in range(24):
                    ahead(act, "qkv", i)
                    act.wait_ge(sem("conv"), i + 1)
                    link(af(tile(Q0 + i), tile(Q0 + i), ACT.Silu), sem("conv_silu"), i + 1)
                ahead(act, "ab")
                act.wait_ge(sem("ab_dve"), 1)
                link(af(sm4[:, AB_E, :, 0:8], sm4[:, AB_A, :, 0:8], ACT.Exp, scale=-1.0))
                link(af(sm4[:, AB_R, 0, 8:16], col("a_log", 0, 8), ACT.Exp))
                link(af(sm4[:, AB_B, :, 0:8], sm4[:, AB_B, :, 0:8], ACT.Exp, scale=-1.0))
                link(af(sm4[:, AB_E, :, 8:16], sm4[:, AB_E, :, 0:8], ACT.Ln, bias=col("one")), sem("ab_act"), 1)
                for i in range(16):
                    if i >= 2:
                        act.wait_ge(sem("qk_normed"), i - 1)
                    rstd("l2", i, tile(28 + i % 2), tile(30 + i % 2), 1.0, sem("l2_rstd"), i + 1,
                         power_bias=(col("qscale") if i < 8 else 0.0))
                act.wait_ge(sem("gc_dve"), 1)
                link(af(sm4[:, EGC, :, :], sm4[:, GC, :, :], ACT.Exp))
                link(af(sm4[:, KDEC, :, 0:8], sm4[:, KDEC, :, 0:8], ACT.Exp), sem("gc_act"), 1)
                for t in range(NT):
                    for hf in range(2):
                        n = 2 * t + hf + 1
                        act.wait_ge(sem("gb_minus"), n)
                        link(af(pair(EGB, hf), heads4(("gb", t, hf)), ACT.Exp), *read(("gb", t, hf)))
                        act.wait_ge(sem("gb_masked"), n)
                        link(af(pair(DT, hf), pair(DT, hf), ACT.Exp), sem("gdn_decay"), n)
                    inverse("gdn", t, 7)
                    for hf in range(2):
                        filled(act, ("vn", t, hf))
                        link(nc.scalar.copy(pair(VN, hf), heads4(("vn", t, hf))), *read(("vn", t, hf)))
                    for hf in range(2):
                        filled(act, ("ot", t, hf))
                        link(nc.scalar.copy(ar[:, V0 + hf * HALF:V0 + (hf + 1) * HALF, t * P:(t + 1) * P],
                                            heads4(("ot", t, hf))), *read(("ot", t, hf)))
                for h in range(H):
                    if h >= 2:
                        act.wait_ge(sem("o_scaled"), h - 1)
                    rstd("onorm", h, tile(28 + h % 2), tile(30 + h % 2), 1.0 / P, sem("o_rstd"), h + 1)
                for h in range(H):
                    filled(act, "z", h)
                    link(af(tile(Q0 + h), pst("z", h), ACT.Silu), *read("z", h))
                for i in range(12):
                    filled(act, "mq", i)
                    if i == 0:
                        act.wait_ge(sem("o_scaled"), 8)
                    link(nc.scalar.copy(tile(QN + i), pst("mq", i)), *read("mq", i))
                for i in range(2):
                    act.wait_ge(sem("angle"), 2)
                    link(af(trig[:, i, :], tile(10 + i) if i == 0 else tile(9), ACT.Sin), sem("trig"), i + 1)
                for i in range(3):
                    filled(act, "mkv", i)
                    if i == 0:
                        act.wait_ge(sem("o_dn"), 8)
                    link(nc.scalar.copy(tile(CKV + i), pst("mkv", i)), *read("mkv", i))
                for i in range(2):
                    link(af(tile(12 + i), tile(CKV + i), ACT.Square), sem("kv_sq"), i + 1)
                rstd("kvn", 0, tile(14), tile(15), 1.0 / RANK, sem("kv_rstd"), 1)
                for k in range(2):
                    act.wait_ge(sem("ckv"), k + 1)
                    high(tileR(CKV_HIGH[k]), tile(CKV + k), *part_ready("high", "ckv", k))
                for h in range(H):
                    filled(act, "uk", h)
                    link(nc.scalar.copy(tile(KN + h), pst("uk", h)), *read("uk", h))
                for i in range(8):
                    filled(act, "mv", i)
                    link(nc.scalar.copy(tile(MV + i), pst("mv", i)), *read("mv", i))
                link(af(tile(12), tile(KROPE), ACT.Square), sem("kr_sq"), 1)
                for h in range(H):
                    if h >= 2:
                        filled(act, "kss", h - 2)
                    link(af(tile(13 + h % 2), tile(KN + h), ACT.Square), sem("kn_sq"), h + 1)
                    if h:
                        if h >= 3:
                            act.wait_ge(sem("k_scaled"), h - 2)
                        rstd("kss", h - 1, tile(15), tile(48 + (h - 1) % 2), 1.0 / 192, sem("k_rstd"), h)
                act.wait_ge(sem("k_scaled"), 6)
                rstd("kss", 7, tile(15), tile(49), 1.0 / 192, sem("k_rstd"), 8)
                for h in range(H):
                    p = h // 2
                    if h % 2 == 0:
                        if p >= 2:
                            filled(act, "qss", 2 * p - 3)
                        else:
                            act.wait_ge(sem("ckv_free"), 1)
                        link(af(tile(8 + p % 2), tile(QR + p), ACT.Square), sem("qr_sq"), p + 1)
                    if h >= 2:
                        filled(act, "qss", h - 2)
                    else:
                        filled(act, "kss", 6 + h)
                    link(af(tile(13 + h % 2), tile(QN + h), ACT.Square), sem("qn_sq"), h + 1)
                    if h:
                        act.wait_ge(sem("q_scaled" if h >= 3 else "k_scaled"), h - 2 if h >= 3 else 6 + h)
                        rstd("qss", h - 1, tile(15), tile(48 + (h - 1) % 2), 1.0 / 192, sem("q_rstd"), h)
                act.wait_ge(sem("q_scaled"), 6)
                rstd("qss", 7, tile(15), tile(49), 1.0 / 192, sem("q_rstd"), 8)
                attention("mla", UNITS, 192 ** -0.5, (12, 13, 14, 11), (15, 48),
                          lambda h, qt, src: (tile(QN + h)[:, qt * P:(qt + 1) * P], src[:, 0:P]))
                for h in range(H):
                    high(tileR(O_DN_HIGH[h]), tile(V0 + h), *part_ready("high", "o_dn", h))
                for h in range(H):
                    high(tileR(O_MLA_HIGH[h]), tile(QN + h), *part_ready("high", "o_mla", h))
                for fb in range(2):
                    for j, what in enumerate(("gate_dn", "gate_mla")):
                        for m in range(4):
                            k = 2 * fb + j
                            filled(act, f"{what}{fb}", m)
                            if k:
                                act.wait_ge(sem("gate_used"), 4 * (k - 1) + m + 1)
                            link(af(tile(8 + m), pst(f"{what}{fb}", m), ACT.Sigmoid), *read(f"{what}{fb}", m))
                for i in range(KD):
                    if i >= 4:
                        ahead(act, "y_mla1", i - 4)
                    act.wait_ge(sem("mix"), i + 1)
                    if i == 0:
                        filled(act, "y_dn1", 3)
                    high(tileR(MIX_HIGH[i]), tile(MIX + i), *part_ready("high", "mix", i))
                for i in range(KD):
                    ahead(act, "wo", i)
                    act.wait_ge(sem("x1"), i + 1)
                    link(af(tile(24 + i), xT[:, i, :], ACT.Square), *norm_step("squares", "rms2", i))
                rstd("rms2", 0, tile(8), tile(9), 1.0 / D, *norm_step("rstd", "rms2"))
                high_input("rms2", lambda i: modT[:, 24 + i:25 + i])
                gelu("")

            def block_2():
                for i in range(KD):
                    ahead(act, "down", i)
                    act.wait_ge(sem("x2"), i + 1)
                    link(af(tile(42 + i), xT[:, i, :], ACT.Square), *norm_step("squares", "rms3", i))
                rstd("rms3", 0, tile(38), tile(39), 1.0 / D, *norm_step("rstd", "rms3"))
                high_input("rms3")
                for i in range(14):
                    ahead(act, "rkv" if i < 12 else "wag", i % 12)
                    act.wait_ge(sem("shifted"), i + 1)
                link(af(tile(WA)[0:64, :], tile(WA)[0:64, :], ACT.Tanh), sem("lora_act"), 1)
                act.wait_ge(small2_in, 32)
                high(narrow[:, 0, 0:64], wix[:].rearrange("p k c -> p (k c)"), sem("narrow_high"), 2)
                link(af(tile(GD), tile(GD), ACT.Sigmoid), sem("lora_act"), 2)
                for what, base, bias in (("wup", LD, "w0"), ("aup", BT, "a0")):
                    for p in range(4):
                        filled(act, what, p)
                        link(af(tile(base + p), pst(what, p), ACT.Sigmoid, bias=col(bias, p)), *read(what, p))
                for p in range(4):
                    filled(act, "gup", p)
                    link(nc.scalar.copy(tile(G2 + p), pst("gup", p)), *read("gup", p))
                for p in range(4):
                    link(af(tile(40 + p), tile(KT + p), ACT.Square, scale=col("k_k", p)), sem("kk_sq"), p + 1)
                for p in range(4):
                    act.wait_ge(sem("kk_clamped"), p + 1)
                    link(af(tile(48), tile(36 + p % 2), ACT.Ln, scale=float(2 ** 20)))
                    if p >= 2:
                        act.wait_ge(sem("kk_used"), p - 1)
                    link(af(tile(38 + p % 2), tile(48), ACT.Exp, scale=-0.5, bias=col("ln1024")), sem("kk_rstd"), p + 1)
                for p in range(4):
                    act.wait_ge(sem("g_cum"), p + 1)
                    gc = tile(GCUM + p % 2)
                    link(af(tile(40), gc, ACT.Exp))
                    link(af(sm2[:, EC + 8 * p:EC + 8 * p + 8], gc[:, 63:S:64], ACT.Exp))
                    link(af(tile(42), gc, ACT.Exp, scale=-1.0))
                    link(af(tile(41), tile(36), ACT.Exp), sem("decays"), p + 1)
                    act.wait_ge(sem("rw_ready"), p + 1)
                for t in range(NT):
                    for what, dst in (("vrow", VROW), ("brow", BROW), ("krow", KROW)):
                        filled(act, (what, t))
                        link(nc.scalar.copy(tile(dst), pst((what, t))), *read((what, t)))
                    filled(act, ("nv", t))
                    link(nc.scalar.copy(tile(NVT), pst(("nv", t))), *read(("nv", t)))
                    inverse("rw", t, 6)
                    for e in range(2):
                        eb, n = slice(64 * e, 64 * e + 64), 2 * t + e
                        ec = slice(t * P + 64 * e, t * P + 64 * e + 64)
                        filled(act, ("ru", t, e))
                        link(nc.scalar.mul(tile(UU)[eb, :], pst(("ru", t, e))[eb, :], -1.0), *read(("ru", t, e)))
                        for par in range(2):
                            b = slice(64 * par, 64 * par + 64)
                            filled(act, ("ry", t, e, par))
                            link(nc.scalar.copy(ar[b, RHO:RHO + 4, ec], pst(("ry", t, e, par))[b, 0:256].rearrange("p (h c) -> p h c", c=64)),
                                 *read(("ry", t, e, par)))
                for p in range(4):
                    act.wait_ge(sem("gn_centred"), p + 1)
                    link(af(tile(36 + p), tile(RHO + p), ACT.Square), sem("gn_sq"), p + 1)
                for p in range(4):
                    if p >= 2:
                        act.wait_ge(sem("gn_used"), p - 1)
                    rstd("gvar", p, tile(40), tile(41 + p % 2), 1.0 / 64, sem("gn_rstd"), p + 1, bias="lnx")
                for p in range(4):
                    act.wait_ge(sem("y_rw"), p + 1)
                    if p == 0:
                        act.wait_ge(sem("y_rw"), 4)
                    high(tileR(Y_HIGH[p]), tile(RHO + p), *part_ready("high", "y_rw", p))
                for i in range(5):
                    filled(act, "ai", i)
                    link(nc.scalar.copy(tile(QI + i), pst("ai", i)), *read("ai", i))
                for i in range(24):
                    w = (i // 8 + 2) * P
                    if i >= 2:
                        act.wait_ge(sem("index_used"), i - 1)
                    filled(act, "index", i)
                    link(af(tile(REL[i % 2])[:, 0:w], pst("index", i)[:, 0:w], ACT.Relu), *read("index", i))
                for i in range(8):
                    filled(act, "aq", i)
                    link(nc.scalar.copy(tile(AQ + i), pst("aq", i)), *read("aq", i))
                for t in range(NT):
                    filled(act, "av", t)
                    link(nc.scalar.copy(tile(AV + t), pst("av", t)), *read("av", t))
                for m in range(8):
                    filled(act, "gate_a", m)
                    link(af(tile(MERGE + m), pst("gate_a", m), ACT.Sigmoid), *read("gate_a", m))
                attention("dsa", UNITS, 64 ** -0.5, (30, 31, 32, 29), (33, 34),
                          lambda h, qt, src: (tile(OA + h // 2)[64 * (h % 2):64 * (h % 2) + 64, qt * P:(qt + 1) * P],
                                              src[64 * (h % 2):64 * (h % 2) + 64, 0:P]))
                for p in range(4):
                    high(tileR(Y_HIGH[p]), tile(OA + p), *part_ready("high", "o_dsa", p))
                for m in range(8):
                    filled(act, "gate_b", m)
                    link(af(tile(AQ + m), pst("gate_b", m), ACT.Sigmoid), *read("gate_b", m))
                for m in range(8):
                    ahead(act, "ya", m)
                    act.wait_ge(sem("merged"), m + 1)
                    high(tileR(MERGE_HIGH[m]), tile(MERGE + m), *part_ready("high", "merged", m))
                for i in range(KD):
                    ahead(act, "wout", i)
                    act.wait_ge(sem("x3"), i + 1)
                    link(af(tile(i), xT[:, i, :], ACT.Square), *norm_step("squares", "rms4", i))
                rstd("rms4", 0, tile(8), tile(9), 1.0 / D, *norm_step("rstd", "rms4"))
                high_input("rms4")
                for p in range(11):
                    for j in range(2):
                        i, job = 2 * p + j, 4 * p + j
                        filled(act, "up_2", job)
                        if i >= 4:
                            act.wait_ge(sem("gated_low_2"), min(i - 3, NG))
                            act.wait_ge(sem("gated_2"), i - 3)
                        link(af(tile(i % 4), pst("up_2", job), ACT.Silu), *read("up_2", job))
                    for i in (2 * p, 2 * p + 1):
                        high_gated("_2", i)
                high_rest("_2")
                for i in range(KD):
                    ahead(act, "down_2", i)
                    act.wait_ge(sem("x4"), i + 1)
                    link(af(tile(42 + i), xT[:, i, :], ACT.Square), *norm_step("squares", "rms5", i))
                rstd("rms5", 0, tile(8), tile(9), 1.0 / D, *norm_step("rstd", "rms5"))

            block_1()
            block_2()

        @block.vector
        def _(dve):
            link = linker(dve, sem("dve_chain"))
            v = nc.vector
            tt, ts, stt = v.tensor_tensor, v.tensor_scalar, v.scalar_tensor_tensor

            def low(dst, src, high_part):
                return tt(dst, src, high_part.bitcast(F32), ALU.subtract)

            def lows(name, high_tiles, base):
                for k, t in enumerate(high_tiles):
                    dve.wait_ge(*part_ready("high", name, k))
                    link(low(tileR(base + k), tile(base + k), tileR(t)), *part_ready("low", name, k))

            def normed(name, rs, scale, shift, dst, kept=None):
                dve.wait_ge(*norm_step("rstd", name))
                for i in range(KD + 2):
                    if i < KD:
                        link(stt(tile(T_OF[name] + i % 4), xT[:, i, :], scale(i), rs, ALU.mult, ALU.mult), *norm_step("scaled", name, i))
                    if i >= 2:
                        j = i - 2
                        dve.wait_ge(*norm_step("high", name, j))
                        if kept and j == 0:
                            dve.wait_ge(*kept)
                        t, h = tile(T_OF[name] + j % 4), hH[:, j, :]
                        if shift is None:
                            link(low(dst(j), t, h), *norm_step("low", name, j))
                        else:
                            link(stt(dst(j), t, shift(j), h.bitcast(F32), ALU.add, ALU.subtract), *norm_step("low", name, j))

            def causal_conv(job, i, out, taps, done, value, bias=None):
                src = pst(job, i)
                n = len(taps)
                link(ts(out, src, taps[-1], bias, ALU.mult, ALU.add if bias is not None else ALU.bypass))
                for j in range(1, n):
                    ins = stt(out[:, j:S], src[:, 0:S - j], taps[n - 1 - j], out[:, j:S], ALU.mult, ALU.add)
                    if j < n - 1:
                        link(ins)
                    else:
                        link(ins, *read(job, i))

            def inverse(name, t, levels):
                am, xtr, xx, mk, p1 = BASES[name]
                for hf in range(2):
                    dve.wait_ge(sem(f"{name}_masked0"), 2 * t + hf + 1)
                    link(tt(pair(xtr, hf), bm(const("ident")), pair(mk, hf), ALU.subtract), sem(f"{name}_xt0"), 2 * t + hf + 1)
                for lv in range(1, levels):
                    for hf in range(2):
                        if lv < levels - 1:
                            filled(dve, (name, "x", t, lv, hf))
                        filled(dve, (name, "xt", t, lv, hf))
                        link(tt(pair(xtr, hf), pair(xtr, hf), heads4((name, "xt", t, lv, hf)), ALU.subtract), *read((name, "xt", t, lv, hf)))
                        if lv < levels - 1:
                            link(tt(pair(xx, hf), pair(xx, hf), heads4((name, "x", t, lv, hf)), ALU.subtract), *read((name, "x", t, lv, hf)))

            def attention(name, units, scale, smt, bias, before=None):
                n = len(units)
                for u in range(n + 1):
                    if u < n:
                        h, qt = units[u]
                        w = (qt + 1) * P
                        if before:
                            before(u)
                        filled(dve, (name, "scores", u))
                        if u >= 4:
                            filled(dve, (name, "turn", u - 4))
                        link(v.tensor_tensor_reduce(out=tile(smt[u % 4])[:, 0:w], in0=pst((name, "scores", u))[:, 0:w], in1=bias(qt),
                                                    scale=1.0, scalar=LOW, op0=ALU.add, op1=ALU.max,
                                                    accum_out=st[:, 8 + u % 4:9 + u % 4]), *read((name, "scores", u)))
                        link(ts(st[:, u % 4:u % 4 + 1], st[:, 8 + u % 4:9 + u % 4], -scale, None, ALU.mult), sem(f"{name}_peak"), u + 1)
                    if u >= 1:
                        h, qt = units[u - 1]
                        w = (qt + 1) * P
                        dve.wait_ge(sem(f"{name}_exp"), u)
                        r = st[:, 12 + (u - 1) % 4:13 + (u - 1) % 4]
                        link(v.reciprocal(r, st[:, 4 + (u - 1) % 4:5 + (u - 1) % 4]))
                        link(ts(tile(smt[(u - 1) % 4])[:, 0:w], tile(smt[(u - 1) % 4])[:, 0:w], r, None, ALU.mult), sem(f"{name}_probs"), u)

            def gated_up(sfx, conv):
                for p in range(11):
                    for j in range(2):
                        i, job = 2 * p + j, 4 * p + j
                        filled(dve, "up" + sfx, job)
                        if i >= 4:
                            dve.wait_ge(sem("gated_low" + sfx), min(i - 3, NG))
                        conv(job, i, tile(i % 4))
                    for j in range(2):
                        i, job = 2 * p + j, 4 * p + 2 + j
                        filled(dve, "up" + sfx, job)
                        dve.wait_ge(sem("gelu" + sfx), i + 1)
                        link(tt(tile(i % 4) if i < NG else tile(G_REST + i - NG), tile(i % 4), pst("up" + sfx, job), ALU.mult), *read("up" + sfx, job))
                        tell(sem("gated" + sfx), i + 1)

            def tell(s, value):
                link(v.memset(st[:, 63:64], 0.0), s, value)

            def rope(dst, src, job, i, tmp):
                filled(dve, job, i)
                link(tt(tmp, pst(job, i), trig[:, 1, :], ALU.mult), *read(job, i))
                link(tt(dst, src, trig[:, 0, :], ALU.mult))
                link(tt(dst, dst, tmp, ALU.add))

            def block_1():
                dve.wait_ge(cols_in, 32)
                dve.wait_ge(sem("silu_c"), 1)

                def ada_products(i):
                    b = i if i < 4 else 2 + i % 2
                    dve.wait_ge(ada_in[b], 16 if i < 4 else 16 * (i // 2))
                    if i >= 2:
                        filled(dve, "ada", i - 2)
                    acc = tile(32 + i % 2)
                    link(ts(acc, tile(ADA_BASE[b]), st[:, 0:1], None, ALU.mult))
                    for k in range(1, KD):
                        ins = stt(acc, tile(ADA_BASE[b] + k), st[:, k:k + 1], acc, ALU.mult, ALU.add)
                        if k < KD - 1:
                            link(ins)
                    link(ins, sem("ada_used"), i + 1)

                def ada_out(i):
                    filled(dve, "ada", i)
                    link(tt(modT[:, 4 * i:4 * i + 4], pst("ada", i)[:, 0:4], col("b_ada", 4 * i, 4), ALU.add), *read("ada", i))

                for i in range(4):
                    ada_products(i)
                for i in range(4):
                    ada_out(i)
                link(stt(amp[:, 0, :], modT[:, 8:16], 1.0, col("norm1", 0, 8), ALU.add, ALU.mult))
                normed("rms1", tile(24), lambda i: amp[:, 0, i:i + 1], lambda i: modT[:, i:i + 1], lambda i: xL[:, i, :])
                dve.wait_ge(sem("narrow_high"), 1)
                link(low(narrow[:, 1, :], wab[:].rearrange("p k c -> p (k c)"), narrow[:, 0, :]), sem("narrow"), 1)
                for m in range(12):
                    for i in (2 * m, 2 * m + 1):
                        filled(dve, "qkv", i)
                        causal_conv("qkv", i, tile(Q0 + i), [col("conv", 4 * i + j) for j in range(4)], None, None)
                        tell(sem("conv"), i + 1)
                    if m < 8:
                        ada_products(4 + m)
                    if 3 <= m < 11:
                        ada_out(1 + m)
                link(stt(amp[:, 1, :], modT[:, 32:40], 1.0, col("norm2", 0, 8), ALU.add, ALU.mult))
                filled(dve, "ab")
                ab = pst("ab")[:, 0:64].rearrange("p (t c) -> p t c", c=16)
                link(tt(sm4[:, AB_X, :, 0:8], ab[:, :, 0:8], bm(col("dt_bias", 0, 8), NT), ALU.add))
                link(v.tensor_copy(sm4[:, AB_B, :, 0:8], ab[:, :, 8:16]), *read("ab"))
                link(ts(sm4[:, AB_A, :, 0:8], sm4[:, AB_X, :, 0:8], -1.0, None, ALU.mult))
                link(tt(sm4[:, AB_A, :, 0:8], sm4[:, AB_X, :, 0:8], sm4[:, AB_A, :, 0:8], ALU.max), sem("ab_dve"), 1)
                dve.wait_ge(sem("ab_act"), 1)
                link(stt(sm4[:, AB_X, :, 0:8], sm4[:, AB_X, :, 0:8], 0.0, sm4[:, AB_E, :, 8:16], ALU.max, ALU.add))
                link(stt(sm4[:, G, :, 0:8], sm4[:, AB_X, :, 0:8], -1.0, bm(sm4[:, AB_R, 0, 8:16], NT), ALU.mult, ALU.mult), sem("g_ready"), 1)
                link(ts(sm4[:, AB_B, :, 0:8], sm4[:, AB_B, :, 0:8], 1.0, None, ALU.add))
                link(v.reciprocal(sm4[:, BETA, :, 0:8], sm4[:, AB_B, :, 0:8]), sem("beta_ready"), 1)
                for i in range(16):
                    dve.wait_ge(sem("l2_rstd"), i + 1)
                    link(tt(tile(Q0 + i), tile(Q0 + i), tile(30 + i % 2), ALU.mult), sem("qk_normed"), i + 1)
                filled(dve, "gc")
                link(v.tensor_copy(sm4[:, GC, :, :], pst("gc")[:, 0:64].rearrange("p (t c) -> p t c", c=16)), *read("gc"))
                link(tt(sm4[:, KDEC, :, 0:8], sm4[:, GC, :, 8:16], sm4[:, GC, :, 0:8], ALU.subtract), sem("gc_dve"), 1)
                dve.wait_ge(sem("gc_act"), 1)
                link(tt(sm4[:, BE, :, 0:8], sm4[:, BETA, :, 0:8], sm4[:, EGC, :, 0:8], ALU.mult))
                for hf in range(2):
                    link(v.memset(pair(ST, hf), 0.0), sem("gdn_state"), hf + 1)
                for t in range(NT):
                    for hf in range(2):
                        n, h0 = 2 * t + hf + 1, hf * HALF
                        filled(dve, ("gb", t, hf))
                        link(tt(pair(DT, hf), heads4(("gb", t, hf)), bh(tok(GC, t, h0, 4)), ALU.subtract), sem("gb_minus"), n)
                        link(tt(pair(DT, hf), pair(DT, hf), bm(const("neg_after")), ALU.add), sem("gb_masked"), n)
                        dve.wait_ge(sem("gdn_decay"), n)
                        filled(dve, ("kk", t, hf))
                        link(tt(pair(AM, hf), heads4(("kk", t, hf)), pair(DT, hf), ALU.mult), *read(("kk", t, hf)))
                        filled(dve, ("bb", t, hf))
                        link(tt(pair(AM, hf), heads4(("bb", t, hf)), pair(AM, hf), ALU.mult), *read(("bb", t, hf)))
                        tell(sem("gdn_a"), n)
                        filled(dve, ("kq", t, hf))
                        link(tt(pair(ATT, hf), heads4(("kq", t, hf)), pair(DT, hf), ALU.mult), *read(("kq", t, hf)))
                        tell(sem("gdn_att"), n)
                        filled(dve, ("kt", t, hf))
                        link(tt(pair(KD_ROW, hf), heads4(("kt", t, hf)), bh(tok(KDEC, t, h0, 4)), ALU.mult), *read(("kt", t, hf)))
                        filled(dve, ("vt", t, hf))
                        link(tt(pair(VB, hf), heads4(("vt", t, hf)), bh(tok(BETA, t, h0, 4)), ALU.mult), *read(("vt", t, hf)))
                    inverse("gdn", t, 7)
                    for hf in range(2):
                        filled(dve, ("ks", t, hf))
                        link(tt(pair(RHS, hf), heads4(("ks", t, hf)), bh(tok(BE, t, hf * HALF, 4)), ALU.mult), *read(("ks", t, hf)))
                        link(tt(pair(RHS, hf), pair(VB, hf), pair(RHS, hf), ALU.subtract), sem("gdn_rhs"), 2 * t + hf + 1)
                    for hf in range(2):
                        filled(dve, ("su", t, hf))
                        link(tt(pair(ST, hf), pair(ST, hf), bh(tok(EGC, t, 8 + hf * HALF, 4)), ALU.mult))
                        link(tt(pair(ST, hf), pair(ST, hf), heads4(("su", t, hf)), ALU.add), *read(("su", t, hf)))
                        tell(sem("gdn_state"), 2 * t + hf + 3)
                for h in range(H):
                    dve.wait_ge(sem("o_rstd"), h + 1)
                    link(stt(tile(V0 + h), tile(V0 + h), col("dn_norm"), tile(30 + h % 2), ALU.mult, ALU.mult), sem("o_scaled"), h + 1)
                for h in range(H):
                    emptied(dve, "z", h)
                    link(tt(tile(V0 + h), tile(V0 + h), tile(Q0 + h), ALU.mult), sem("o_dn"), h + 1)
                dve.wait_ge(sem("wide_in"), 16)
                dve.wait_ge(pos_in, 16)
                link(v.tensor_copy(tile(8), trig[:, 0, :].bitcast(I32)))
                link(ts(tile(8), tile(8), col("inv_freq"), None, ALU.mult))
                for i in range(2):
                    dst = tile(9) if i == 0 else tile(10)
                    link(ts(tile(11), tile(8), 1.0 / (2 * np.pi), 0.25 * i, ALU.mult, ALU.add))
                    link(ts(tile(11), tile(11), 12582912.0, None, ALU.add))
                    link(ts(tile(11), tile(11), -12582912.0, None, ALU.add))
                    link(stt(dst, tile(11), -TURN[0], tile(8), ALU.mult, ALU.add))
                    link(stt(dst, tile(11), -TURN[1], dst, ALU.mult, ALU.add))
                    link(stt(dst, tile(11), -TURN[2], dst, ALU.mult, ALU.add))
                    if i:
                        link(ts(dst, dst, float(np.float32(np.pi / 2)), None, ALU.add))
                    link(ts(dst, dst, PI_IN, -PI_IN, ALU.min, ALU.max), sem("angle"), i + 1)
                dve.wait_ge(sem("kv_rstd"), 1)
                for k in range(2):
                    link(stt(tile(CKV + k), tile(CKV + k), col("kv_norm", k), tile(15), ALU.mult, ALU.mult), sem("ckv"), k + 1)
                lows("ckv", CKV_HIGH, CKV)
                dve.wait_ge(sem("kr_sq"), 1)
                link(ts(tile(KROPE), tile(KROPE), col("kn_rope"), None, ALU.mult), sem("kr_w"), 1)
                dve.wait_ge(sem("trig"), 2)
                for h in range(H):
                    dve.wait_ge(sem("k_rstd"), h + 1)
                    rs = tile(48 + h % 2)
                    b = slice(64 * (h % 2), 64 * (h % 2) + 64)
                    link(stt(tile(KN + h), tile(KN + h), col("kn_nope"), rs, ALU.mult, ALU.mult))
                    link(v.tensor_copy(tile(KR + h // 2)[b, :], rs[b, :]), sem("k_scaled"), h + 1)
                rope(tile(KRW), tile(KROPE), "krot", 0, tile(12))
                for p in range(4):
                    link(tt(tile(KR + p), tile(KR + p), tile(KRW), ALU.mult))
                filled(dve, "mv", 7)
                link(v.memset(st[:, 62:63], 0.0), sem("ckv_free"), 1)
                for h in range(H):
                    dve.wait_ge(sem("q_rstd"), h + 1)
                    rs = tile(48 + h % 2)
                    b = slice(64 * (h % 2), 64 * (h % 2) + 64)
                    link(stt(tile(QN + h), tile(QN + h), col("qn_nope"), rs, ALU.mult, ALU.mult))
                    link(stt(tile(QR + h // 2)[b, :], tile(QR + h // 2)[b, :], col("qn_rope")[b, :], rs[b, :], ALU.mult, ALU.mult),
                         sem("q_scaled"), h + 1)
                    if h % 2:
                        link(v.memset(st[:, 62:63], 0.0), sem("qr_w"), h // 2 + 1)
                for p in range(4):
                    rope(tile(QR + p), tile(QR + p), "qrot", p, tile(8 + p % 2))
                link(v.memset(st[:, 62:63], 0.0), sem("mla_qk"), 1)
                attention("mla", UNITS, 192 ** -0.5, (12, 13, 14, 11), lambda qt: wide[:, 0, S - (qt + 1) * P:S])
                lows("o_dn", O_DN_HIGH, V0)
                lows("o_mla", O_MLA_HIGH, QN)
                for fb in range(2):
                    for m in range(4):
                        emptied(dve, f"gate_dn{fb}", m)
                        filled(dve, f"y_dn{fb}", m)
                        link(tt(tile(MIX + 4 * fb + m), tile(8 + m), pst(f"y_dn{fb}", m), ALU.mult), *read(f"y_dn{fb}", m))
                        tell(sem("gate_used"), 8 * fb + m + 1)
                    for m in range(4):
                        emptied(dve, f"gate_mla{fb}", m)
                        filled(dve, f"y_mla{fb}", m)
                        link(tt(tile(12 + m % 2), tile(8 + m), pst(f"y_mla{fb}", m), ALU.mult), *read(f"y_mla{fb}", m))
                        tell(sem("gate_used"), 8 * fb + 4 + m + 1)
                        link(tt(tile(MIX + 4 * fb + m), tile(MIX + 4 * fb + m), tile(12 + m % 2), ALU.add), sem("mix"), 4 * fb + m + 1)
                lows("mix", MIX_HIGH, MIX)
                dve.wait_ge(x_in, 32)
                for i in range(KD):
                    filled(dve, "wo", i)
                    link(stt(xT[:, i, :], pst("wo", i), modT[:, 16 + i:17 + i], xT[:, i, :], ALU.mult, ALU.add), *read("wo", i))
                    tell(sem("x1"), i + 1)
                normed("rms2", tile(9), lambda i: amp[:, 1, i:i + 1], lambda i: modT[:, 24 + i:25 + i],
                       lambda i: tileR(H_LOW + i))

                def conv(job, i, dst):
                    causal_conv("up", job, dst, [col("fconv", 3 * i + j) for j in range(3)], None, None, bias=col("fbias", i))
                    tell(sem("fconv"), i + 1)

                filled(dve, "rms2")
                gated_up("", conv)
                for i in range(KD):
                    filled(dve, "down", i)
                    link(stt(xT[:, i, :], pst("down", i), modT[:, 40 + i:41 + i], xT[:, i, :], ALU.mult, ALU.add), *read("down", i))
                    tell(sem("x2"), i + 1)

            def block_2():
                link(ts(sm2[:, OM_MU:OM_MU + 14], col("mu", 0, 14), -1.0, 1.0, ALU.mult, ALU.add))
                link(ts(sm2[:, OM_KA:OM_KA + 4], col("k_a", 0, 4), -1.0, 1.0, ALU.mult, ALU.add))
                normed("rms3", tile(39), lambda i: col("norm1_2", i), None, lambda i: xL[:, i, :], (sem("x_kept"), 16))
                for i in range(14):
                    job, k = ("rkv", i) if i < 12 else ("wag", i - 12)
                    filled(dve, job, k)
                    causal_conv(job, k, tile(i), [col("mu", i), sm2[:, OM_MU + i:OM_MU + i + 1]], None, None)
                    tell(sem("shifted"), i + 1)
                dve.wait_ge(sem("narrow_high"), 2)
                link(low(narrow[:, 1, 0:64], wix[:].rearrange("p k c -> p (k c)"), narrow[:, 0, 0:64]), sem("narrow"), 2)
                for p in range(4):
                    filled(dve, "kkn", p)
                    if p >= 2:
                        dve.wait_ge(sem("kk_rstd"), p - 1)
                    link(ts(tile(36 + p % 2), pst("kkn", p), 1e-24, None, ALU.max), *read("kkn", p))
                    tell(sem("kk_clamped"), p + 1)
                    dve.wait_ge(sem("kk_rstd"), p + 1)
                    link(stt(tile(KAP + p), tile(KT + p), col("k_k", p), tile(38 + p % 2), ALU.mult, ALU.mult), sem("kk_used"), p + 1)
                    emptied(dve, "aup", p)
                    link(ts(tile(47), tile(BT + p), col("k_a", p), sm2[:, OM_KA + p:OM_KA + p + 1], ALU.mult, ALU.add))
                    link(tt(tile(KT + p), tile(KT + p), tile(47), ALU.mult))
                    link(tt(tile(BT + p), tile(BT + p), tile(KAP + p), ALU.mult))
                for p in range(4):
                    link(stt(tile(44 + p), tile(RHO + p), col("r_k", p), tile(KT + p), ALU.mult, ALU.mult), sem("bonus_in"), p + 1)
                for p in range(4):
                    filled(dve, "bon", p)
                    link(tt(tile(BV + p), pst("bon", p), tile(V2 + p), ALU.mult), *read("bon", p))
                for p in range(4):
                    gc = tile(GCUM + p % 2)
                    emptied(dve, "wup", p)
                    link(ts(tile(LD + p), tile(LD + p), -float(np.exp(-0.5)), None, ALU.mult))
                    link(v.tensor_tensor_scan(gc, wide[:, 3, :], tile(LD + p), 0.0, ALU.mult, ALU.add))
                    link(tt(tile(36), gc, tile(LD + p), ALU.subtract), sem("g_cum"), p + 1)
                    dve.wait_ge(sem("decays"), p + 1)
                    link(tt(tile(RHO + p), tile(RHO + p), tile(40), ALU.mult))
                    link(tt(tile(KAP + p), tile(KAP + p), tile(41), ALU.mult))
                    link(tt(tile(BT + p), tile(BT + p), tile(42), ALU.mult))
                    link(tt(tile(KT + p), tile(KT + p), tile(42), ALU.mult), sem("rw_ready"), p + 1)
                link(v.memset(tile(ST2)[:, 0:256], 0.0), sem("rw_state"), 1)
                for t in range(NT):
                    for par in range(2):
                        n = 2 * t + par + 1
                        filled(dve, ("rm", t, par))
                        link(v.tensor_copy(pair(36, par), heads4(("rm", t, par))), *read(("rm", t, par)))
                        tell(sem("rw_a"), n)
                        filled(dve, ("rn", t, par))
                        link(tt(pair(NTR, par), heads4(("rn", t, par)), bm(const("strict64")), ALU.mult), *read(("rn", t, par)))
                        tell(sem("rw_n"), n)
                        for k, (what, dst) in enumerate((("rb", BRT), ("rk", KRT))):
                            filled(dve, (what, t, par))
                            link(tt(pair(dst, par), heads4((what, t, par)), bm(const("incl64")), ALU.mult), *read((what, t, par)))
                            tell(sem("rw_b"), 2 * n + k - 1)
                    inverse("rw", t, 6)
                    emptied(dve, ("nv", t))
                    for e in range(2):
                        eb, n = slice(64 * e, 64 * e + 64), 2 * t + e
                        for par in range(2):
                            filled(dve, ("rs", t, e, par))
                            view = lambda x: x[eb, :].rearrange("p (k two c) -> p k two c", two=2, c=64)[:, :, par, :]
                            link(tt(view(tile(RSB)), pst(("rs", t, e, par))[eb, 0:256].rearrange("p (k c) -> p k c", c=64), view(tile(NVT)), ALU.add),
                                 *read(("rs", t, e, par)))
                        tell(sem("rw_rhs"), n + 1)
                        filled(dve, ("rz", t, e))
                        link(tt(tile(ST2)[:, 0:256], tile(ST2)[:, 0:256], pst(("rz", t, e))[:, 0:256], ALU.add), *read(("rz", t, e)))
                        s4 = tile(ST2)[:, 0:256].rearrange("p (k c) -> p k c", c=64)
                        link(tt(s4, s4, bh(sm2[:, EC + n:EC + 32:8], 64), ALU.mult), sem("rw_state"), n + 2)
                    filled(dve, ("yi", t))
                    for par in range(2):
                        emptied(dve, ("ry", t, 1, par))
                    y4 = ar[:, RHO:RHO + 4, t * P:(t + 1) * P]
                    link(tt(y4, y4, heads4(("yi", t)), ALU.add), *read(("yi", t)))
                    for k in range(4):
                        tell(sem("y_sum"), 4 * t + k + 1)
                for p in range(4):
                    filled(dve, "gmean", p)
                    link(stt(tile(RHO + p), pst("gmean", p), -1.0 / 64, tile(RHO + p), ALU.mult, ALU.add), *read("gmean", p))
                    tell(sem("gn_centred"), p + 1)
                for p in range(4):
                    dve.wait_ge(sem("gn_rstd"), p + 1)
                    link(stt(tile(RHO + p), tile(RHO + p), col("lnx_g", p), tile(41 + p % 2), ALU.mult, ALU.mult), sem("gn_used"), p + 1)
                    link(stt(tile(RHO + p), tile(RHO + p), col("lnx_b", p), tile(BV + p), ALU.add, ALU.add))
                    link(tt(tile(RHO + p), tile(RHO + p), tile(G2 + p), ALU.mult), sem("y_rw"), p + 1)
                lows("y_rw", Y_HIGH, RHO)
                filled(dve, "wi")
                link(v.tensor_copy(sm2[:, WI:WI + 32], pst("wi")[:, 0:32]), *read("wi"))
                dve.wait_ge(trig_in, 16)
                for i in range(5):
                    rope(tile(QI + i), tile(QI + i), "irot", i, tile(39))
                link(v.memset(st[:, 62:63], 0.0), sem("index_qk"), 1)
                for i in range(24):
                    q, h = i // 8, i % 8
                    w = (q + 2) * P
                    acc, wt = tile(SCO + q)[:, 0:w], sm2[:, WI + 8 * (q + 1) + h:WI + 8 * (q + 1) + h + 1]
                    emptied(dve, "index", i)
                    if h == 0:
                        link(ts(acc, tile(REL[i % 2])[:, 0:w], wt, None, ALU.mult), sem("index_used"), i + 1)
                    else:
                        link(stt(acc, tile(REL[i % 2])[:, 0:w], wt, acc, ALU.mult, ALU.add), sem("index_used"), i + 1)
                for i in range(8):
                    rope(tile(AQ + i), tile(AQ + i), "arot", i, tile(39))
                link(v.memset(st[:, 62:63], 0.0), sem("dsa_qk"), 1)
                for q in range(3):
                    w = (q + 2) * P
                    acc, work, sel = (tile(i)[:, 0:w] for i in (SCO + q, WORK, SEL + q))
                    top = sm2[:, TOP8:TOP8 + 8]
                    link(stt(acc, acc, 64 ** -0.5 * 8 ** -0.5, wide[:, 2, S - w:S], ALU.mult, ALU.add))
                    for r in range(TOPK // 8):
                        src = work if r else acc
                        link(v.max(top, src))
                        link(v.match_replace(work, top, src, -3.3e38))
                    link(tt(sel, work, acc, ALU.is_equal))
                    link(ts(sel, sel, NEG, None, ALU.mult))
                for m in range(8):
                    filled(dve, "yr", m)
                    emptied(dve, "gate_a", m)
                    link(tt(tile(MERGE + m), tile(MERGE + m), pst("yr", m), ALU.mult), *read("yr", m))
                attention("dsa", UNITS, 64 ** -0.5, (30, 31, 32, 29),
                          lambda qt: tile(SEL + qt - 1)[:, 0:(qt + 1) * P] if qt else wide[:, 1, S - P:S])
                lows("o_dsa", Y_HIGH, OA)
                for m in range(8):
                    filled(dve, "ya", m)
                    emptied(dve, "gate_b", m)
                    link(tt(tile(AQ + m), tile(AQ + m), pst("ya", m), ALU.mult), *read("ya", m))
                    link(tt(tile(MERGE + m), tile(MERGE + m), tile(AQ + m), ALU.add), sem("merged"), m + 1)
                lows("merged", MERGE_HIGH, MERGE)
                dve.wait_ge(sem("x3_in"), 16)
                for i in range(KD):
                    filled(dve, "wout", i)
                    link(tt(xT[:, i, :], xT[:, i, :], pst("wout", i), ALU.add), *read("wout", i))
                    tell(sem("x3"), i + 1)
                normed("rms4", tile(9), lambda i: col("norm2_2", i), None, lambda i: tileR(H_LOW + i))
                for p in range(11):
                    for j in range(2):
                        i, job = 2 * p + j, 4 * p + 2 + j
                        filled(dve, "up_2", job)
                        emptied(dve, "up_2", 4 * p + j)
                        link(tt(tile(i % 4) if i < NG else tile(G_REST + i - NG), tile(i % 4), pst("up_2", job), ALU.mult), *read("up_2", job))
                        tell(sem("gated_2"), i + 1)
                for i in range(KD):
                    filled(dve, "down_2", i)
                    link(tt(xT[:, i, :], xT[:, i, :], pst("down_2", i), ALU.add), *read("down_2", i))
                    tell(sem("x4"), i + 1)
                dve.wait_ge(*norm_step("rstd", "rms5"))
                for i in range(KD):
                    link(stt(xT[:, i, :], xT[:, i, :], col("normf", i), tile(9), ALU.mult, ALU.mult), sem("y_out"), i + 1)

            block_1()
            block_2()

        @block.gpsimd
        def _(pool):
            link = linker(pool, sem("pool_chain"))
            g = nc.gpsimd
            tt = g.tensor_tensor
            lows = [0]

            def split(value):
                while lows[0] < len(panel_release):
                    n = lows[0]
                    if n >= SPLIT and panel_release[n - SPLIT] > value:
                        break
                    lows[0] += 1
                    pool.wait_ge(panel_high, n + 1)
                    link(tt(W[:, n % SPLIT, 1, :], raw[:, n % RAW, :], W[:, n % SPLIT, 0, :].bitcast(F32), ALU.subtract), panel_low, n + 1)

            split_before[pool] = split

            def low_gated(sfx):
                for i in range(NF):
                    ahead(pool, "up" + sfx, 43 if i >= NG else 4 * (i // 2) + 2 + i % 2)
                    pool.wait_ge(sem("gated_high" + sfx), i + 1)
                    if i < NG:
                        link(tt(tileR(G_LOW + i), tile(i % 4), tileR(G_HIGH + i).bitcast(F32), ALU.subtract), sem("gated_low" + sfx), i + 1)
                    else:
                        rest = G_REST + i - NG
                        link(tt(tileR(rest), tile(rest), hH[:, i - NG, :].bitcast(F32), ALU.subtract), sem("gated_low" + sfx), i + 1)

            def inverse(name, t, levels):
                am, xtr, xx, mk, p1 = BASES[name]
                for lv in range(levels):
                    for hf in range(2):
                        if lv == 0:
                            ahead(pool, (name, "x0", t, hf))
                            pool.wait_ge(sem(f"{name}_a"), 2 * t + hf + 1)
                            s, value = sem(f"{name}_masked0"), 2 * t + hf + 1
                        else:
                            s, value = sem(f"{name}_masked"), (t * (levels - 1) + lv - 1) * 2 + hf + 1
                            if lv == 1:
                                pool.wait_ge(sem(f"{name}_xt0"), 2 * t + hf + 1)
                            else:
                                filled(pool, (name, "p1", t, lv - 1, hf))
                        link(tt(pair(mk, hf), pair(am, hf), bm(const(f"lvl{lv}")), ALU.mult), s, value)

            def block_1():
                for i in range(16):
                    ahead(pool, "qkv", i)
                    pool.wait_ge(sem("conv_silu"), i + 1)
                    if i >= 4:
                        filled(pool, "l2", i - 4)
                    link(tt(tile(24 + i % 4), tile(Q0 + i), tile(Q0 + i), ALU.mult), sem("l2_sq"), i + 1)
                pool.wait_ge(consts_in, 16)
                for t in range(NT):
                    for hf in range(2):
                        n = 2 * t + hf + 1
                        emptied(pool, ("gb", t, hf))
                        if n == 1:
                            pool.wait_ge(sem("qk_normed"), 16)
                        if t:
                            filled(pool, ("ot", t - 1, hf))
                        link(tt(pair(QE, hf), ar[:, Q0 + hf * HALF:Q0 + (hf + 1) * HALF, t * P:(t + 1) * P], pair(EGB, hf), ALU.mult),
                             sem("gdn_qe"), n)
                    inverse("gdn", t, 7)
                emptied(pool, ("ot", NT - 1, 1))
                emptied(pool, ("ot", NT - 1, 0))
                for h in range(H):
                    if h >= 4:
                        filled(pool, "onorm", h - 4)
                    link(tt(tile(24 + h % 4), tile(V0 + h), tile(V0 + h), ALU.mult), sem("onorm_sq"), h + 1)
                low_gated("")

            block_1()
            for t in range(NT):
                inverse("rw", t, 6)
            low_gated("_2")
            split(last["rms5", 0])


_T = 2 * np.pi
TURN = [201.0 / 32.0]
_r = _T - TURN[0]
TURN.append(float(np.float32(np.round(_r * 2 ** 22) / 2 ** 22)))
TURN.append(float(np.float32(_r - TURN[1])))
PI_IN = float(np.nextafter(np.float32(np.pi), np.float32(0)))


def _panels(w, width=256, size=PANEL):
    out = []
    kt = w.shape[0] // P
    per = size // width
    for n in range(0, w.shape[1], width):
        for k in range(0, kt, per):
            part = w[k * P:min(kt, k + per) * P, n:n + width]
            x = np.zeros((P, per, width), w.dtype)
            x[:, :part.shape[0] // P, :part.shape[1]] = part.reshape(-1, P, part.shape[1]).transpose(1, 0, 2)
            out.append(x.reshape(P, size))
    return out


def _col(v):
    return np.asarray(v).reshape(-1, P).T


def _row(v):
    return np.broadcast_to(np.asarray(v).reshape(1, -1), (P, np.asarray(v).size))


def _pairs(w, n):
    k = w.shape[0]
    return w.reshape(k, 2, n // 256, 256).transpose(0, 2, 1, 3).reshape(k, 2 * n)


def lay_out_2(f, c, out, panels):
    w = f["w_in_2"]
    c["norm1_2"], c["norm2_2"], c["normf"] = _col(f["norm1_g_2"]), _col(f["norm2_g_2"]), _col(f["normf_g_2"])
    c["mu"] = _col(f["tshift_mu_2"])
    for n in ("w0", "a0", "k_k", "k_a", "lnx_g", "lnx_b"):
        c[n] = _col(f[n + "_2"])
    c["r_k"] = _col(f["r_k_2"].reshape(-1))
    c["ln1024"] = np.full((P, 1), 10 * np.log(2.0), np.float32)
    out["lora"] = np.ascontiguousarray(np.stack([np.concatenate([f["w_decay_up_2"], f["a_up_2"]], 0), f["g_up_2"]], 1))
    out["wix"] = np.ascontiguousarray(w[:, 3904:3912].reshape(KD, P, 8).transpose(1, 0, 2))
    kidx = w[:, 3840:3904]
    panels += _panels(w[:, 0:1536]) + _panels(w[:, 1536:1792])
    panels += _panels(np.concatenate([w[:, 3328:3840], kidx, kidx], 1))
    panels += _panels(w[:, 1792:2816]) + _panels(w[:, 2816:3328])
    panels += _panels(w[:, 3912:4936]) + _panels(f["w_o_rwkv_2"], S) + _panels(w[:, 4936:5960]) + _panels(f["w_o_att_2"], S)
    panels += _panels(f["w_out_2"]) + _panels(_pairs(f["w_ffn_in_2"], FF)) + _panels(f["w_ffn_out_2"])


def lay_out(i):
    f = {k: np.asarray(v) for k, v in i.items()}
    cm, wide, inv = constants()
    out = {"cm": cm, "wide": np.ascontiguousarray(wide[:, [0, 1, 2, 5]]), "trig": np.ascontiguousarray(wide[:, [3, 4]])}
    c = {"one": np.ones((P, 1), np.float32), "eps": np.full((P, 1), EPS, np.float32),
         "qscale": np.full((P, 1), -0.5 * np.log(128.0), np.float32), "lnx": np.full((P, 1), LNX_EPS, np.float32), "inv_freq": inv}
    panels = []
    w_in = f["w_in"][0]
    at = np.cumsum([0, 1024, 1024, 1024, 1024, 8, 8, 1536, 256, 64, 1024, 1024])
    q, k, v, z, al, be, mq, ckv, kr, gd, gm = (w_in[:, at[j]:at[j + 1]] for j in range(11))
    c["b_ada"], c["norm1"] = _col(f["b_ada"][0]), _col(f["norm1_w"][0])
    c["conv"] = f["dn_conv_w"][0].reshape(4, 24, P).transpose(2, 1, 0).reshape(P, 96)
    c["dn_norm"] = _col(f["dn_norm_w"][0])
    c["kv_norm"] = _col(f["mla_kv_norm_w"][0])
    for n, w in (("qn", f["mla_q_norm_w"][0]), ("kn", f["mla_k_norm_w"][0])):
        c[n + "_nope"] = _col(w[:128])
        c[n + "_rope"] = _col(np.concatenate([w[128:], w[128:]]))
    c["norm2"] = _col(f["norm2_w"][0])
    c["fconv"] = f["ffn_conv_w"][0].reshape(3, NF, P).transpose(2, 1, 0).reshape(P, 3 * NF)
    c["fbias"] = _col(f["ffn_conv_b"][0])
    c["a_log"], c["dt_bias"] = _row(f["dn_a_log"][0]), _row(f["dn_dt_bias"][0])
    mq = mq.reshape(D, H, 192)
    nope, rope = mq[:, :, :128].reshape(D, 1024), mq[:, :, 128:].reshape(D, 512)
    out["ada"] = np.stack(_panels(f["w_ada"][0], S, KD * S)).reshape(12, P, KD, S)
    panels += _panels(np.concatenate([q, k, v], 1))
    panels += _panels(z) + _panels(np.concatenate([nope, rope], 1)) + _panels(np.concatenate([ckv, kr, kr], 1))
    panels += [w.reshape(2, P, 1024).transpose(1, 0, 2).reshape(P, 2048) for w in (f["mla_w_uk"][0], f["mla_w_uv"][0])]
    gd, gm, yd, ym = _panels(gd), _panels(gm), _panels(f["w_out_dn"][0]), _panels(f["w_out_mla"][0])
    panels += [x for b in range(2) for p in (gd, yd, gm, ym) for x in p[2 * b:2 * b + 2]]
    panels += _panels(f["w_o"][0]) + _panels(_pairs(f["ffn_w_up"][0], FF)) + _panels(f["ffn_w_down"][0])
    out["wab"] = np.ascontiguousarray(np.concatenate([al, be], 1).reshape(KD, P, 16).transpose(1, 0, 2))
    out["cT"] = np.ascontiguousarray(_col(f["c"][0]))
    out["posb"] = np.ascontiguousarray(_row(f["positions"][0]).astype(np.int32))
    lay_out_2(f, c, out, panels)
    out["panels"] = np.stack(panels)
    out["cols"] = np.concatenate([c[n] if n in c else np.zeros((P, w), np.float32) for n, w in COLS], 1).astype(np.float32)
    out["xT"] = np.ascontiguousarray(f["x"][0].T.reshape(KD, P, S).transpose(1, 0, 2))
    return out


def kernel(**inputs):
    import concourse.bacc as bacc
    from concourse.bass_utils import run_bass_kernel_spmd

    arrays = lay_out(inputs)
    nc = bacc.Bacc("TRN2", target_bir_lowering=False, num_devices=1)
    aps = {n: nc.dram_tensor(n + "_dram", x.shape, mybir.dt.from_np(x.dtype), kind="ExternalInput").ap() for n, x in arrays.items()}
    aps["out"] = nc.dram_tensor("out_dram", (P, KD, S), F32, kind="ExternalOutput").ap()
    build(nc, aps)
    r = run_bass_kernel_spmd(nc, [{n + "_dram": x for n, x in arrays.items()}], core_ids=[0])
    y = r.results[0]["out_dram"]
    return np.ascontiguousarray(y.transpose(1, 0, 2).reshape(D, S).T).reshape(1, S, D)
```

```python
from contextlib import ExitStack

import numpy as np

import concourse.bass as bass
from concourse import mybir

F32 = mybir.dt.float32
F32R = mybir.dt.float32r
I32 = mybir.dt.int32
ALU = mybir.AluOpType
ACT = mybir.ActivationFunctionType
AX_X = mybir.AxisListType.X

P = 128
S = 512
D = 1024
KD = D // P
NT = S // P
H = 8
FF = 2816
NF = FF // P
HALF = H // 2
RANK = 256
ROPE = 64
N64 = 64
TOPK = 128
EPS = 1e-6
LNX_EPS = 64e-5
NEG = -1e30
LOW = -3e38
PANEL = 2048
RAW = 2
SPLIT = 2
ADA_BASE = (8, 16, 34, 42)
ADA_AFTER = (0, 1, 3, 4, 6, 7, 9, 10)
L2_AFTER = {4: 0, 6: 1, 8: 2, 10: 3}


class Order:

    def __init__(self):
        self.job, self.last, self.n, self.steps = {}, {}, 0, 0

    def add(self, name, jobs=1, steps=1, first=0):
        for i in range(first, first + jobs):
            self.job[name, i] = self.n
            for s in range(steps):
                self.steps += 1
                self.last[name, i, s] = self.steps
            self.last[name, i] = self.steps
            self.n += 1

    def add_together(self, name, jobs, steps):
        for i in jobs:
            self.job[name, i] = self.n
            self.n += 1
        for s in range(steps):
            for i in jobs:
                self.steps += 1
                self.last[name, i, s] = self.last[name, i] = self.steps

    def bank(self, name, i=0):
        return self.job[name, i] % 8

    def use(self, name, i=0):
        return self.job[name, i] // 8


CONST_128 = ["ident", "ones", "top64", "low64", "same64", "rot", "utri", "neg_after", "strict64",
             "incl64"] + [f"lvl{i}" for i in range(7)]


def constants():
    j, c = np.meshgrid(np.arange(P), np.arange(P), indexing="ij")
    m = {}
    m["ident"] = j == c
    m["ones"] = j >= 0
    m["top64"] = j < 64
    m["low64"] = j >= 64
    m["same64"] = j // 64 == c // 64
    same = j // 64 == c // 64
    m["rot"] = np.where(same & (j % 64 == c % 64 + 32), -1.0, 0) + np.where(same & (j % 64 + 32 == c % 64), 1.0, 0)
    m["utri"] = j <= c
    m["neg_after"] = np.where(j > c, NEG, 0)
    m["strict64"] = same & (j < c)
    m["incl64"] = same & (j <= c)
    for i in range(7):
        b = 1 << i
        m[f"lvl{i}"] = (j // (2 * b) == c // (2 * b)) & (j % (2 * b) < b) & (c % (2 * b) >= b)
    sq = np.stack([np.asarray(m[k], np.float32) for k in CONST_128], 1)
    wide = np.zeros((6, P, S), np.float32)
    q, k = j, c
    wide[0, :, S - P:] = np.where((q < 64) & (k >= 64), NEG, 0)
    wide[1, :, S - P:] = np.where(k > q, NEG, 0)
    wide[2, :, S - P:] = np.where(k > q, LOW, 0)
    half = 32
    inv = (1.0 / (np.float32(10000.0) ** (np.arange(half, dtype=np.float32) * np.float32(2.0) / np.float32(64)))).astype(np.float32)
    ang = np.arange(S, dtype=np.float32)[None, :] * inv[np.arange(P) % 32][:, None]
    wide[3] = np.cos(ang)
    wide[4] = np.sin(ang)
    wide[5] = (np.arange(S) % 64 != 0)[None, :]
    inv_mla = (np.float32(10000.0) ** (-np.arange(half, dtype=np.float32) / np.float32(half))).astype(np.float32)
    col = inv_mla[np.arange(P) % 32][:, None].astype(np.float32)
    return np.ascontiguousarray(sq), np.ascontiguousarray(wide.transpose(1, 0, 2)), np.ascontiguousarray(col)


COLS = [("one", 1), ("eps", 1), ("qscale", 1), ("lnx", 1), ("ln1024", 1), ("b_ada", 48), ("norm1", 8), ("conv", 96), ("dn_norm", 1),
        ("kv_norm", 2), ("qn_nope", 1), ("qn_rope", 1), ("kn_nope", 1), ("kn_rope", 1), ("norm2", 8), ("fconv", 66),
        ("fbias", 22), ("a_log", 8), ("dt_bias", 8), ("inv_freq", 1),
        ("norm1_2", 8), ("mu", 14), ("w0", 4), ("a0", 4), ("k_k", 4), ("k_a", 4), ("r_k", 4), ("lnx_g", 4), ("lnx_b", 4),
        ("norm2_2", 8), ("normf", 8)]
COL_AT, NCOLS = {}, 0
for _name, _width in COLS:
    COL_AT[_name] = NCOLS
    NCOLS += _width

def attention_order(order, name, units):
    n = len(units)
    for u in range(n + 3):
        if u < n:
            order.add((name, "scores", u))
        if 2 <= u < n + 2:
            order.add((name, "turn", u - 2))
        if u >= 3:
            order.add((name, "values", u - 3))


GDN_BETWEEN = {1: [("kq", 0)], 2: [("kq", 1)], 3: [("kt", 0)], 4: [("kt", 1)], 5: [("vt", 0)], 6: [("vt", 1)]}
RW_BETWEEN = {1: [("vrow", 0), ("rn", 0)], 2: [("rn", 1)], 3: [("rb", 0), ("brow", 0)], 4: [("nv", 0), ("rb", 1)],
              5: [("rk", 0), ("rk", 1), ("krow", 0)]}


def inverse_order(order, name, t, levels, between):
    for hf in range(2):
        order.add((name, "x0", t, hf))
    for lv in range(1, levels):
        for hf in range(2):
            order.add((name, "p1", t, lv, hf))
        for what, hf in between[lv]:
            order.add((what, t, hf))
        for hf in range(2):
            order.add((name, "xt", t, lv, hf))
            if lv < levels - 1:
                order.add((name, "x", t, lv, hf))


def plan_1(order):
    order.add("ada")
    order.add("rms1")
    order.add("ada", 3, first=1)
    for m in range(12):
        order.add("qkv", 2, first=2 * m)
        if m - 2 in ADA_AFTER:
            order.add("ada", first=4 + ADA_AFTER.index(m - 2))
        if m in L2_AFTER:
            order.add("l2", 4, first=4 * L2_AFTER[m])
        if m == 9:
            order.add("ab")
        if m == 10:
            order.add("ab_turn")
    order.add("ada", first=11)
    order.add("gc")
    for t in range(NT):
        for hf in range(2):
            for what in ("gb", "bb", "kk"):
                order.add((what, t, hf))
        inverse_order(order, "gdn", t, 7, GDN_BETWEEN)
        for what in ("ks", "vn", "ot", "su"):
            for hf in range(2):
                order.add((what, t, hf))
    order.add("onorm", 8)
    order.add("z", 8)
    order.add("mkv", 3)
    order.add("mq", 4)
    order.add("kvn")
    order.add("mq", 4, first=4)
    order.add("krot")
    order.add("mq", 4, first=8)
    order.add("uk", 8)
    order.add("qss", 8)
    order.add("mv", 8)
    order.add("qrot", 4)
    order.add("kss", 8)
    order.add("gate_dn0", 2)
    attention_order(order, "mla", UNITS)
    order.add("gate_dn0", 2, first=2)
    for fb in range(2):
        if fb:
            order.add("gate_dn1", 4)
        order.add(f"y_dn{fb}", 4)
        order.add(f"gate_mla{fb}", 4)
        order.add(f"y_mla{fb}", 4)
    order.add("wo", 8)
    order.add("rms2")
    order.add("up", 44)
    for p in range(4):
        order.add_together("down", (2 * p, 2 * p + 1), 3)


def plan_2(order):
    order.add("rms3")
    order.add("rkv", 12)
    order.add("wag", 2)
    for what in ("kkn", "wup", "aup", "bon", "gup"):
        order.add(what, 4)
    for t in range(NT):
        for par in range(2):
            order.add(("rm", t, par))
        inverse_order(order, "rw", t, 6, RW_BETWEEN)
        for e in range(2):
            for par in range(2):
                order.add(("rs", t, e, par))
            order.add(("ru", t, e))
            for par in range(2):
                order.add(("ry", t, e, par))
            order.add(("rz", t, e))
        order.add(("yi", t))
    order.add("gmean", 4)
    order.add("gvar", 4)
    order.add("ai", 5)
    order.add("wi")
    order.add("wi_turn")
    order.add("irot", 5)
    order.add("index", 24)
    order.add("aq", 8)
    order.add_together("av", range(NT), 2)
    order.add("arot", 8)
    order.add("gate_a", 8)
    order.add("yr", 8)
    attention_order(order, "dsa", UNITS)
    order.add("gate_b", 8)
    order.add("ya", 8)
    order.add("wout", 8)
    order.add("rms4")
    order.add("up_2", 44)
    for p in range(4):
        order.add_together("down_2", (2 * p, 2 * p + 1), 3)
    order.add("rms5")


UNITS = [(h, qt) for h in range(H) for qt in range(NT)]


def panel_plan(order):
    first, release = {}, []

    def add(stage, releases):
        first[stage] = len(release)
        release.extend(releases)

    last = order.last

    def each(stage, jobs, per=2):
        add(stage, [last[stage, min(i + per, jobs) - 1] for i in range(0, jobs, per)])

    each("qkv", 24)
    each("z", 8)
    each("mkv", 3)
    each("mq", 12)
    add("ukv", [last["uk", 7], last["mv", 7]])
    for fb in range(2):
        for what in ("gate_dn", "y_dn", "gate_mla", "y_mla"):
            each(f"{what}{fb}", 4)
    each("wo", 8)
    each("up", 44)
    add("down", [last["down", 2 * p + 1, s] for p in range(4) for s in range(3)])
    each("rkv", 12)
    each("wag", 2)
    each("ai", 5)
    each("aq", 8)
    add("av", [last["av", NT - 1, s] for s in range(2)])
    each("gate_a", 8)
    each("yr", 8, 4)
    each("gate_b", 8)
    each("ya", 8, 4)
    each("wout", 8)
    each("up_2", 44)
    add("down_2", [last["down_2", 2 * p + 1, s] for p in range(4) for s in range(3)])
    return first, release


def build(nc, a):
    order = Order()
    plan_1(order)
    plan_2(order)
    bank, use, last = order.bank, order.use, order.last
    panel_first, panel_release = panel_plan(order)

    with ExitStack() as ctx:
        def sb(name, shape, dt=F32):
            return ctx.enter_context(nc.sbuf_tensor(name, shape, dt))

        sems = {}

        def sem(name):
            if name not in sems:
                sems[name] = ctx.enter_context(nc.semaphore(name))
            return sems[name]

        with nc.sbuf_tensor("xT", [P, KD, S], F32) as xT:
            pass
        xL = sb("xL", [P, KD, S], F32R)
        hH = sb("hH", [P, KD, S], F32R)
        raw = sb("raw", [P, RAW, PANEL])
        W = sb("W", [P, SPLIT, 2, PANEL], F32R)
        with nc.sbuf_tensor("ar", [P, 50, S], F32) as ar:
            pass
        arR = sb("arR", [P, 50, S], F32R)
        cm = sb("cm", [P, len(CONST_128), P])
        wide = sb("wide", [P, 4, S])
        trig = sb("trig", [P, 2, S])
        cols = sb("cols", [P, NCOLS])
        modT = sb("modT", [P, 48])
        amp = sb("amp", [P, 2, KD])
        cT = sb("cT", [P, KD])
        wab = sb("wab", [P, KD, 16])
        narrow = sb("narrow", [P, 2, KD * 16], F32R)
        sm4 = sb("sm4", [P, 12, NT, 16])
        st = sb("st", [P, 64])
        wix = sb("wix", [P, KD, 8])
        sm2 = sb("sm2", [P, 160])
        ps = ctx.enter_context(nc.psum_tensor("ps", [P, 8, S], F32))

        def col(name, i=0, n=1):
            return cols[:, COL_AT[name] + i:COL_AT[name] + i + n]

        def const(name):
            return cm[:, CONST_128.index(name), :]

        pe_done = sem("pe_done")
        bank_read = [sem(f"bank{b}_read") for b in range(8)]
        panel_in = [sem(f"panel_in{s}") for s in range(RAW)]
        panel_high, panel_low = sem("panel_high"), sem("panel_low")
        ada_in = [sem(f"ada_in{b}") for b in range(4)]
        cols_in, consts_in, x_in, small2_in, ab_in, pos_in, trig_in, out_sent = (
            sem(n) for n in ("cols_in", "consts_in", "x_in", "small2_in", "ab_in", "pos_in", "trig_in", "out_sent"))

        def pst(name, i=0):
            return ps[:, bank(name, i), :]

        split_before = {}

        def ahead(eng, name, i=0):
            if eng in split_before:
                split_before[eng](last[name, i])

        def filled(eng, name, i=0):
            ahead(eng, name, i)
            eng.wait_ge(pe_done, last[name, i])

        def read(name, i=0):
            return bank_read[bank(name, i)], use(name, i) + 1

        def emptied(eng, name, i=0):
            ahead(eng, name, i)
            eng.wait_ge(*read(name, i))

        def linker(eng, chain):
            n = [0]

            def link(ins, s=None, value=None):
                if s is None:
                    n[0] += 1
                    s, value = chain, n[0]
                ins.then_inc(s, 1)
                eng.wait_ge(s, value)
            return link

        def tile(i):
            return ar[:, i, :]

        def tileR(i):
            return arR[:, i, :]

        def parts_in(high, low):
            return lambda k: (tileR(high[k]), tileR(low[k]))

        def h_mix(k):
            return hH[:, k, :], xL[:, k, :]

        def h_ff(k):
            return hH[:, k, :], tileR(H_LOW + k)

        def pair(i, hf):
            return ar[:, i + hf, :].rearrange("p (h c) -> p h c", c=P)

        def heads(i, h):
            return ar[:, i + h // HALF, (h % HALF) * P:(h % HALF + 1) * P]

        Q0, K0, V0 = 0, 8, 16
        BASES = {"gdn": (26, 36, 38, 40, 42), "rw": (36, 38, 40, 42, 44)}
        DT, AM, ATT, KD_ROW, VB, QE, XTR, XX, MK, P1, EGB, VN, ST = 24, 26, 28, 30, 32, 34, 36, 38, 40, 42, 44, 48, 46
        RHS = DT
        LORA = 46
        lora = ar[:, LORA:LORA + 2, :]
        RHO, KT, V2, WA, GD, BT, G2, LD, KAP, BV = 0, 4, 8, 12, 13, 14, 18, 22, 26, 32
        NTR, BRT, KRT, VROW, BROW, KROW, RSB, UU, ST2, NVT = 46, 48, 22, 24, 25, 12, 13, 30, 31, 46
        AQ, AK, QI, KI, AV, SEL, SCO, WORK, REL, OA, MERGE = 4, 8, 12, 16, 18, 22, 25, 28, (29, 17), 35, 42
        OM_MU, OM_KA, EC, WI, TOP8 = 0, 14, 24, 56, 88
        QN, QR, KN, KR, MV, CKV, KROPE, KRW = 24, 32, 36, 44, 0, 8, 10, 11
        MIX = 0
        H_LOW, G_HIGH, G_LOW, NG, G_REST = 42, 4, 20, 16, 36
        O_DN_HIGH, O_MLA_HIGH, MIX_HIGH = list(range(36, 44)), [32, 33, 34, 35, 44, 45, 46, 47], list(range(16, 24))
        CKV_HIGH, Y_HIGH, MERGE_HIGH = [12, 13], list(range(30, 34)), list(range(12, 20))

        def bh(x, n=P):
            return x.unsqueeze(2).to_broadcast([x.shape[0], x.shape[1], n])

        def bm(x, n=HALF):
            return x.unsqueeze(1).to_broadcast([x.shape[0], n, x.shape[1]])

        def heads4(name, i=0):
            return pst(name, i).rearrange("p (h c) -> p h c", c=P)

        AB_X, AB_A, AB_E, AB_B, G, GC, EGC, KDEC, BE, BETA, AB_R = range(11)

        def tok(which, t, lo=0, n=8):
            return sm4[:, which, t, lo:lo + n]

        RS_Q, RS_K = (15, 48, 44, 45), (15, 48, 12, 13)
        SPLIT_AT = {"ckv": 0, "o_dn": 2, "o_mla": 10, "mix": 18, "y_rw": 26, "o_dsa": 30, "merged": 34}

        def part_ready(which, name, k):
            return sem(f"operand_{which}"), SPLIT_AT[name] + k + 1

        def norm_step(what, name, i=0):
            n = int(name[3:]) - 1
            return sem(f"norm_{what}"), n + 1 if what in ("rstd", "added") else KD * n + i + 1

        T_OF = {"rms1": 25, "rms2": 10, "rms3": 34, "rms4": 10}

        block = ctx.enter_context(nc.Block())

        @block.sync
        def _(sp):
            sp.dma_start(cols[:], a["cols"]).then_inc(cols_in, 16)
            sp.dma_start(cT[:], a["cT"]).then_inc(cols_in, 16)

            def load_ada(i):
                if i >= 4:
                    sp.wait_ge(sem("ada_used"), i - 2)
                b = i if i < 4 else 2 + i % 2
                sp.dma_start(ar[:, ADA_BASE[b]:ADA_BASE[b] + 8, :], a["ada"][i]).then_inc(ada_in[b], 16)

            load_ada(0)
            load_ada(1)
            sp.dma_start(xT[:], a["xT"]).then_inc(x_in, 16)
            sp.dma_start(cm[:], a["cm"]).then_inc(consts_in, 16)
            load_ada(2)
            load_ada(3)
            ada_loads = {1: 4, 2: 5, **{m + 3: 6 + j for j, m in enumerate(ADA_AFTER[:6])}}
            for n, free in enumerate(panel_release):
                if n >= RAW:
                    sp.wait_ge(panel_low, n - RAW + 1)
                sp.dma_start(raw[:, n % RAW, :], a["panels"][n]).then_inc(panel_in[n % RAW], 16)
                if n == 1:
                    sp.dma_start(wab[:], a["wab"]).then_inc(ab_in, 16)
                    sp.dma_start(wide[:], a["wide"]).then_inc(sem("wide_in"), 16)
                    sp.dma_start(trig[:, 0, :].bitcast(I32), a["posb"]).then_inc(pos_in, 16)
                if n in ada_loads:
                    load_ada(ada_loads[n])
                if n == panel_first["wo"]:
                    sp.wait_ge(pe_done, last["gate_mla1", 3])
                    sp.dma_start(xT[:], a["xT"]).then_inc(x_in, 16)
                if n == panel_first["rkv"] + 1:
                    for i in range(KD):
                        emptied(sp, "down", i)
                    sp.dma_start(a["out"], xT[:]).then_inc(sem("x_kept"), 16)
                    sp.wait_ge(pe_done, last["rms3", 0])
                    sp.dma_start(lora[:], a["lora"]).then_inc(small2_in, 16)
                    sp.dma_start(wix[:], a["wix"]).then_inc(small2_in, 16)
                    sp.dma_start(trig[:], a["trig"]).then_inc(trig_in, 16)
                if n == panel_first["wout"]:
                    sp.wait_ge(sem("x_kept"), 16)
                    sp.wait_ge(pe_done, last["gate_b", 7])
                    sp.dma_start(xT[:], a["out"]).then_inc(sem("x3_in"), 16)
            for i in range(0, KD, 2):
                sp.wait_ge(sem("y_out"), i + 2)
                sp.dma_start(a["out"][:, i:i + 2, :], xT[:, i:i + 2, :]).then_inc(out_sent, 16)
            sp.wait_ge(out_sent, 16 * (KD // 2))

        @block.tensor
        def _(pe):
            mm = nc.tensor.matmul

            def begin(name, i=0):
                if use(name, i):
                    pe.wait_ge(bank_read[bank(name, i)], use(name, i))

            def end(ins):
                ins.then_inc(pe_done, 1)

            def panel(stage, i=0, width=256):
                n = panel_first[stage] + i
                pe.wait_ge(panel_low, n + 1)
                return [W[:, n % SPLIT, j, :].rearrange("p (k c) -> p k c", c=width) for j in range(2)]

            def product(out, lhs, rhs, first, final):
                mm(out, lhs[0], rhs[0], start=first, stop=False)
                mm(out, lhs[0], rhs[1], start=False, stop=False)
                return mm(out, lhs[1], rhs[0], start=False, stop=final)

            def project(stage, src, jobs, ready=None, kt=KD, per=2, i0=0):
                for i in range(i0, i0 + jobs):
                    w = panel(stage, i // per, PANEL // kt)
                    begin(stage, i)
                    for k in range(kt):
                        if ready and i == 0:
                            pe.wait_ge(*ready(k))
                        ins = product(pst(stage, i), [x[:, k, (i % per) * P:(i % per + 1) * P] for x in w], src(k), k == 0, k == kt - 1)
                    end(ins)

            def narrow_product(name, n, count):
                pe.wait_ge(sem("narrow"), count)
                begin(name)
                for k in range(KD):
                    ins = product(pst(name)[0:n, :], [narrow[:, j, k * n:(k + 1) * n] for j in range(2)], h_mix(k), k == 0, k == KD - 1)
                end(ins)

            def narrow_turn(name, src, n):
                emptied(pe, name)
                begin(f"{name}_turn")
                for t in range(NT):
                    ins = nc.tensor.transpose(pst(f"{name}_turn")[:, t * n:(t + 1) * n], src[0:n, t * P:(t + 1) * P], const("ident")[0:n, 0:n])
                end(ins)

            def tokens(x, t):
                return [part[:, t * P:(t + 1) * P] for part in x]

            def column_sums(name, i, squares, waits=(), sel="ones"):
                begin(name, i)
                for k, sq in enumerate(squares):
                    if k < len(waits):
                        pe.wait_ge(*waits[k])
                    ins = mm(pst(name, i), sel[k] if isinstance(sel, list) else const(sel), sq,
                             start=(k == 0), stop=(k == len(squares) - 1))
                end(ins)

            def inverse(name, t, levels, between, job):
                am, xtr, xx, mk, p1 = BASES[name]
                for hf in range(2):
                    pe.wait_ge(sem(f"{name}_xt0"), 2 * t + hf + 1)
                    begin((name, "x0", t, hf))
                    for h in range(HALF):
                        ins = nc.tensor.transpose(heads4((name, "x0", t, hf))[:, h, :], pair(xtr, hf)[:, h, :], const("ident"))
                    end(ins)
                for lv in range(1, levels):
                    for hf in range(2):
                        k = (t * (levels - 1) + lv - 1) * 2 + hf
                        pe.wait_ge(sem(f"{name}_masked"), k + 1)
                        if lv == 1:
                            emptied(pe, (name, "x0", t, hf))
                        else:
                            emptied(pe, (name, "xt", t, lv - 1, hf))
                            emptied(pe, (name, "x", t, lv - 1, hf))
                        begin((name, "p1", t, lv, hf))
                        for h in range(HALF):
                            ins = mm(heads4((name, "p1", t, lv, hf))[:, h, :], pair(mk, hf)[:, h, :], pair(xx, hf)[:, h, :],
                                     start=True, stop=True)
                        end(ins)
                    for what, hf in between[lv]:
                        job(what, t, hf)
                    for hf in range(2):
                        emptied(pe, (name, "p1", t, lv, hf))
                        begin((name, "xt", t, lv, hf))
                        for h in range(HALF):
                            ins = mm(heads4((name, "xt", t, lv, hf))[:, h, :], pair(p1, hf)[:, h, :], pair(xtr, hf)[:, h, :],
                                     start=True, stop=True)
                        end(ins)
                        if lv < levels - 1:
                            begin((name, "x", t, lv, hf))
                            for h in range(HALF):
                                ins = mm(heads4((name, "x", t, lv, hf))[:, h, :], pair(xtr, hf)[:, h, :], pair(p1, hf)[:, h, :],
                                         start=True, stop=True)
                            end(ins)

            def attention(name, units, score, value, smt, ptt):
                n = len(units)
                for u in range(n + 3):
                    if u < n:
                        h, qt = units[u]
                        begin((name, "scores", u))
                        end(score(pst((name, "scores", u))[:, 0:(qt + 1) * P], h, qt))
                    if 2 <= u < n + 2:
                        h, qt = units[u - 2]
                        pe.wait_ge(sem(f"{name}_probs"), u - 1)
                        begin((name, "turn", u - 2))
                        for kt in range(qt + 1):
                            ins = nc.tensor.transpose(pst((name, "turn", u - 2))[:, kt * P:(kt + 1) * P],
                                                      tile(smt[(u - 2) % 4])[:, kt * P:(kt + 1) * P], const("ident"))
                        end(ins)
                    if u >= 3:
                        h, qt = units[u - 3]
                        emptied(pe, (name, "turn", u - 3))
                        begin((name, "values", u - 3))
                        for kt in range(qt + 1):
                            out, lhs = value(pst((name, "values", u - 3)), h, kt)
                            ins = mm(out, lhs, tile(ptt[(u - 3) % 2])[:, kt * P:(kt + 1) * P], start=(kt == 0), stop=(kt == qt))
                        end(ins)

            def feed_forward(sfx, norm):
                project("up" + sfx, h_ff, 44, lambda k: norm_step("low", norm, k))
                for p in range(4):
                    jobs = (2 * p, 2 * p + 1)
                    for s in range(3):
                        w = panel("down" + sfx, 3 * p + s)
                        nk = min(8, NF - 8 * s)
                        if p == 0:
                            pe.wait_ge(sem("gated_low" + sfx), min(8 * s + 8, NF))
                        for m, i in enumerate(jobs):
                            if s == 0:
                                begin("down" + sfx, i)
                            for k in range(nk):
                                kk = 8 * s + k
                                g = (tileR(G_HIGH + kk), tileR(G_LOW + kk)) if kk < NG else (hH[:, kk - NG, :], tileR(G_REST + kk - NG))
                                ins = product(pst("down" + sfx, i), [x[:, k, m * P:(m + 1) * P] for x in w], g, kk == 0, kk == NF - 1)
                            end(ins)

            def block_1():
                def ada(i):
                    if i == 0:
                        pe.wait_ge(ada_in[0], 16)
                    else:
                        pe.wait_ge(sem("ada_used"), i)
                    begin("ada", i)
                    for m in range(4):
                        out, c = pst("ada", i)[:, m:m + 1], slice(m * P, (m + 1) * P)
                        if i == 0:
                            for k in range(KD):
                                ins = mm(out, tile(ADA_BASE[0] + k)[:, c], st[:, k:k + 1], start=(k == 0), stop=(k == KD - 1))
                        else:
                            ins = mm(out, tile(32 + i % 2)[:, c], const("ones")[:, 0:1], start=True, stop=True)
                    end(ins)

                pe.wait_ge(sem("silu_c"), 1)
                ada(0)
                pe.wait_ge(consts_in, 16)
                column_sums("rms1", 0, [tile(i) for i in (0, 6, 7)],
                            [norm_step("added", "rms1"), norm_step("squares", "rms1", 6), norm_step("squares", "rms1", 7)])
                for i in range(1, 4):
                    ada(i)
                for m in range(12):
                    project("qkv", h_mix, 2, lambda k: norm_step("low", "rms1", k), i0=2 * m)
                    if m - 2 in ADA_AFTER:
                        ada(4 + ADA_AFTER.index(m - 2))
                    if m in L2_AFTER:
                        for i in range(4 * L2_AFTER[m], 4 * L2_AFTER[m] + 4):
                            column_sums("l2", i, [tile(24 + i % 4)], [(sem("l2_sq"), i + 1)])
                    if m == 9:
                        narrow_product("ab", 16, 1)
                    if m == 10:
                        narrow_turn("ab", tile(V0 + 7), 16)
                ada(11)
                pe.wait_ge(sem("g_ready"), 1)
                begin("gc")
                for t in range(NT):
                    mm(pst("gc")[:, t * 16:t * 16 + 8], const("utri"), tok(G, t), start=True, stop=True)
                    ins = mm(pst("gc")[:, t * 16 + 8:t * 16 + 16], const("ones"), tok(G, t), start=True, stop=True)
                end(ins)
                def gdn_job(what, t, hf):
                    c = slice(t * P, (t + 1) * P)
                    begin((what, t, hf))
                    for h in range(hf * HALF, (hf + 1) * HALF):
                        out = heads4((what, t, hf))[:, h % HALF, :]
                        if what in ("kk", "kq"):
                            ins = mm(out, tile(K0 + h)[:, c], tile((K0 if what == "kk" else Q0) + h)[:, c], start=True, stop=True)
                        else:
                            ins = nc.tensor.transpose(out, tile((K0 if what == "kt" else V0) + h)[:, c], const("ident"))
                    end(ins)

                for t in range(NT):
                    c = slice(t * P, (t + 1) * P)
                    for hf in range(2):
                        hs = range(hf * HALF, (hf + 1) * HALF)
                        begin(("gb", t, hf))
                        for h in hs:
                            ins = mm(heads4(("gb", t, hf))[:, h % HALF, :], tok(G, t, h, 1).to_broadcast([P, P]), const("utri"),
                                     start=True, stop=True)
                        end(ins)
                        pe.wait_ge(sem("beta_ready"), 1)
                        begin(("bb", t, hf))
                        for h in hs:
                            ins = mm(heads4(("bb", t, hf))[:, h % HALF, :], tok(BETA, t, h, 1).to_broadcast([P, P]), const("ident"),
                                     start=True, stop=True)
                        end(ins)
                        pe.wait_ge(sem("qk_normed"), 16)
                        gdn_job("kk", t, hf)
                    if t == 0:
                        pe.wait_ge(sem("conv_silu"), 24)
                    inverse("gdn", t, 7, GDN_BETWEEN, gdn_job)
                    for hf in range(2):
                        begin(("ks", t, hf))
                        if t:
                            pe.wait_ge(sem("gdn_state"), 2 * t + hf + 1)
                        else:
                            pe.wait_ge(sem("gdn_state"), hf + 1)
                        for h in range(hf * HALF, (hf + 1) * HALF):
                            ins = mm(heads4(("ks", t, hf))[:, h % HALF, :], tile(K0 + h)[:, c], heads(ST, h), start=True, stop=True)
                        end(ins)
                    for hf in range(2):
                        pe.wait_ge(sem("gdn_rhs"), 2 * t + hf + 1)
                        emptied(pe, ("gdn", "xt", t, 6, hf))
                        begin(("vn", t, hf))
                        for h in range(HALF):
                            ins = mm(heads4(("vn", t, hf))[:, h, :], pair(XTR, hf)[:, h, :], pair(RHS, hf)[:, h, :],
                                     start=True, stop=True)
                        end(ins)
                    for hf in range(2):
                        emptied(pe, ("vn", t, hf))
                        pe.wait_ge(sem("gdn_qe"), 2 * t + hf + 1)
                        emptied(pe, ("kq", t, hf))
                        begin(("ot", t, hf))
                        for h in range(hf * HALF, (hf + 1) * HALF):
                            o = heads4(("ot", t, hf))[:, h % HALF, :]
                            mm(o, heads(ST, h), heads(QE, h), start=True, stop=False)
                            ins = mm(o, heads(VN, h), heads(ATT, h), start=False, stop=True)
                        end(ins)
                    for hf in range(2):
                        begin(("su", t, hf))
                        for h in range(hf * HALF, (hf + 1) * HALF):
                            ins = mm(heads4(("su", t, hf))[:, h % HALF, :], heads(KD_ROW, h), heads(VN, h), start=True, stop=True)
                        end(ins)
                for h in range(H):
                    column_sums("onorm", h, [tile(24 + h % 4)], [(sem("onorm_sq"), h + 1)])
                project("z", h_mix, 8)
                project("mkv", h_mix, 3)
                project("mq", h_mix, 4)
                column_sums("kvn", 0, [tile(12), tile(13)], [(sem("kv_sq"), i + 1) for i in range(2)])
                project("mq", h_mix, 4, i0=4)
                pe.wait_ge(sem("kr_w"), 1)
                begin("krot")
                end(mm(pst("krot"), const("rot"), tile(KRW), start=True, stop=True))
                project("mq", h_mix, 4, i0=8)
                w = panel("ukv", 0, D)
                latent = parts_in(CKV_HIGH, [CKV, CKV + 1])
                pe.wait_ge(*part_ready("low", "ckv", 1))
                for h in range(H):
                    begin("uk", h)
                    for k in range(2):
                        ins = product(pst("uk", h), [x[:, k, h * P:(h + 1) * P] for x in w], latent(k), k == 0, k == 1)
                    end(ins)
                for h in range(H):
                    column_sums("qss", h, [tile(MV + h // 2), tile(MV + 4 + h % 4)],
                                [(sem("qr_sq"), h // 2 + 1), (sem("nope_sq"), h + 1)],
                                sel=[const("low64" if h % 2 else "top64"), const("ones")])
                w = panel("ukv", 1, D)
                for i in range(8):
                    t, half = i // 2, i % 2
                    begin("mv", i)
                    for k in range(2):
                        ins = product(pst("mv", i), tokens(latent(k), t), [x[:, k, half * S:(half + 1) * S] for x in w], k == 0, k == 1)
                    end(ins)
                for p in range(4):
                    pe.wait_ge(sem("qr_w"), p + 1)
                    begin("qrot", p)
                    end(mm(pst("qrot", p), const("rot"), tile(QR + p), start=True, stop=True))
                for h in range(H):
                    column_sums("kss", h, [tile(8), tile((14, 49)[h % 2])], [(sem("kr_sq"), 1), (sem("nope_sq"), H + h + 1)],
                                sel=[const("top64"), const("ones")])

                emptied(pe, "mv", 7)

                def score(out, h, qt):
                    if qt == 0:
                        pe.wait_ge(sem("k_scaled"), h + 1)
                    b = slice(64 * (h % 2), 64 * (h % 2) + 64)
                    mm(out, tile(QN + h)[:, qt * P:(qt + 1) * P], tile(KN + h)[:, 0:(qt + 1) * P], start=True, stop=False)
                    return mm(out, tile(QR + h // 2)[b, qt * P:(qt + 1) * P], tile(KR + h // 2)[b, 0:(qt + 1) * P],
                              start=False, stop=True)

                def value(out, h, kt):
                    return out[:, 0:P], ar[:, MV + 2 * kt + h // 4, (h % 4) * P:(h % 4 + 1) * P]

                project("gate_dn0", h_mix, 2)
                attention("mla", UNITS, score, value, (12, 13, 14, 11), (15, 48))
                project("gate_dn0", h_mix, 2, i0=2)
                for fb in range(2):
                    if fb:
                        project("gate_dn1", h_mix, 4)
                    project(f"y_dn{fb}", parts_in(O_DN_HIGH, range(V0, V0 + 8)), 4, lambda k: part_ready("low", "o_dn", k))
                    project(f"gate_mla{fb}", h_mix, 4)
                    project(f"y_mla{fb}", parts_in(O_MLA_HIGH, range(QN, QN + 8)), 4, lambda k: part_ready("low", "o_mla", k))
                project("wo", parts_in(MIX_HIGH, range(MIX, MIX + 8)), 8, lambda k: part_ready("low", "mix", k))
                column_sums("rms2", 0, [tile(i) for i in (24, 30, 31)],
                            [norm_step("added", "rms2"), norm_step("squares", "rms2", 6), norm_step("squares", "rms2", 7)])
                feed_forward("", "rms2")

            def head64(x, h):
                return x[64 * (h % 2):64 * (h % 2) + 64]

            def block_2():
                pe.wait_ge(consts_in, 16)
                column_sums("rms3", 0, [tile(i) for i in (42, 48, 49)],
                            [norm_step("added", "rms3"), norm_step("squares", "rms3", 6), norm_step("squares", "rms3", 7)])
                project("rkv", h_mix, 12, lambda k: norm_step("low", "rms3", k))
                project("wag", h_mix, 2)
                for p in range(4):
                    column_sums("kkn", p, [tile(40 + p)], [(sem("kk_sq"), p + 1)], sel="same64")
                pe.wait_ge(small2_in, 32)
                pe.wait_ge(sem("lora_act"), 2)
                for p in range(4):
                    begin("wup", p)
                    end(mm(pst("wup", p), lora[0:64, 0, p * P:(p + 1) * P], tile(WA)[0:64, :], start=True, stop=True))
                for p in range(4):
                    begin("aup", p)
                    end(mm(pst("aup", p), lora[64:P, 0, p * P:(p + 1) * P], tile(WA)[64:P, :], start=True, stop=True))
                for p in range(4):
                    column_sums("bon", p, [tile((44, 45, 48, 49)[p])], [(sem("bonus_in"), p + 1)], sel="same64")
                for p in range(4):
                    begin("gup", p)
                    end(mm(pst("gup", p), lora[:, 1, p * P:(p + 1) * P], tile(GD), start=True, stop=True))

                def rw_job(what, t, par):
                    c = slice(t * P, (t + 1) * P)
                    if what == "nv":
                        for half in range(2):
                            emptied(pe, ("rn", t, half))
                        emptied(pe, ("vrow", t, 0))
                    begin((what, t, par))
                    if what == "nv":
                        for h in range(H):
                            ins = mm(pst(("nv", t, 0))[:, h * 64:(h + 1) * 64], pair(NTR, h % 2)[:, h // 2, :], tile(VROW)[:, h * 64:(h + 1) * 64],
                                     start=True, stop=True)
                    elif what in ("vrow", "brow", "krow"):
                        for p in range(4):
                            ins = nc.tensor.transpose(heads4((what, t, 0))[:, p, :], tile({"vrow": V2, "brow": BT, "krow": KT}[what] + p)[:, c], const("ident"))
                    else:
                        b = slice(64 * par, 64 * par + 64)
                        lhs, rhs = {"rm": (BT, KAP), "rn": (KT, KAP), "rb": (BT, RHO), "rk": (KT, RHO)}[what]
                        for p in range(4):
                            ins = mm(heads4((what, t, par))[:, p, :], tile(lhs + p)[b, c], tile(rhs + p)[b, c], start=True, stop=True)
                    end(ins)

                pe.wait_ge(sem("rw_ready"), 4)
                pe.wait_ge(sem("beta_decayed"), 4)
                for t in range(NT):
                    c = slice(t * P, (t + 1) * P)
                    for par in range(2):
                        rw_job("rm", t, par)
                    inverse("rw", t, 6, RW_BETWEEN, rw_job)
                    for e in range(2):
                        eb, n = slice(64 * e, 64 * e + 64), 2 * t + e
                        ec = slice(t * P + 64 * e, t * P + 64 * e + 64)
                        pe.wait_ge(sem("rw_state"), n + 1)
                        for par in range(2):
                            b = slice(64 * par, 64 * par + 64)
                            begin(("rs", t, e, par))
                            for p in range(4):
                                ins = mm(pst(("rs", t, e, par))[eb, p * 64:(p + 1) * 64], tile(KAP + p)[b, ec],
                                         tile(ST2)[b, p * 64:(p + 1) * 64], start=True, stop=True)
                            end(ins)
                        if e == 0:
                            for par in range(2):
                                emptied(pe, ("rw", "xt", t, 5, par))
                        pe.wait_ge(sem("rw_rhs"), n + 1)
                        begin(("ru", t, e))
                        for h in range(H):
                            ins = mm(pst(("ru", t, e))[eb, h * 64:(h + 1) * 64], pair(38, h % 2)[eb, h // 2, eb],
                                     tile(RSB)[eb, h * 64:(h + 1) * 64], start=True, stop=True)
                        end(ins)
                        for par in range(2):
                            b = slice(64 * par, 64 * par + 64)
                            begin(("ry", t, e, par))
                            for p in range(4):
                                ins = mm(pst(("ry", t, e, par))[b, p * 64:(p + 1) * 64], tile(ST2)[b, p * 64:(p + 1) * 64],
                                         tile(RHO + p)[b, ec], start=True, stop=True)
                            end(ins)
                        emptied(pe, ("ru", t, e))
                        emptied(pe, ("brow", t, 0))
                        emptied(pe, ("krow", t, 0))
                        begin(("rz", t, e))
                        for h in range(H):
                            o = head64(pst(("rz", t, e)), h)[:, (h // 2) * 64:(h // 2) * 64 + 64]
                            mm(o, tile(BROW)[eb, h * 64:(h + 1) * 64], tile(UU)[eb, h * 64:(h + 1) * 64], start=True, stop=False)
                            ins = mm(o, tile(KROW)[eb, h * 64:(h + 1) * 64], tile(VROW)[eb, h * 64:(h + 1) * 64], start=False, stop=True)
                        end(ins)
                    for par in range(2):
                        emptied(pe, ("rb", t, par))
                        emptied(pe, ("rk", t, par))
                    begin(("yi", t))
                    for h in range(H):
                        o = head64(pst(("yi", t)), h)[:, (h // 2) * P:(h // 2 + 1) * P]
                        mm(o, tile(VROW)[:, h * 64:(h + 1) * 64], pair(KRT, h % 2)[:, h // 2, :], start=True, stop=False)
                        ins = mm(o, tile(UU)[:, h * 64:(h + 1) * 64], pair(BRT, h % 2)[:, h // 2, :], start=False, stop=True)
                    end(ins)
                for p in range(4):
                    column_sums("gmean", p, [tile(RHO + p)], [read(("yi", NT - 1))], sel="same64")
                for p in range(4):
                    column_sums("gvar", p, [tile(36 + p)], [(sem("gn_sq"), p + 1)], sel="same64")
                project("ai", h_mix, 5)
                narrow_product("wi", 8, 2)
                narrow_turn("wi", tile(39), 8)
                for i in range(5):
                    emptied(pe, "ai", i)
                    begin("irot", i)
                    end(mm(pst("irot", i), const("rot"), tile(QI + i), start=True, stop=True))
                for i in range(24):
                    qt, h = i // 8 + 1, i % 8
                    if qt == 1:
                        pe.wait_ge(sem("index_qk"), h // 2 + 2)
                    begin("index", i)
                    end(mm(pst("index", i)[:, 0:(qt + 1) * P], head64(tile(QI + h // 2), h)[:, qt * P:(qt + 1) * P],
                           head64(tile(KI), h)[:, 0:(qt + 1) * P], start=True, stop=True))
                project("aq", h_mix, 8)
                for s in range(2):
                    w = panel("av", s)
                    for t in range(NT):
                        if s == 0:
                            begin("av", t)
                        for k in range(KD):
                            ins = product(pst("av", t)[:, 256 * s:256 * s + 256], tokens(h_mix(k), t), [x[:, k, :] for x in w], k == 0, k == KD - 1)
                        end(ins)
                for i in range(8):
                    emptied(pe, "aq", i)
                    begin("arot", i)
                    end(mm(pst("arot", i), const("rot"), tile(AQ + i), start=True, stop=True))
                project("gate_a", h_mix, 8)
                project("yr", parts_in(Y_HIGH, range(RHO, RHO + 4)), 8, lambda k: part_ready("low", "y_rw", k), kt=4, per=4)
                pe.wait_ge(sem("dsa_qk"), 1)
                emptied(pe, "av", 3)

                def score(out, h, qt):
                    return mm(out, head64(tile(AQ + h // 2), h)[:, qt * P:(qt + 1) * P], head64(tile(AK + h // 2), h)[:, 0:(qt + 1) * P],
                              start=True, stop=True)

                def value(out, h, kt):
                    return head64(out, h)[:, 0:P], tile(AV + kt)[:, h * 64:(h + 1) * 64]

                attention("dsa", UNITS, score, value, (30, 31, 32, 29), (33, 34))
                project("gate_b", h_mix, 8)
                project("ya", parts_in(Y_HIGH, range(OA, OA + 4)), 8, lambda k: part_ready("low", "o_dsa", k), kt=4, per=4)
                project("wout", parts_in(MERGE_HIGH, range(MERGE, MERGE + 8)), 8, lambda k: part_ready("low", "merged", k))
                column_sums("rms4", 0, [tile(i) for i in (0, 6, 7)],
                            [norm_step("added", "rms4"), norm_step("squares", "rms4", 6), norm_step("squares", "rms4", 7)])
                feed_forward("_2", "rms4")
                column_sums("rms5", 0, [tile(i) for i in (42, 48, 49)],
                            [norm_step("added", "rms5"), norm_step("squares", "rms5", 6), norm_step("squares", "rms5", 7)])

            block_1()
            block_2()

        @block.scalar
        def _(act):
            link = linker(act, sem("act_chain"))
            af = nc.scalar.activation
            highs = [0]

            def split(value):
                while highs[0] < len(panel_release):
                    n = highs[0]
                    if n >= SPLIT:
                        if panel_release[n - SPLIT] > value:
                            break
                        act.wait_ge(pe_done, panel_release[n - SPLIT])
                    highs[0] += 1
                    act.wait_ge(panel_in[n % RAW], 16 * (n // RAW + 1))
                    link(nc.scalar.copy(W[:, n % SPLIT, 0, :], raw[:, n % RAW, :]), panel_high, n + 1)

            def high(dst, src, done, value):
                link(nc.scalar.copy(dst, src), done, value)

            def high_input(name, shift=None):
                for i in range(KD):
                    act.wait_ge(*norm_step("scaled", name, i))
                    if shift is None:
                        high(hH[:, i, :], tile(T_OF[name] + i % 4), *norm_step("high", name, i))
                    else:
                        link(af(hH[:, i, :], tile(T_OF[name] + i % 4), ACT.Identity, bias=shift(i)), *norm_step("high", name, i))

            def high_gated(sfx, i):
                if i < NG:
                    emptied(act, "up" + sfx, 4 * (i // 2) + 2 + i % 2)
                    high(tileR(G_HIGH + i), tile(i % 4), sem("gated_high" + sfx), i + 1)

            def high_rest(sfx):
                for i in range(NG, NF):
                    if i == NG:
                        filled(act, "up" + sfx, 43)
                    emptied(act, "up" + sfx, 4 * (i // 2) + 2 + i % 2)
                    high(hH[:, i - NG, :], tile(G_REST + i - NG), sem("gated_high" + sfx), i + 1)

            def squares(name, base, k=KD):
                for i in range(k):
                    link(af(tile(base + i), xT[:, i, :], ACT.Square), *norm_step("squares", name, i))

            def rstd(job, i, tmp, out, scale, done, value, bias="eps", power_bias=0.0):
                filled(act, job, i)
                link(af(tmp, pst(job, i), ACT.Ln, bias=col(bias), scale=scale), *read(job, i))
                link(af(out, tmp, ACT.Exp, bias=power_bias, scale=-0.5), done, value)

            def logarithm_next():
                link(af(st[:, 60:61], col("one"), ACT.Ln))

            def rstds(job, jobs, tiles, scale, done, used=None, bias="eps", power_bias=0.0):
                for i in jobs:
                    filled(act, job, i)
                    if used and i >= len(tiles):
                        act.wait_ge(used, i - len(tiles) + 1)
                    out = tile(tiles[i % len(tiles)])
                    link(af(out, pst(job, i), ACT.Ln, bias=col(bias), scale=scale), *read(job, i))
                for i in jobs:
                    out = tile(tiles[i % len(tiles)])
                    link(af(out, out, ACT.Exp, bias=power_bias, scale=-0.5), done, i + 1)

            def inverse(name, t, levels):
                am, xtr, xx, mk, p1 = BASES[name]
                for hf in range(2):
                    filled(act, (name, "x0", t, hf))
                    link(nc.scalar.copy(pair(xx, hf), heads4((name, "x0", t, hf))), *read((name, "x0", t, hf)))
                for lv in range(1, levels):
                    for hf in range(2):
                        filled(act, (name, "p1", t, lv, hf))
                        link(nc.scalar.copy(pair(p1, hf), heads4((name, "p1", t, lv, hf))), *read((name, "p1", t, lv, hf)))
                    if name == "rw":
                        for what, dst in (("vrow", VROW), ("brow", BROW), ("krow", KROW), ("nv", NVT)):
                            if (what, 0) in RW_BETWEEN[lv]:
                                filled(act, (what, t, 0))
                                link(nc.scalar.copy(tile(dst), pst((what, t, 0))), *read((what, t, 0)))

            def attention(name, units, scale, smt, ptt, out):
                n = len(units)
                for u in range(n + 3):
                    if u < n:
                        h, qt = units[u]
                        w = (qt + 1) * P
                        act.wait_ge(sem(f"{name}_peak"), u + 1)
                        link(af(tile(smt[u % 4])[:, 0:w], tile(smt[u % 4])[:, 0:w], ACT.Exp, bias=st[:, u % 4:u % 4 + 1],
                                scale=scale, accum_out=st[:, 4 + u % 4:5 + u % 4]), sem(f"{name}_exp"), u + 1)
                    if 2 <= u < n + 2:
                        h, qt = units[u - 2]
                        w = (qt + 1) * P
                        filled(act, (name, "turn", u - 2))
                        if u >= 4:
                            filled(act, (name, "values", u - 4))
                        link(nc.scalar.copy(tile(ptt[(u - 2) % 2])[:, 0:w], pst((name, "turn", u - 2))[:, 0:w]), *read((name, "turn", u - 2)))
                    if u >= 3:
                        h, qt = units[u - 3]
                        filled(act, (name, "values", u - 3))
                        dst, src = out(h, qt, pst((name, "values", u - 3)))
                        link(nc.scalar.copy(dst, src), *read((name, "values", u - 3)))

            def gelu(sfx):
                for p in range(11):
                    for i in (2 * p, 2 * p + 1):
                        emptied(act, "up" + sfx, 4 * p + i % 2)
                        link(af(tile(i % 4), tile(i % 4), ACT.Gelu), sem("gelu" + sfx), i + 1)
                    for i in (2 * p, 2 * p + 1):
                        high_gated(sfx, i)
                high_rest(sfx)

            def block_1():
                act.wait_ge(cols_in, 32)
                link(af(st[:, 0:8], cT[:], ACT.Silu), sem("silu_c"), 1)
                act.wait_ge(x_in, 16)
                squares("rms1", 0)
                logarithm_next()
                rstd("rms1", 0, tile(24), tile(24), 1.0 / D, *norm_step("rstd", "rms1"))
                split_before[act] = split
                split(0)
                high_input("rms1", lambda i: modT[:, i:i + 1])
                act.wait_ge(ab_in, 16)
                high(narrow[:, 0, :], wab[:].rearrange("p k c -> p (k c)"), sem("narrow_high"), 1)
                for i in range(24):
                    ahead(act, "qkv", min(i // 2 * 2 + 3, 23))
                    emptied(act, "qkv", i)
                    link(af(tile(Q0 + i), tile(Q0 + i), ACT.Silu), sem("conv_silu"), i + 1)
                    if i == 19:
                        filled(act, "ab")
                        link(nc.scalar.copy(tile(V0 + 7)[0:16, :], pst("ab")[0:16, :]), *read("ab"))
                    if i in (7, 11, 15, 19):
                        rstds("l2", range(i - 7, i - 3), (28, 29, 30, 31), 1.0, sem("l2_rstd"), sem("qk_normed"),
                              power_bias=(col("qscale") if i < 15 else 0.0))
                act.wait_ge(sem("ab_dve"), 1)
                link(af(sm4[:, AB_E, :, 0:8], sm4[:, AB_A, :, 0:8], ACT.Exp, scale=-1.0))
                link(af(sm4[:, AB_R, 0, 8:16], col("a_log", 0, 8), ACT.Exp))
                link(af(sm4[:, AB_B, :, 0:8], sm4[:, AB_B, :, 0:8], ACT.Exp, scale=-1.0))
                link(af(sm4[:, AB_E, :, 8:16], sm4[:, AB_E, :, 0:8], ACT.Ln, bias=col("one")), sem("ab_act"), 1)
                act.wait_ge(sem("gc_dve"), 1)
                link(af(sm4[:, EGC, :, :], sm4[:, GC, :, :], ACT.Exp))
                link(af(sm4[:, KDEC, :, 0:8], sm4[:, KDEC, :, 0:8], ACT.Exp), sem("gc_act"), 1)
                for t in range(NT):
                    for hf in range(2):
                        n = 2 * t + hf + 1
                        act.wait_ge(sem("gb_minus"), n)
                        link(af(pair(EGB, hf), heads4(("gb", t, hf)), ACT.Exp), *read(("gb", t, hf)))
                        act.wait_ge(sem("gb_masked"), n)
                        link(af(pair(DT, hf), pair(DT, hf), ACT.Exp), sem("gdn_decay"), n)
                    inverse("gdn", t, 7)
                    for hf in range(2):
                        filled(act, ("vn", t, hf))
                        link(nc.scalar.copy(pair(VN, hf), heads4(("vn", t, hf))), *read(("vn", t, hf)))
                    for hf in range(2):
                        filled(act, ("ot", t, hf))
                        link(nc.scalar.copy(ar[:, V0 + hf * HALF:V0 + (hf + 1) * HALF, t * P:(t + 1) * P],
                                            heads4(("ot", t, hf))), *read(("ot", t, hf)))
                for g in range(2):
                    rstds("onorm", range(4 * g, 4 * g + 4), (28, 29, 30, 31), 1.0 / P, sem("o_rstd"), sem("o_scaled"))
                for h in range(H):
                    filled(act, "z", h)
                    link(af(tile(Q0 + h), pst("z", h), ACT.Silu), *read("z", h))
                for i in range(3):
                    filled(act, "mkv", i)
                    link(nc.scalar.copy(tile(CKV + i), pst("mkv", i)), *read("mkv", i))
                for i in range(2):
                    link(af(tile(12 + i), tile(CKV + i), ACT.Square), sem("kv_sq"), i + 1)
                for i in range(12):
                    filled(act, "mq", i)
                    if i == 0:
                        act.wait_ge(sem("o_scaled"), 8)
                    link(nc.scalar.copy(tile(QN + i), pst("mq", i)), *read("mq", i))
                    if i == 3:
                        act.wait_ge(sem("angle"), 2)
                        for k in range(2):
                            link(af(trig[:, k, :], tile(42 - k), ACT.Sin), sem("trig"), k + 1)
                        rstd("kvn", 0, tile(14), tile(15), 1.0 / RANK, sem("kv_rstd"), 1)
                        for k in range(2):
                            act.wait_ge(sem("ckv"), k + 1)
                            high(tileR(CKV_HIGH[k]), tile(CKV + k), *part_ready("high", "ckv", k))
                for p in range(4):
                    link(af(tile(MV + p), tile(QR + p), ACT.Square), sem("qr_sq"), p + 1)
                for h in range(H):
                    filled(act, "uk", h)
                    link(nc.scalar.copy(tile(KN + h), pst("uk", h)), *read("uk", h))
                act.wait_ge(sem("k_rotated"), 1)
                for g in range(2):
                    rstds("qss", range(4 * g, 4 * g + 4), RS_Q, 1.0 / 192, sem("q_rstd"), sem("q_scaled"))
                for i in range(8):
                    filled(act, "mv", i)
                    link(nc.scalar.copy(tile(MV + i), pst("mv", i)), *read("mv", i))
                link(af(tile(8), tile(KROPE), ACT.Square), sem("kr_sq"), 1)
                act.wait_ge(sem("q_scaled"), 8)
                for g in range(2):
                    rstds("kss", range(4 * g, 4 * g + 4), RS_K, 1.0 / 192, sem("k_rstd"), sem("k_scaled"))
                for m in range(2):
                    filled(act, "gate_dn0", m)
                    link(af(tile(8 + m), pst("gate_dn0", m), ACT.Sigmoid), *read("gate_dn0", m))
                attention("mla", UNITS, 192 ** -0.5, (12, 13, 14, 11), (15, 48),
                          lambda h, qt, src: (tile(QN + h)[:, qt * P:(qt + 1) * P], src[:, 0:P]))
                for h in range(H):
                    high(tileR(O_DN_HIGH[h]), tile(V0 + h), *part_ready("high", "o_dn", h))
                for h in range(H):
                    high(tileR(O_MLA_HIGH[h]), tile(QN + h), *part_ready("high", "o_mla", h))
                for fb in range(2):
                    for j, what in enumerate(("gate_dn", "gate_mla")):
                        for m in range(4):
                            k = 2 * fb + j
                            if k == 0 and m < 2:
                                continue
                            filled(act, f"{what}{fb}", m)
                            if k:
                                act.wait_ge(sem("gate_used"), 4 * (k - 1) + m + 1)
                            link(af(tile(8 + m), pst(f"{what}{fb}", m), ACT.Sigmoid), *read(f"{what}{fb}", m))
                for i in range(KD):
                    if i >= 4:
                        ahead(act, "y_mla1", i - 4)
                    act.wait_ge(sem("mix"), i + 1)
                    if i == 0:
                        filled(act, "y_dn1", 3)
                    high(tileR(MIX_HIGH[i]), tile(MIX + i), *part_ready("high", "mix", i))
                for i in range(KD):
                    emptied(act, "wo", i)
                    link(af(tile(24 + i), xT[:, i, :], ACT.Square), *norm_step("squares", "rms2", i))
                logarithm_next()
                rstd("rms2", 0, tile(8), tile(9), 1.0 / D, *norm_step("rstd", "rms2"))
                high_input("rms2", lambda i: modT[:, 24 + i:25 + i])
                gelu("")

            def block_2():
                for i in range(KD):
                    emptied(act, "down", i)
                    link(af(tile(42 + i), xT[:, i, :], ACT.Square), *norm_step("squares", "rms3", i))
                logarithm_next()
                rstd("rms3", 0, tile(38), tile(39), 1.0 / D, *norm_step("rstd", "rms3"))
                high_input("rms3")
                for i in range(14):
                    emptied(act, *(("rkv", i) if i < 12 else ("wag", i - 12)))
                    if 4 <= i < 8:
                        link(af(tile(36 + i), tile(i), ACT.Square, scale=col("k_k", i - 4)), sem("kk_sq"), i - 3)
                link(af(tile(WA)[0:64, :], tile(WA)[0:64, :], ACT.Tanh), sem("lora_act"), 1)
                act.wait_ge(small2_in, 32)
                high(narrow[:, 0, 0:64], wix[:].rearrange("p k c -> p (k c)"), sem("narrow_high"), 2)
                link(af(tile(GD), tile(GD), ACT.Sigmoid), sem("lora_act"), 2)
                for what, base, bias in (("wup", LD, "w0"), ("aup", BT, "a0")):
                    for p in range(4):
                        filled(act, what, p)
                        link(af(tile(base + p), pst(what, p), ACT.Sigmoid, bias=col(bias, p)), *read(what, p))
                for p in range(4):
                    emptied(act, "kkn", p)
                    link(af(tile(36 + p), tile(36 + p), ACT.Ln, scale=float(2 ** 20)))
                for p in range(4):
                    link(af(tile(36 + p), tile(36 + p), ACT.Exp, scale=-0.5, bias=col("ln1024")), sem("kk_rstd"), p + 1)
                for p in range(4):
                    act.wait_ge(sem("g_cum"), p + 1)
                    gc = tile(40 + p)
                    if p >= 2:
                        act.wait_ge(sem("rho_decayed"), p - 1)
                    link(af(tile(30 + p % 2), gc, ACT.Exp))
                    link(af(sm2[:, EC + 8 * p:EC + 8 * p + 8], gc[:, 63:S:64], ACT.Exp))
                    link(af(gc, gc, ACT.Exp, scale=-1.0))
                    link(af(tile(LD + p), tile(LD + p), ACT.Exp), sem("decays"), p + 1)
                for p in range(4):
                    filled(act, "gup", p)
                    link(nc.scalar.copy(tile(G2 + p), pst("gup", p)), *read("gup", p))
                for t in range(NT):
                    inverse("rw", t, 6)
                    for e in range(2):
                        eb, n = slice(64 * e, 64 * e + 64), 2 * t + e
                        ec = slice(t * P + 64 * e, t * P + 64 * e + 64)
                        filled(act, ("ru", t, e))
                        link(nc.scalar.mul(tile(UU)[eb, :], pst(("ru", t, e))[eb, :], -1.0), *read(("ru", t, e)))
                        for par in range(2):
                            b = slice(64 * par, 64 * par + 64)
                            filled(act, ("ry", t, e, par))
                            link(nc.scalar.copy(ar[b, RHO:RHO + 4, ec], pst(("ry", t, e, par))[b, 0:256].rearrange("p (h c) -> p h c", c=64)),
                                 *read(("ry", t, e, par)))
                for p in range(4):
                    emptied(act, "gmean", p)
                    link(af(tile(36 + p), tile(RHO + p), ACT.Square), sem("gn_sq"), p + 1)
                rstds("gvar", range(4), (40, 41, 42, 43), 1.0 / 64, sem("gn_rstd"), bias="lnx")
                for p in range(4):
                    act.wait_ge(sem("y_rw"), p + 1)
                    if p == 0:
                        act.wait_ge(sem("y_rw"), 4)
                    high(tileR(Y_HIGH[p]), tile(RHO + p), *part_ready("high", "y_rw", p))
                for i in range(5):
                    filled(act, "ai", i)
                    link(nc.scalar.copy(tile(QI + i), pst("ai", i)), *read("ai", i))
                filled(act, "wi")
                link(nc.scalar.copy(tile(39)[0:8, :], pst("wi")[0:8, :]), *read("wi"))
                for i in range(24):
                    w = (i // 8 + 2) * P
                    if i >= 2:
                        act.wait_ge(sem("index_used"), i - 1)
                    filled(act, "index", i)
                    link(af(tile(REL[i % 2])[:, 0:w], pst("index", i)[:, 0:w], ACT.Relu), *read("index", i))
                for i in range(8):
                    filled(act, "aq", i)
                    link(nc.scalar.copy(tile(AQ + i), pst("aq", i)), *read("aq", i))
                for t in range(NT):
                    filled(act, "av", t)
                    link(nc.scalar.copy(tile(AV + t), pst("av", t)), *read("av", t))
                for m in range(8):
                    filled(act, "gate_a", m)
                    link(af(tile(MERGE + m), pst("gate_a", m), ACT.Sigmoid), *read("gate_a", m))
                attention("dsa", UNITS, 64 ** -0.5, (30, 31, 32, 29), (33, 34),
                          lambda h, qt, src: (tile(OA + h // 2)[64 * (h % 2):64 * (h % 2) + 64, qt * P:(qt + 1) * P],
                                              src[64 * (h % 2):64 * (h % 2) + 64, 0:P]))
                for p in range(4):
                    high(tileR(Y_HIGH[p]), tile(OA + p), *part_ready("high", "o_dsa", p))
                for m in range(8):
                    filled(act, "gate_b", m)
                    link(af(tile(AQ + m), pst("gate_b", m), ACT.Sigmoid), *read("gate_b", m))
                for m in range(8):
                    ahead(act, "ya", m)
                    act.wait_ge(sem("merged"), m + 1)
                    high(tileR(MERGE_HIGH[m]), tile(MERGE + m), *part_ready("high", "merged", m))
                for i in range(KD):
                    emptied(act, "wout", i)
                    link(af(tile(i), xT[:, i, :], ACT.Square), *norm_step("squares", "rms4", i))
                logarithm_next()
                rstd("rms4", 0, tile(8), tile(9), 1.0 / D, *norm_step("rstd", "rms4"))
                high_input("rms4")
                for p in range(11):
                    for j in range(2):
                        i, job = 2 * p + j, 4 * p + j
                        filled(act, "up_2", job)
                        if i >= 4:
                            act.wait_ge(sem("gated_low_2"), min(i - 3, NG))
                            emptied(act, "up_2", 4 * ((i - 4) // 2) + 2 + i % 2)
                        link(af(tile(i % 4), pst("up_2", job), ACT.Silu), *read("up_2", job))
                    for i in (2 * p, 2 * p + 1):
                        high_gated("_2", i)
                high_rest("_2")
                for i in range(KD):
                    emptied(act, "down_2", i)
                    link(af(tile(42 + i), xT[:, i, :], ACT.Square), *norm_step("squares", "rms5", i))
                logarithm_next()
                rstd("rms5", 0, tile(8), tile(9), 1.0 / D, *norm_step("rstd", "rms5"))

            block_1()
            block_2()

        @block.vector
        def _(dve):
            link = linker(dve, sem("dve_chain"))
            v = nc.vector
            tt, ts, stt = v.tensor_tensor, v.tensor_scalar, v.scalar_tensor_tensor

            def low(dst, src, high_part):
                return tt(dst, src, high_part.bitcast(F32), ALU.subtract)

            def lows(name, high_tiles, base):
                for k, t in enumerate(high_tiles):
                    dve.wait_ge(*part_ready("high", name, k))
                    link(low(tileR(base + k), tile(base + k), tileR(t)), *part_ready("low", name, k))

            def normed(name, rs, scale, shift, dst, kept=None):
                dve.wait_ge(*norm_step("rstd", name))
                for i in range(KD + 2):
                    if i < KD:
                        link(stt(tile(T_OF[name] + i % 4), xT[:, i, :], scale(i), rs, ALU.mult, ALU.mult), *norm_step("scaled", name, i))
                    if i >= 2:
                        j = i - 2
                        dve.wait_ge(*norm_step("high", name, j))
                        if kept and j == 0:
                            dve.wait_ge(*kept)
                        t, h = tile(T_OF[name] + j % 4), hH[:, j, :]
                        if shift is None:
                            link(low(dst(j), t, h), *norm_step("low", name, j))
                        else:
                            link(stt(dst(j), t, shift(j), h.bitcast(F32), ALU.add, ALU.subtract), *norm_step("low", name, j))

            def causal_conv(job, i, out, taps, done, value, bias=None):
                src = pst(job, i)
                n = len(taps)
                link(ts(out, src, taps[-1], bias, ALU.mult, ALU.add if bias is not None else ALU.bypass))
                for j in range(1, n):
                    ins = stt(out[:, j:S], src[:, 0:S - j], taps[n - 1 - j], out[:, j:S], ALU.mult, ALU.add)
                    if j < n - 1:
                        link(ins)
                    else:
                        link(ins, *read(job, i))

            def inverse(name, t, levels, between, job):
                am, xtr, xx, mk, p1 = BASES[name]
                for hf in range(2):
                    dve.wait_ge(sem(f"{name}_masked0"), 2 * t + hf + 1)
                    link(tt(pair(xtr, hf), bm(const("ident")), pair(mk, hf), ALU.subtract), sem(f"{name}_xt0"), 2 * t + hf + 1)
                for lv in range(1, levels):
                    for hf in range(2):
                        if lv < levels - 1:
                            filled(dve, (name, "x", t, lv, hf))
                        filled(dve, (name, "xt", t, lv, hf))
                        link(tt(pair(xtr, hf), pair(xtr, hf), heads4((name, "xt", t, lv, hf)), ALU.subtract), *read((name, "xt", t, lv, hf)))
                        if lv < levels - 1:
                            link(tt(pair(xx, hf), pair(xx, hf), heads4((name, "x", t, lv, hf)), ALU.subtract), *read((name, "x", t, lv, hf)))
                    for what, hf in between[lv]:
                        job(what, t, hf)

            def attention(name, units, scale, smt, bias, before=None):
                n = len(units)
                for u in range(n + 1):
                    if u < n:
                        h, qt = units[u]
                        w = (qt + 1) * P
                        if before:
                            before(u)
                        filled(dve, (name, "scores", u))
                        if u >= 4:
                            filled(dve, (name, "turn", u - 4))
                        link(v.tensor_tensor_reduce(out=tile(smt[u % 4])[:, 0:w], in0=pst((name, "scores", u))[:, 0:w], in1=bias(qt),
                                                    scale=1.0, scalar=LOW, op0=ALU.add, op1=ALU.max,
                                                    accum_out=st[:, 8 + u % 4:9 + u % 4]), *read((name, "scores", u)))
                        link(ts(st[:, u % 4:u % 4 + 1], st[:, 8 + u % 4:9 + u % 4], -scale, None, ALU.mult), sem(f"{name}_peak"), u + 1)
                    if u >= 1:
                        h, qt = units[u - 1]
                        w = (qt + 1) * P
                        dve.wait_ge(sem(f"{name}_exp"), u)
                        r = st[:, 12 + (u - 1) % 4:13 + (u - 1) % 4]
                        link(v.reciprocal(r, st[:, 4 + (u - 1) % 4:5 + (u - 1) % 4]))
                        link(ts(tile(smt[(u - 1) % 4])[:, 0:w], tile(smt[(u - 1) % 4])[:, 0:w], r, None, ALU.mult), sem(f"{name}_probs"), u)

            def gated_up(sfx, conv):
                for p in range(11):
                    for j in range(2):
                        i, job = 2 * p + j, 4 * p + j
                        filled(dve, "up" + sfx, job)
                        if i >= 4:
                            dve.wait_ge(sem("gated_low" + sfx), min(i - 3, NG))
                        conv(job, i, tile(i % 4))
                    for j in range(2):
                        i, job = 2 * p + j, 4 * p + 2 + j
                        filled(dve, "up" + sfx, job)
                        dve.wait_ge(sem("gelu" + sfx), i + 1)
                        link(tt(tile(i % 4) if i < NG else tile(G_REST + i - NG), tile(i % 4), pst("up" + sfx, job), ALU.mult), *read("up" + sfx, job))

            def tell(s, value):
                link(v.memset(st[:, 63:64], 0.0), s, value)

            def rope(dst, src, job, i, tmp):
                filled(dve, job, i)
                link(tt(tmp, pst(job, i), trig[:, 1, :], ALU.mult), *read(job, i))
                link(tt(dst, src, trig[:, 0, :], ALU.mult))
                link(tt(dst, dst, tmp, ALU.add))

            def block_1():
                dve.wait_ge(cols_in, 32)
                dve.wait_ge(sem("silu_c"), 1)

                def ada_products(i):
                    b = i if i < 4 else 2 + i % 2
                    dve.wait_ge(ada_in[b], 16 if i < 4 else 16 * (i // 2))
                    if i >= 3:
                        filled(dve, "ada", i - 2)
                    acc = tile(32 + i % 2)
                    link(ts(acc, tile(ADA_BASE[b]), st[:, 0:1], None, ALU.mult))
                    for k in range(1, KD):
                        ins = stt(acc, tile(ADA_BASE[b] + k), st[:, k:k + 1], acc, ALU.mult, ALU.add)
                        if k < KD - 1:
                            link(ins)
                    link(ins, sem("ada_used"), i)

                def ada_out(i):
                    filled(dve, "ada", i)
                    link(tt(modT[:, 4 * i:4 * i + 4], pst("ada", i)[:, 0:4], col("b_ada", 4 * i, 4), ALU.add), *read("ada", i))

                for i in range(1, 4):
                    ada_products(i)
                for i in range(4):
                    ada_out(i)
                link(stt(amp[:, 0, :], modT[:, 8:16], 1.0, col("norm1", 0, 8), ALU.add, ALU.mult))
                normed("rms1", tile(24), lambda i: amp[:, 0, i:i + 1], lambda i: modT[:, i:i + 1], lambda i: xL[:, i, :])
                dve.wait_ge(sem("narrow_high"), 1)
                link(low(narrow[:, 1, :], wab[:].rearrange("p k c -> p (k c)"), narrow[:, 0, :]), sem("narrow"), 1)
                def unit_heads(g):
                    for i in range(4 * g, 4 * g + 4):
                        dve.wait_ge(sem("l2_rstd"), i + 1)
                        link(tt(tile(Q0 + i), tile(Q0 + i), tile(28 + i % 4), ALU.mult), sem("qk_normed"), i + 1)

                for m in range(12):
                    if m == 11:
                        filled(dve, "ab_turn")
                        ab = pst("ab_turn")[:, 0:64].rearrange("p (t c) -> p t c", c=16)
                        link(tt(sm4[:, AB_X, :, 0:8], ab[:, :, 0:8], bm(col("dt_bias", 0, 8), NT), ALU.add))
                        link(v.tensor_copy(sm4[:, AB_B, :, 0:8], ab[:, :, 8:16]), *read("ab_turn"))
                        link(ts(sm4[:, AB_A, :, 0:8], sm4[:, AB_X, :, 0:8], -1.0, None, ALU.mult))
                        link(tt(sm4[:, AB_A, :, 0:8], sm4[:, AB_X, :, 0:8], sm4[:, AB_A, :, 0:8], ALU.max), sem("ab_dve"), 1)
                    for i in (2 * m, 2 * m + 1):
                        filled(dve, "qkv", i)
                        causal_conv("qkv", i, tile(Q0 + i), [col("conv", 4 * i + j) for j in range(4)], None, None)
                    if m in ADA_AFTER:
                        ada_products(4 + ADA_AFTER.index(m))
                    if m - 3 in ADA_AFTER:
                        ada_out(4 + ADA_AFTER.index(m - 3))
                    if m - 2 in L2_AFTER:
                        unit_heads(L2_AFTER[m - 2])
                unit_heads(3)
                ada_out(10)
                ada_out(11)
                link(stt(amp[:, 1, :], modT[:, 32:40], 1.0, col("norm2", 0, 8), ALU.add, ALU.mult))
                dve.wait_ge(sem("ab_act"), 1)
                link(stt(sm4[:, AB_X, :, 0:8], sm4[:, AB_X, :, 0:8], 0.0, sm4[:, AB_E, :, 8:16], ALU.max, ALU.add))
                link(stt(sm4[:, G, :, 0:8], sm4[:, AB_X, :, 0:8], -1.0, bm(sm4[:, AB_R, 0, 8:16], NT), ALU.mult, ALU.mult), sem("g_ready"), 1)
                link(ts(sm4[:, AB_B, :, 0:8], sm4[:, AB_B, :, 0:8], 1.0, None, ALU.add))
                link(v.reciprocal(sm4[:, BETA, :, 0:8], sm4[:, AB_B, :, 0:8]), sem("beta_ready"), 1)
                filled(dve, "gc")
                link(v.tensor_copy(sm4[:, GC, :, :], pst("gc")[:, 0:64].rearrange("p (t c) -> p t c", c=16)), *read("gc"))
                link(tt(sm4[:, KDEC, :, 0:8], sm4[:, GC, :, 8:16], sm4[:, GC, :, 0:8], ALU.subtract), sem("gc_dve"), 1)
                dve.wait_ge(sem("gc_act"), 1)
                link(tt(sm4[:, BE, :, 0:8], sm4[:, BETA, :, 0:8], sm4[:, EGC, :, 0:8], ALU.mult))
                for hf in range(2):
                    link(v.memset(pair(ST, hf), 0.0), sem("gdn_state"), hf + 1)
                def gdn_job(what, t, hf):
                    h0 = hf * HALF
                    filled(dve, (what, t, hf))
                    dst, factor = {"kq": (ATT, pair(DT, hf)), "kt": (KD_ROW, bh(tok(KDEC, t, h0, 4))), "vt": (VB, bh(tok(BETA, t, h0, 4)))}[what]
                    link(tt(pair(dst, hf), heads4((what, t, hf)), factor, ALU.mult), *read((what, t, hf)))

                for t in range(NT):
                    for hf in range(2):
                        n, h0 = 2 * t + hf + 1, hf * HALF
                        filled(dve, ("gb", t, hf))
                        link(tt(pair(DT, hf), heads4(("gb", t, hf)), bh(tok(GC, t, h0, 4)), ALU.subtract), sem("gb_minus"), n)
                        link(tt(pair(DT, hf), pair(DT, hf), bm(const("neg_after")), ALU.add), sem("gb_masked"), n)
                        dve.wait_ge(sem("gdn_decay"), n)
                        filled(dve, ("kk", t, hf))
                        link(tt(pair(AM, hf), heads4(("kk", t, hf)), pair(DT, hf), ALU.mult), *read(("kk", t, hf)))
                        filled(dve, ("bb", t, hf))
                        link(tt(pair(AM, hf), heads4(("bb", t, hf)), pair(AM, hf), ALU.mult), *read(("bb", t, hf)))
                    inverse("gdn", t, 7, GDN_BETWEEN, gdn_job)
                    for hf in range(2):
                        filled(dve, ("ks", t, hf))
                        link(tt(pair(RHS, hf), heads4(("ks", t, hf)), bh(tok(BE, t, hf * HALF, 4)), ALU.mult), *read(("ks", t, hf)))
                        link(tt(pair(RHS, hf), pair(VB, hf), pair(RHS, hf), ALU.subtract), sem("gdn_rhs"), 2 * t + hf + 1)
                    for hf in range(2):
                        filled(dve, ("su", t, hf))
                        link(tt(pair(ST, hf), pair(ST, hf), bh(tok(EGC, t, 8 + hf * HALF, 4)), ALU.mult))
                        link(tt(pair(ST, hf), pair(ST, hf), heads4(("su", t, hf)), ALU.add), *read(("su", t, hf)))
                        tell(sem("gdn_state"), 2 * t + hf + 3)
                for h in range(H):
                    dve.wait_ge(sem("o_rstd"), h + 1)
                    link(stt(tile(V0 + h), tile(V0 + h), col("dn_norm"), tile(28 + h % 4), ALU.mult, ALU.mult), sem("o_scaled"), h + 1)
                for h in range(H):
                    emptied(dve, "z", h)
                    link(tt(tile(V0 + h), tile(V0 + h), tile(Q0 + h), ALU.mult), sem("o_dn"), h + 1)
                dve.wait_ge(sem("wide_in"), 16)
                dve.wait_ge(pos_in, 16)
                link(v.tensor_copy(tile(40), trig[:, 0, :].bitcast(I32)))
                link(ts(tile(40), tile(40), col("inv_freq"), None, ALU.mult))
                for i in range(2):
                    dst = tile(41) if i == 0 else tile(42)
                    link(ts(tile(43), tile(40), 1.0 / (2 * np.pi), 0.25 * i, ALU.mult, ALU.add))
                    link(ts(tile(43), tile(43), 12582912.0, None, ALU.add))
                    link(ts(tile(43), tile(43), -12582912.0, None, ALU.add))
                    link(stt(dst, tile(43), -TURN[0], tile(40), ALU.mult, ALU.add))
                    link(stt(dst, tile(43), -TURN[1], dst, ALU.mult, ALU.add))
                    link(stt(dst, tile(43), -TURN[2], dst, ALU.mult, ALU.add))
                    if i:
                        link(ts(dst, dst, float(np.float32(np.pi / 2)), None, ALU.add))
                    link(ts(dst, dst, PI_IN, -PI_IN, ALU.min, ALU.max), sem("angle"), i + 1)
                dve.wait_ge(sem("kv_rstd"), 1)
                for k in range(2):
                    link(stt(tile(CKV + k), tile(CKV + k), col("kv_norm", k), tile(15), ALU.mult, ALU.mult), sem("ckv"), k + 1)
                lows("ckv", CKV_HIGH, CKV)
                link(ts(tile(KRW), tile(KROPE), col("kn_rope"), None, ALU.mult), sem("kr_w"), 1)
                dve.wait_ge(sem("trig"), 2)
                rope(tile(KRW), tile(KRW), "krot", 0, tile(48))
                link(v.memset(st[:, 62:63], 0.0), sem("k_rotated"), 1)
                for h in range(H):
                    dve.wait_ge(sem("q_rstd"), h + 1)
                    rs = tile(RS_Q[h % 4])
                    b = slice(64 * (h % 2), 64 * (h % 2) + 64)
                    link(stt(tile(QN + h), tile(QN + h), col("qn_nope"), rs, ALU.mult, ALU.mult))
                    link(stt(tile(QR + h // 2)[b, :], tile(QR + h // 2)[b, :], col("qn_rope")[b, :], rs[b, :], ALU.mult, ALU.mult),
                         sem("q_scaled"), h + 1)
                    if h % 2:
                        link(v.memset(st[:, 62:63], 0.0), sem("qr_w"), h // 2 + 1)
                for p in range(4):
                    rope(tile(QR + p), tile(QR + p), "qrot", p, tile(46 + p % 2))
                for h in range(H):
                    dve.wait_ge(sem("k_rstd"), h + 1)
                    rs = tile(RS_K[h % 4])
                    b = slice(64 * (h % 2), 64 * (h % 2) + 64)
                    link(stt(tile(KN + h), tile(KN + h), col("kn_nope"), rs, ALU.mult, ALU.mult))
                    link(tt(tile(KR + h // 2)[b, :], tile(KRW)[b, :], rs[b, :], ALU.mult), sem("k_scaled"), h + 1)
                attention("mla", UNITS, 192 ** -0.5, (12, 13, 14, 11), lambda qt: wide[:, 0, S - (qt + 1) * P:S])
                lows("o_dn", O_DN_HIGH, V0)
                lows("o_mla", O_MLA_HIGH, QN)
                for fb in range(2):
                    for m in range(4):
                        emptied(dve, f"gate_dn{fb}", m)
                        filled(dve, f"y_dn{fb}", m)
                        link(tt(tile(MIX + 4 * fb + m), tile(8 + m), pst(f"y_dn{fb}", m), ALU.mult), *read(f"y_dn{fb}", m))
                        tell(sem("gate_used"), 8 * fb + m + 1)
                    for m in range(4):
                        emptied(dve, f"gate_mla{fb}", m)
                        filled(dve, f"y_mla{fb}", m)
                        link(tt(tile(12 + m % 2), tile(8 + m), pst(f"y_mla{fb}", m), ALU.mult), *read(f"y_mla{fb}", m))
                        tell(sem("gate_used"), 8 * fb + 4 + m + 1)
                        link(tt(tile(MIX + 4 * fb + m), tile(MIX + 4 * fb + m), tile(12 + m % 2), ALU.add), sem("mix"), 4 * fb + m + 1)
                lows("mix", MIX_HIGH, MIX)
                dve.wait_ge(x_in, 32)
                for i in range(KD):
                    filled(dve, "wo", i)
                    link(stt(xT[:, i, :], pst("wo", i), modT[:, 16 + i:17 + i], xT[:, i, :], ALU.mult, ALU.add), *read("wo", i))
                normed("rms2", tile(9), lambda i: amp[:, 1, i:i + 1], lambda i: modT[:, 24 + i:25 + i],
                       lambda i: tileR(H_LOW + i))

                def conv(job, i, dst):
                    causal_conv("up", job, dst, [col("fconv", 3 * i + j) for j in range(3)], None, None, bias=col("fbias", i))

                filled(dve, "rms2")
                gated_up("", conv)
                for i in range(KD):
                    filled(dve, "down", i)
                    link(stt(xT[:, i, :], pst("down", i), modT[:, 40 + i:41 + i], xT[:, i, :], ALU.mult, ALU.add), *read("down", i))

            def block_2():
                link(ts(sm2[:, OM_MU:OM_MU + 14], col("mu", 0, 14), -1.0, 1.0, ALU.mult, ALU.add))
                link(ts(sm2[:, OM_KA:OM_KA + 4], col("k_a", 0, 4), -1.0, 1.0, ALU.mult, ALU.add))
                normed("rms3", tile(39), lambda i: col("norm1_2", i), None, lambda i: xL[:, i, :], (sem("x_kept"), 16))
                for i in range(14):
                    job, k = ("rkv", i) if i < 12 else ("wag", i - 12)
                    filled(dve, job, k)
                    causal_conv(job, k, tile(i), [col("mu", i), sm2[:, OM_MU + i:OM_MU + i + 1]], None, None)
                dve.wait_ge(sem("narrow_high"), 2)
                link(low(narrow[:, 1, 0:64], wix[:].rearrange("p k c -> p (k c)"), narrow[:, 0, 0:64]), sem("narrow"), 2)
                for p in range(4):
                    filled(dve, "kkn", p)
                    link(ts(tile(36 + p), pst("kkn", p), 1e-24, None, ALU.max), *read("kkn", p))
                for p in range(4):
                    emptied(dve, "wup", p)
                    link(ts(tile(LD + p), tile(LD + p), -float(np.exp(-0.5)), None, ALU.mult))
                    link(v.tensor_tensor_scan(tile(40 + p), wide[:, 3, :], tile(LD + p), 0.0, ALU.mult, ALU.add))
                    link(tt(tile(LD + p), tile(40 + p), tile(LD + p), ALU.subtract), sem("g_cum"), p + 1)
                for p in range(4):
                    link(ts(tile(KAP + p), tile(KT + p), col("k_k", p), None, ALU.mult))
                    emptied(dve, "aup", p)
                    tmp = tile((44, 45, 48, 49)[p])
                    link(ts(tmp, tile(BT + p), col("k_a", p), sm2[:, OM_KA + p:OM_KA + p + 1], ALU.mult, ALU.add), sem("a_read"), p + 1)
                    link(tt(tile(KT + p), tile(KT + p), tmp, ALU.mult))
                    link(stt(tmp, tile(RHO + p), col("r_k", p), tile(KT + p), ALU.mult, ALU.mult), sem("bonus_in"), p + 1)
                for p in range(4):
                    filled(dve, "bon", p)
                    link(tt(tile(BV + p), pst("bon", p), tile(V2 + p), ALU.mult), *read("bon", p))
                for p in range(4):
                    dve.wait_ge(sem("decays"), p + 1)
                    link(tt(tile(RHO + p), tile(RHO + p), tile(30 + p % 2), ALU.mult), sem("rho_decayed"), p + 1)
                    dve.wait_ge(sem("beta_made"), p + 1)
                    link(tt(tile(KAP + p), tile(KAP + p), tile(LD + p), ALU.mult))
                    link(tt(tile(KT + p), tile(KT + p), tile(40 + p), ALU.mult), sem("rw_ready"), p + 1)
                dve.wait_ge(sem("beta_decayed"), 4)
                def rw_job(what, t, par):
                    if what in ("rn", "rb", "rk"):
                        dst, mask = {"rn": (NTR, "strict64"), "rb": (BRT, "incl64"), "rk": (KRT, "incl64")}[what]
                        filled(dve, (what, t, par))
                        link(tt(pair(dst, par), heads4((what, t, par)), bm(const(mask)), ALU.mult), *read((what, t, par)))

                link(v.memset(tile(ST2)[:, 0:256], 0.0), sem("rw_state"), 1)
                for t in range(NT):
                    for par in range(2):
                        n = 2 * t + par + 1
                        filled(dve, ("rm", t, par))
                        link(v.tensor_copy(pair(36, par), heads4(("rm", t, par))), *read(("rm", t, par)))
                    inverse("rw", t, 6, RW_BETWEEN, rw_job)
                    emptied(dve, ("nv", t, 0))
                    for e in range(2):
                        eb, n = slice(64 * e, 64 * e + 64), 2 * t + e
                        for par in range(2):
                            filled(dve, ("rs", t, e, par))
                            view = lambda x: x[eb, :].rearrange("p (k two c) -> p k two c", two=2, c=64)[:, :, par, :]
                            link(tt(view(tile(RSB)), pst(("rs", t, e, par))[eb, 0:256].rearrange("p (k c) -> p k c", c=64), view(tile(NVT)), ALU.add),
                                 *read(("rs", t, e, par)))
                        tell(sem("rw_rhs"), n + 1)
                        filled(dve, ("rz", t, e))
                        link(tt(tile(ST2)[:, 0:256], tile(ST2)[:, 0:256], pst(("rz", t, e))[:, 0:256], ALU.add), *read(("rz", t, e)))
                        s4 = tile(ST2)[:, 0:256].rearrange("p (k c) -> p k c", c=64)
                        link(tt(s4, s4, bh(sm2[:, EC + n:EC + 32:8], 64), ALU.mult), sem("rw_state"), n + 2)
                    filled(dve, ("yi", t))
                    for par in range(2):
                        emptied(dve, ("ry", t, 1, par))
                    y4 = ar[:, RHO:RHO + 4, t * P:(t + 1) * P]
                    link(tt(y4, y4, heads4(("yi", t)), ALU.add), *read(("yi", t)))
                for p in range(4):
                    filled(dve, "gmean", p)
                    link(stt(tile(RHO + p), pst("gmean", p), -1.0 / 64, tile(RHO + p), ALU.mult, ALU.add), *read("gmean", p))
                for p in range(4):
                    dve.wait_ge(sem("gn_rstd"), p + 1)
                    link(stt(tile(RHO + p), tile(RHO + p), col("lnx_g", p), tile(40 + p), ALU.mult, ALU.mult))
                    link(stt(tile(RHO + p), tile(RHO + p), col("lnx_b", p), tile(BV + p), ALU.add, ALU.add))
                    link(tt(tile(RHO + p), tile(RHO + p), tile(G2 + p), ALU.mult), sem("y_rw"), p + 1)
                lows("y_rw", Y_HIGH, RHO)
                filled(dve, "wi_turn")
                link(v.tensor_copy(sm2[:, WI:WI + 32], pst("wi_turn")[:, 0:32]), *read("wi_turn"))
                dve.wait_ge(trig_in, 16)
                for n, i in enumerate((4, 0, 1, 2, 3)):
                    rope(tile(QI + i), tile(QI + i), "irot", i, tile(39))
                    link(v.memset(st[:, 62:63], 0.0), sem("index_qk"), n + 1)
                for i in range(24):
                    q, h = i // 8, i % 8
                    w = (q + 2) * P
                    acc, wt = tile(SCO + q)[:, 0:w], sm2[:, WI + 8 * (q + 1) + h:WI + 8 * (q + 1) + h + 1]
                    emptied(dve, "index", i)
                    if h == 0:
                        link(ts(acc, tile(REL[i % 2])[:, 0:w], wt, None, ALU.mult), sem("index_used"), i + 1)
                    else:
                        link(stt(acc, tile(REL[i % 2])[:, 0:w], wt, acc, ALU.mult, ALU.add), sem("index_used"), i + 1)
                for q in range(3):
                    w = (q + 2) * P
                    acc, work, sel = (tile(i)[:, 0:w] for i in (SCO + q, WORK, SEL + q))
                    top = sm2[:, TOP8:TOP8 + 8]
                    link(stt(acc, acc, 64 ** -0.5 * 8 ** -0.5, wide[:, 2, S - w:S], ALU.mult, ALU.add))
                    for r in range(TOPK // 8):
                        src = work if r else acc
                        link(v.max(top, src))
                        link(v.match_replace(work, top, src, -3.3e38))
                    link(tt(sel, work, acc, ALU.is_equal))
                    link(ts(sel, sel, NEG, None, ALU.mult))
                for i in range(8):
                    rope(tile(AQ + i), tile(AQ + i), "arot", i, tile(39))
                link(v.memset(st[:, 62:63], 0.0), sem("dsa_qk"), 1)
                for m in range(8):
                    filled(dve, "yr", m)
                    emptied(dve, "gate_a", m)
                    link(tt(tile(MERGE + m), tile(MERGE + m), pst("yr", m), ALU.mult), *read("yr", m))
                attention("dsa", UNITS, 64 ** -0.5, (30, 31, 32, 29),
                          lambda qt: tile(SEL + qt - 1)[:, 0:(qt + 1) * P] if qt else wide[:, 1, S - P:S])
                lows("o_dsa", Y_HIGH, OA)
                for m in range(8):
                    filled(dve, "ya", m)
                    emptied(dve, "gate_b", m)
                    link(tt(tile(AQ + m), tile(AQ + m), pst("ya", m), ALU.mult), *read("ya", m))
                    link(tt(tile(MERGE + m), tile(MERGE + m), tile(AQ + m), ALU.add), sem("merged"), m + 1)
                lows("merged", MERGE_HIGH, MERGE)
                dve.wait_ge(sem("x3_in"), 16)
                for i in range(KD):
                    filled(dve, "wout", i)
                    link(tt(xT[:, i, :], xT[:, i, :], pst("wout", i), ALU.add), *read("wout", i))
                normed("rms4", tile(9), lambda i: col("norm2_2", i), None, lambda i: tileR(H_LOW + i))
                for p in range(11):
                    for j in range(2):
                        i, job = 2 * p + j, 4 * p + 2 + j
                        filled(dve, "up_2", job)
                        emptied(dve, "up_2", 4 * p + j)
                        link(tt(tile(i % 4) if i < NG else tile(G_REST + i - NG), tile(i % 4), pst("up_2", job), ALU.mult), *read("up_2", job))
                for i in range(KD):
                    filled(dve, "down_2", i)
                    link(tt(xT[:, i, :], xT[:, i, :], pst("down_2", i), ALU.add), *read("down_2", i))
                dve.wait_ge(*norm_step("rstd", "rms5"))
                for i in range(KD):
                    link(stt(xT[:, i, :], xT[:, i, :], col("normf", i), tile(9), ALU.mult, ALU.mult), sem("y_out"), i + 1)

            block_1()
            block_2()

        @block.gpsimd
        def _(pool):
            link = linker(pool, sem("pool_chain"))
            g = nc.gpsimd
            tt = g.tensor_tensor
            lows = [0]

            def split(value):
                while lows[0] < len(panel_release):
                    n = lows[0]
                    if n >= SPLIT and panel_release[n - SPLIT] > value:
                        break
                    lows[0] += 1
                    pool.wait_ge(panel_high, n + 1)
                    link(tt(W[:, n % SPLIT, 1, :], raw[:, n % RAW, :], W[:, n % SPLIT, 0, :].bitcast(F32), ALU.subtract), panel_low, n + 1)

            split_before[pool] = split

            def add_squares(name, base, stage=None):
                for i in range(1, KD - 2):
                    if stage:
                        ahead(pool, stage, i)
                    pool.wait_ge(*norm_step("squares", name, i))
                    ins = tt(tile(base), tile(base), tile(base + i), ALU.add)
                    if i < KD - 3:
                        link(ins)
                    else:
                        link(ins, *norm_step("added", name))

            def low_gated(sfx):
                for i in range(NF):
                    ahead(pool, "up" + sfx, 43 if i >= NG else 4 * (i // 2) + 2 + i % 2)
                    pool.wait_ge(sem("gated_high" + sfx), i + 1)
                    if i < NG:
                        link(tt(tileR(G_LOW + i), tile(i % 4), tileR(G_HIGH + i).bitcast(F32), ALU.subtract), sem("gated_low" + sfx), i + 1)
                    else:
                        rest = G_REST + i - NG
                        link(tt(tileR(rest), tile(rest), hH[:, i - NG, :].bitcast(F32), ALU.subtract), sem("gated_low" + sfx), i + 1)

            def inverse(name, t, levels):
                am, xtr, xx, mk, p1 = BASES[name]
                for lv in range(levels):
                    for hf in range(2):
                        if lv == 0:
                            emptied(pool, ("bb" if name == "gdn" else "rm", t, hf))
                            s, value = sem(f"{name}_masked0"), 2 * t + hf + 1
                        else:
                            s, value = sem(f"{name}_masked"), (t * (levels - 1) + lv - 1) * 2 + hf + 1
                            if lv == 1:
                                pool.wait_ge(sem(f"{name}_xt0"), 2 * t + hf + 1)
                            else:
                                filled(pool, (name, "p1", t, lv - 1, hf))
                        link(tt(pair(mk, hf), pair(am, hf), bm(const(f"lvl{lv}")), ALU.mult), s, value)

            def block_1():
                add_squares("rms1", 0)
                for i in range(16):
                    ahead(pool, "qkv", min(i + 2, 23))
                    pool.wait_ge(sem("conv_silu"), i + 1)
                    if i >= 4:
                        filled(pool, "l2", i - 4)
                    link(tt(tile(24 + i % 4), tile(Q0 + i), tile(Q0 + i), ALU.mult), sem("l2_sq"), i + 1)
                pool.wait_ge(consts_in, 16)
                for t in range(NT):
                    for hf in range(2):
                        n = 2 * t + hf + 1
                        emptied(pool, ("gb", t, hf))
                        if n == 1:
                            pool.wait_ge(sem("qk_normed"), 16)
                        if t:
                            filled(pool, ("ot", t - 1, hf))
                        link(tt(pair(QE, hf), ar[:, Q0 + hf * HALF:Q0 + (hf + 1) * HALF, t * P:(t + 1) * P], pair(EGB, hf), ALU.mult),
                             sem("gdn_qe"), n)
                    inverse("gdn", t, 7)
                emptied(pool, ("ot", NT - 1, 1))
                emptied(pool, ("ot", NT - 1, 0))
                for h in range(H):
                    if h >= 4:
                        filled(pool, "onorm", h - 4)
                    link(tt(tile(24 + h % 4), tile(V0 + h), tile(V0 + h), ALU.mult), sem("onorm_sq"), h + 1)
                for i in range(2 * H):
                    if i == 0:
                        ahead(pool, "z", 7)
                        pool.wait_ge(sem("o_dn"), H)
                    emptied(pool, *(("mq", i) if i < H else ("uk", i - H)))
                    if i >= H + 2:
                        filled(pool, "kss", i - H - 2)
                    elif 4 <= i < H:
                        filled(pool, "qss", i - 4)
                    x = tile(QN + i) if i < H else tile(KN + i - H)
                    link(tt(tile(MV + 4 + i % 4) if i < H else tile((14, 49)[i % 2]), x, x, ALU.mult), sem("nope_sq"), i + 1)
                add_squares("rms2", 24, "wo")
                low_gated("")
                add_squares("rms3", 42, "down")

            block_1()
            for p in range(4):
                ahead(pool, "gup", 3)
                pool.wait_ge(sem("a_read"), p + 1)
                pool.wait_ge(sem("kk_rstd"), p + 1)
                link(tt(tile(KAP + p), tile(KAP + p), tile(36 + p), ALU.mult))
                link(tt(tile(BT + p), tile(BT + p), tile(KAP + p), ALU.mult), sem("beta_made"), p + 1)
            for p in range(4):
                pool.wait_ge(sem("decays"), p + 1)
                link(tt(tile(BT + p), tile(BT + p), tile(40 + p), ALU.mult), sem("beta_decayed"), p + 1)
            for t in range(NT):
                inverse("rw", t, 6)
            add_squares("rms4", 0, "wout")
            low_gated("_2")
            add_squares("rms5", 42, "down_2")
            split(last["rms5", 0])


_T = 2 * np.pi
TURN = [201.0 / 32.0]
_r = _T - TURN[0]
TURN.append(float(np.float32(np.round(_r * 2 ** 22) / 2 ** 22)))
TURN.append(float(np.float32(_r - TURN[1])))
PI_IN = float(np.nextafter(np.float32(np.pi), np.float32(0)))


def _panels(w, width=256, size=PANEL):
    out = []
    kt = w.shape[0] // P
    per = size // width
    for n in range(0, w.shape[1], width):
        for k in range(0, kt, per):
            part = w[k * P:min(kt, k + per) * P, n:n + width]
            x = np.zeros((P, per, width), w.dtype)
            x[:, :part.shape[0] // P, :part.shape[1]] = part.reshape(-1, P, part.shape[1]).transpose(1, 0, 2)
            out.append(x.reshape(P, size))
    return out


def _col(v):
    return np.asarray(v).reshape(-1, P).T


def _row(v):
    return np.broadcast_to(np.asarray(v).reshape(1, -1), (P, np.asarray(v).size))


def _pairs(w, n):
    k = w.shape[0]
    return w.reshape(k, 2, n // 256, 256).transpose(0, 2, 1, 3).reshape(k, 2 * n)


def lay_out_2(f, c, out, panels):
    w = f["w_in_2"]
    c["norm1_2"], c["norm2_2"], c["normf"] = _col(f["norm1_g_2"]), _col(f["norm2_g_2"]), _col(f["normf_g_2"])
    c["mu"] = _col(f["tshift_mu_2"])
    for n in ("w0", "a0", "k_k", "k_a", "lnx_g", "lnx_b"):
        c[n] = _col(f[n + "_2"])
    c["r_k"] = _col(f["r_k_2"].reshape(-1))
    c["ln1024"] = np.full((P, 1), 10 * np.log(2.0), np.float32)
    out["lora"] = np.ascontiguousarray(np.stack([np.concatenate([f["w_decay_up_2"], f["a_up_2"]], 0), f["g_up_2"]], 1))
    out["wix"] = np.ascontiguousarray(w[:, 3904:3912].reshape(KD, P, 8).transpose(1, 0, 2))
    kidx = w[:, 3840:3904]
    panels += _panels(w[:, 0:1536]) + _panels(w[:, 1536:1792])
    panels += _panels(np.concatenate([w[:, 3328:3840], kidx, kidx], 1))
    panels += _panels(w[:, 1792:2816]) + _panels(w[:, 2816:3328])
    panels += _panels(w[:, 3912:4936]) + _panels(f["w_o_rwkv_2"], S) + _panels(w[:, 4936:5960]) + _panels(f["w_o_att_2"], S)
    panels += _panels(f["w_out_2"]) + _panels(_pairs(f["w_ffn_in_2"], FF)) + _panels(f["w_ffn_out_2"])


def lay_out(i):
    f = {k: np.asarray(v) for k, v in i.items()}
    cm, wide, inv = constants()
    out = {"cm": cm, "wide": np.ascontiguousarray(wide[:, [0, 1, 2, 5]]), "trig": np.ascontiguousarray(wide[:, [3, 4]])}
    c = {"one": np.ones((P, 1), np.float32), "eps": np.full((P, 1), EPS, np.float32),
         "qscale": np.full((P, 1), -0.5 * np.log(128.0), np.float32), "lnx": np.full((P, 1), LNX_EPS, np.float32), "inv_freq": inv}
    panels = []
    w_in = f["w_in"][0]
    at = np.cumsum([0, 1024, 1024, 1024, 1024, 8, 8, 1536, 256, 64, 1024, 1024])
    q, k, v, z, al, be, mq, ckv, kr, gd, gm = (w_in[:, at[j]:at[j + 1]] for j in range(11))
    c["b_ada"], c["norm1"] = _col(f["b_ada"][0]), _col(f["norm1_w"][0])
    c["conv"] = f["dn_conv_w"][0].reshape(4, 24, P).transpose(2, 1, 0).reshape(P, 96)
    c["dn_norm"] = _col(f["dn_norm_w"][0])
    c["kv_norm"] = _col(f["mla_kv_norm_w"][0])
    for n, w in (("qn", f["mla_q_norm_w"][0]), ("kn", f["mla_k_norm_w"][0])):
        c[n + "_nope"] = _col(w[:128])
        c[n + "_rope"] = _col(np.concatenate([w[128:], w[128:]]))
    c["norm2"] = _col(f["norm2_w"][0])
    c["fconv"] = f["ffn_conv_w"][0].reshape(3, NF, P).transpose(2, 1, 0).reshape(P, 3 * NF)
    c["fbias"] = _col(f["ffn_conv_b"][0])
    c["a_log"], c["dt_bias"] = _row(f["dn_a_log"][0]), _row(f["dn_dt_bias"][0])
    mq = mq.reshape(D, H, 192)
    nope, rope = mq[:, :, :128].reshape(D, 1024), mq[:, :, 128:].reshape(D, 512)
    out["ada"] = np.stack(_panels(f["w_ada"][0], S, KD * S)).reshape(12, P, KD, S)
    panels += _panels(np.concatenate([q, k, v], 1))
    panels += _panels(z) + _panels(np.concatenate([ckv, kr, kr], 1)) + _panels(np.concatenate([nope, rope], 1))
    panels += [w.reshape(2, P, 1024).transpose(1, 0, 2).reshape(P, 2048) for w in (f["mla_w_uk"][0], f["mla_w_uv"][0])]
    gd, gm, yd, ym = _panels(gd), _panels(gm), _panels(f["w_out_dn"][0]), _panels(f["w_out_mla"][0])
    panels += [x for b in range(2) for p in (gd, yd, gm, ym) for x in p[2 * b:2 * b + 2]]
    panels += _panels(f["w_o"][0]) + _panels(_pairs(f["ffn_w_up"][0], FF)) + _panels(f["ffn_w_down"][0])
    out["wab"] = np.ascontiguousarray(np.concatenate([al, be], 1).reshape(KD, P, 16).transpose(1, 0, 2))
    out["cT"] = np.ascontiguousarray(_col(f["c"][0]))
    out["posb"] = np.ascontiguousarray(_row(f["positions"][0]).astype(np.int32))
    lay_out_2(f, c, out, panels)
    out["panels"] = np.stack(panels)
    out["cols"] = np.concatenate([c[n] if n in c else np.zeros((P, w), np.float32) for n, w in COLS], 1).astype(np.float32)
    out["xT"] = np.ascontiguousarray(f["x"][0].T.reshape(KD, P, S).transpose(1, 0, 2))
    return out


def kernel(**inputs):
    import concourse.bacc as bacc
    from concourse.bass_utils import run_bass_kernel_spmd

    arrays = lay_out(inputs)
    nc = bacc.Bacc("TRN2", target_bir_lowering=False, num_devices=1)
    aps = {n: nc.dram_tensor(n + "_dram", x.shape, mybir.dt.from_np(x.dtype), kind="ExternalInput").ap() for n, x in arrays.items()}
    aps["out"] = nc.dram_tensor("out_dram", (P, KD, S), F32, kind="ExternalOutput").ap()
    build(nc, aps)
    r = run_bass_kernel_spmd(nc, [{n + "_dram": x for n, x in arrays.items()}], core_ids=[0])
    y = r.results[0]["out_dram"]
    return np.ascontiguousarray(y.transpose(1, 0, 2).reshape(D, S).T).reshape(1, S, D)
```
